# Optimizing a Trainium2 kernel written in Bass

```python
import jax, jax.numpy as jnp
from jax import lax
import numpy as np

D_MODEL = 2048
BATCH = 1
SEQ = 256
DEPTH = 1

GRID_W = 64
N_META = 16
EPS = 1e-6
NEG_INF = -1e30
NA_HEADS = 8
NA_HEAD_DIM = 128
NA_WIN_ROWS = 8
NA_WIN_COLS = 16
NA_COL_BLOCK = 16
NA_KEY_COLS = NA_COL_BLOCK + NA_WIN_COLS
MLA_HEADS = 8
MLA_Q_RANK = 512
MLA_KV_RANK = 256
MLA_NOPE_DIM = 128
MLA_ROPE_DIM = 64
MLA_V_DIM = 128
MLA_QK_DIM = MLA_NOPE_DIM + MLA_ROPE_DIM
ROPE_THETA = 10000.0
Q_BLOCK = 128
D_FF = 5632
CONV_W = 3

NA_WIDTH = NA_HEADS * NA_HEAD_DIM
MLA_WIDTH = MLA_HEADS * MLA_V_DIM
D_MIX = NA_WIDTH + MLA_WIDTH
IN_COLS = 3 * NA_WIDTH + MLA_Q_RANK + MLA_KV_RANK + MLA_ROPE_DIM
IN_SPLITS = [NA_WIDTH, 2 * NA_WIDTH, 3 * NA_WIDTH, 3 * NA_WIDTH + MLA_Q_RANK, 3 * NA_WIDTH + MLA_Q_RANK + MLA_KV_RANK]


def rmsnorm(x, g):
    xf = x.astype(jnp.float32)
    y = xf * lax.rsqrt(jnp.mean(xf * xf, axis=-1, keepdims=True) + EPS)
    return (y * g.astype(jnp.float32)).astype(x.dtype)

def rope_tables(length, dtype):
    inv = ROPE_THETA ** (-jnp.arange(0, MLA_ROPE_DIM, 2, dtype=jnp.float32) / MLA_ROPE_DIM)
    ang = jnp.arange(length, dtype=jnp.float32)[:, None] * inv[None, :]
    return jnp.cos(ang)[:, None, :].astype(dtype), jnp.sin(ang)[:, None, :].astype(dtype)

def apply_rope(x, cos, sin):
    half = x.shape[-1] // 2
    x1, x2 = x[..., :half], x[..., half:]
    return jnp.concatenate([x1 * cos - x2 * sin, x2 * cos + x1 * sin], axis=-1)

def neighbourhood_attention(q, k, v, rpb, meta_bias):
    B, L, H, D = q.shape
    T = L - N_META
    rows = T // GRID_W
    kh = min(NA_WIN_ROWS, rows)
    scale = D ** -0.5
    n_cb = GRID_W // NA_COL_BLOCK
    qm, km, vm = q[:, :N_META], k[:, :N_META], v[:, :N_META]

    s_mm = jnp.einsum('bqhd,bkhd->bhqk', qm, km).astype(jnp.float32) * scale + meta_bias.astype(jnp.float32)[None, :, None, :]
    p_mm = jax.nn.softmax(s_mm, axis=-1).astype(vm.dtype)
    meta_out = jnp.einsum('bhqk,bkhd->bqhd', p_mm, vm)

    qg = q[:, N_META:].reshape(B, rows, GRID_W, H, D)
    kg = k[:, N_META:].reshape(B, rows, GRID_W, H, D)
    vg = v[:, N_META:].reshape(B, rows, GRID_W, H, D)

    qcols = np.arange(GRID_W).reshape(n_cb, NA_COL_BLOCK)
    col_start = np.clip(qcols - NA_WIN_COLS // 2, 0, GRID_W - NA_WIN_COLS)
    kblk_start = np.clip(np.arange(n_cb) * NA_COL_BLOCK - NA_WIN_COLS // 2, 0, GRID_W - NA_KEY_COLS)
    key_cols = kblk_start[:, None] + np.arange(NA_KEY_COLS)[None, :]
    col_valid = (key_cols[:, None, :] >= col_start[:, :, None]) & (key_cols[:, None, :] < col_start[:, :, None] + NA_WIN_COLS)
    col_mask = jnp.asarray(np.where(col_valid, 0.0, NEG_INF), jnp.float32)
    dc_idx = np.clip(key_cols[:, None, :] - qcols[:, :, None] + NA_WIN_COLS - 1, 0, 2 * NA_WIN_COLS - 2)
    rpb32 = rpb.astype(jnp.float32)
    mbias = meta_bias.astype(jnp.float32)[None, None, None]

    def row_block(r):
        rs = jnp.clip(r - kh // 2, 0, rows - kh)
        kb = lax.dynamic_slice_in_dim(kg, rs, kh, axis=1)[:, :, key_cols]
        vb = lax.dynamic_slice_in_dim(vg, rs, kh, axis=1)[:, :, key_cols]
        qr = lax.dynamic_index_in_dim(qg, r, axis=1, keepdims=False).reshape(B, n_cb, NA_COL_BLOCK, H, D)
        s_win = jnp.einsum('bjqhd,bijkhd->bjqhik', qr, kb).astype(jnp.float32) * scale
        dr_idx = rs + jnp.arange(kh) - r + NA_WIN_ROWS - 1
        bias = rpb32[:, dr_idx][:, :, dc_idx].transpose(2, 3, 0, 1, 4)
        s_win = s_win + bias[None] + col_mask[None, :, :, None, None, :]
        s_met = jnp.einsum('bjqhd,bmhd->bjqhm', qr, km).astype(jnp.float32) * scale + mbias
        s = jnp.concatenate([s_met, s_win.reshape(B, n_cb, NA_COL_BLOCK, H, kh * NA_KEY_COLS)], axis=-1)
        p = jax.nn.softmax(s, axis=-1).astype(vb.dtype)
        p_win = p[..., N_META:].reshape(B, n_cb, NA_COL_BLOCK, H, kh, NA_KEY_COLS)
        out = jnp.einsum('bjqhm,bmhd->bjqhd', p[..., :N_META], vm) + jnp.einsum('bjqhik,bijkhd->bjqhd', p_win, vb)
        return out.reshape(B, GRID_W, H, D)

    real = lax.map(row_block, jnp.arange(rows))
    real = real.transpose(1, 0, 2, 3, 4).reshape(B, T, H, D)
    return jnp.concatenate([meta_out, real], axis=1)

def mla_attention(cq, ckv, k_pe, cq_g, ckv_g, w_q_up, w_kv_up, q_g, k_g, cos, sin):
    B, L, _ = cq.shape
    q = (rmsnorm(cq, cq_g) @ w_q_up).reshape(B, L, MLA_HEADS, MLA_QK_DIM)
    kv = (rmsnorm(ckv, ckv_g) @ w_kv_up).reshape(B, L, MLA_HEADS, MLA_NOPE_DIM + MLA_V_DIM)
    k_nope, v = kv[..., :MLA_NOPE_DIM], kv[..., MLA_NOPE_DIM:]
    k = jnp.concatenate([k_nope, jnp.broadcast_to(k_pe[:, :, None, :], (B, L, MLA_HEADS, MLA_ROPE_DIM))], axis=-1)
    q = rmsnorm(q, q_g)
    k = rmsnorm(k, k_g)
    q = jnp.concatenate([q[..., :MLA_NOPE_DIM], apply_rope(q[..., MLA_NOPE_DIM:], cos, sin)], axis=-1)
    k = jnp.concatenate([k[..., :MLA_NOPE_DIM], apply_rope(k[..., MLA_NOPE_DIM:], cos, sin)], axis=-1)
    scale = MLA_QK_DIM ** -0.5

    def attend(qb):
        s = jnp.einsum('bqhd,bkhd->bhqk', qb, k).astype(jnp.float32) * scale
        p = jax.nn.softmax(s, axis=-1).astype(v.dtype)
        return jnp.einsum('bhqk,bkhd->bqhd', p, v)

    out_meta = attend(q[:, :N_META])
    nb = (L - N_META) // Q_BLOCK
    qr = q[:, N_META:].reshape(B, nb, Q_BLOCK, MLA_HEADS, MLA_QK_DIM).transpose(1, 0, 2, 3, 4)
    out_real = lax.map(attend, qr).transpose(1, 0, 2, 3, 4).reshape(B, L - N_META, MLA_HEADS, MLA_V_DIM)
    return jnp.concatenate([out_meta, out_real], axis=1)

def conv_glu(x, w_gate, w_up, conv_w, conv_b, w_down):
    L = x.shape[1]
    g = x @ w_gate
    u = x @ w_up
    pad = CONV_W // 2
    gp = jnp.pad(g, ((0, 0), (pad, pad), (0, 0)))
    gc = conv_b
    for i in range(CONV_W):
        gc = gc + conv_w[i] * gp[:, i:i + L]
    return (jax.nn.silu(gc) * u) @ w_down

def first_inputs(seed: int = 0) -> dict:
    key = jax.random.key(seed)
    ks = jax.random.split(key, 24)
    f32 = jnp.float32

    def nrm(k, shape, s):
        return jax.random.normal(k, shape, f32) * s

    def gain(k, shape):
        return 1.0 + 0.05 * jax.random.normal(k, shape, f32)

    return {
        "x": nrm(ks[0], (BATCH, SEQ, D_MODEL), 1.0),
        "meta_tokens": nrm(ks[1], (N_META, D_MODEL), 1.0),
        "mix_norm_g": gain(ks[2], (DEPTH, D_MODEL)),
        "w_in": nrm(ks[3], (DEPTH, D_MODEL, IN_COLS), D_MODEL ** -0.5),
        "na_q_g": gain(ks[4], (DEPTH, NA_HEAD_DIM)),
        "na_k_g": gain(ks[5], (DEPTH, NA_HEAD_DIM)),
        "na_rpb": nrm(ks[6], (DEPTH, NA_HEADS, 2 * NA_WIN_ROWS - 1, 2 * NA_WIN_COLS - 1), 0.1),
        "na_meta_bias": nrm(ks[7], (DEPTH, NA_HEADS, N_META), 0.1),
        "mla_cq_g": gain(ks[8], (DEPTH, MLA_Q_RANK)),
        "mla_ckv_g": gain(ks[9], (DEPTH, MLA_KV_RANK)),
        "w_q_up": nrm(ks[10], (DEPTH, MLA_Q_RANK, MLA_HEADS * MLA_QK_DIM), MLA_Q_RANK ** -0.5),
        "w_kv_up": nrm(ks[11], (DEPTH, MLA_KV_RANK, MLA_HEADS * (MLA_NOPE_DIM + MLA_V_DIM)), MLA_KV_RANK ** -0.5),
        "mla_q_g": gain(ks[12], (DEPTH, MLA_QK_DIM)),
        "mla_k_g": gain(ks[13], (DEPTH, MLA_QK_DIM)),
        "na_out_g": gain(ks[14], (DEPTH, NA_WIDTH)),
        "mla_out_g": gain(ks[15], (DEPTH, MLA_WIDTH)),
        "w_out": nrm(ks[16], (DEPTH, D_MIX, D_MODEL), D_MIX ** -0.5),
        "ffn_norm_g": gain(ks[17], (DEPTH, D_MODEL)),
        "w_gate": nrm(ks[18], (DEPTH, D_MODEL, D_FF), D_MODEL ** -0.5),
        "w_up": nrm(ks[19], (DEPTH, D_MODEL, D_FF), D_MODEL ** -0.5),
        "conv_w": nrm(ks[20], (DEPTH, CONV_W, D_FF), CONV_W ** -0.5),
        "conv_b": nrm(ks[21], (DEPTH, D_FF), 0.01),
        "w_down": nrm(ks[22], (DEPTH, D_FF, D_MODEL), D_FF ** -0.5),
    }

def first_block(x, meta_tokens, mix_norm_g, w_in, na_q_g, na_k_g, na_rpb, na_meta_bias, mla_cq_g, mla_ckv_g,
              w_q_up, w_kv_up, mla_q_g, mla_k_g, na_out_g, mla_out_g, w_out, ffn_norm_g, w_gate, w_up,
              conv_w, conv_b, w_down):
    B = x.shape[0]
    meta = jnp.broadcast_to(meta_tokens.astype(x.dtype)[None], (B, N_META, D_MODEL))
    h = jnp.concatenate([meta, x], axis=1)
    L = h.shape[1]
    cos, sin = rope_tables(L, x.dtype)
    for l in range(DEPTH):
        hn = rmsnorm(h, mix_norm_g[l])
        proj = hn @ w_in[l]
        q_a, k_a, v_a, cq, ckv, k_pe = jnp.split(proj, IN_SPLITS, axis=-1)
        q_a = rmsnorm(q_a.reshape(B, L, NA_HEADS, NA_HEAD_DIM), na_q_g[l])
        k_a = rmsnorm(k_a.reshape(B, L, NA_HEADS, NA_HEAD_DIM), na_k_g[l])
        v_a = v_a.reshape(B, L, NA_HEADS, NA_HEAD_DIM)
        out_a = neighbourhood_attention(q_a, k_a, v_a, na_rpb[l], na_meta_bias[l]).reshape(B, L, NA_WIDTH)
        out_b = mla_attention(cq, ckv, k_pe, mla_cq_g[l], mla_ckv_g[l], w_q_up[l], w_kv_up[l],
                              mla_q_g[l], mla_k_g[l], cos, sin).reshape(B, L, MLA_WIDTH)
        mix = jnp.concatenate([rmsnorm(out_a, na_out_g[l]), rmsnorm(out_b, mla_out_g[l])], axis=-1)
        h = h + mix @ w_out[l]
        h = h + conv_glu(rmsnorm(h, ffn_norm_g[l]), w_gate[l], w_up[l], conv_w[l], conv_b[l], w_down[l])
    return h[:, N_META:]


CONV_WIDTH = 3
CONV_GROUPS = 8
D_CONV = D_MODEL // 2
HGRN_HEADS = 8
HGRN_DK = 128
HGRN_DV = (D_MODEL // 2) // HGRN_HEADS
D_HGRN_K = HGRN_HEADS * HGRN_DK
D_HGRN_V = HGRN_HEADS * HGRN_DV
CHUNK = 64
D_FF_2 = ((8 * D_MODEL // 3 + 255) // 256) * 256
N_MOD = 6
SPLITS = (D_CONV, D_CONV, D_CONV, D_HGRN_K, D_HGRN_K, D_HGRN_V, D_HGRN_V, D_MODEL, D_MODEL)
D_IN = sum(SPLITS)


def rmsnorm_2(x, g):
    xf = x.astype(jnp.float32)
    y = xf * lax.rsqrt(jnp.mean(xf * xf, axis=-1, keepdims=True) + EPS)
    return (y * g.astype(jnp.float32)).astype(x.dtype)

def causal_depthwise_conv(u, w):
    s = u.shape[1]
    upad = jnp.pad(u, ((0, 0), (CONV_WIDTH - 1, 0), (0, 0)))
    y = w[0] * upad[:, 0:s]
    for k in range(1, CONV_WIDTH):
        y = y + w[k] * upad[:, k:k + s]
    return y

def to_chunks(t):
    b, s, h, d = t.shape
    return t.reshape(b, s // CHUNK, CHUNK, h, d).transpose(1, 0, 3, 2, 4)

def from_chunks(t):
    n, b, h, c, d = t.shape
    return t.transpose(1, 0, 3, 2, 4).reshape(b, n * c, h, d)

def hgrn2_chunked(q, k, v, log_f):
    qc, kc, vc = to_chunks(q), to_chunks(k), to_chunks(v)
    bc = jnp.cumsum(to_chunks(log_f), axis=3)
    causal = jnp.tril(jnp.ones((CHUNK, CHUNK), dtype=bool))[:, :, None]
    b_, h_ = q.shape[0], q.shape[2]
    s0 = jnp.zeros((b_, h_, HGRN_DK, HGRN_DV), jnp.float32)

    def step(state, xs):
        qi, ki, vi, bi = xs
        b_last = bi[:, :, -1:, :]
        o_inter = jnp.einsum('bhtk,bhkv->bhtv', qi * jnp.exp(bi), state)
        diff = bi[:, :, :, None, :] - bi[:, :, None, :, :]
        decay = jnp.exp(jnp.where(causal, diff, -jnp.inf))
        scores = jnp.einsum('bhtk,bhtsk,bhsk->bhts', qi, decay, ki)
        o_intra = jnp.einsum('bhts,bhsv->bhtv', scores, vi)
        new_state = (jnp.swapaxes(jnp.exp(b_last), -1, -2) * state
                     + jnp.einsum('bhsk,bhsv->bhkv', ki * jnp.exp(b_last - bi), vi))
        return new_state, o_inter + o_intra

    _, o = lax.scan(step, s0, (qc, kc, vc, bc))
    return from_chunks(o)

def second_inputs(seed: int = 0) -> dict:
    key = jax.random.key(seed)
    ks = jax.random.split(key, 20)

    def nrm(k, shape, fan_in):
        return jax.random.normal(k, shape, jnp.float32) * (fan_in ** -0.5)

    def gain(k, shape):
        return 1.0 + 0.02 * jax.random.normal(k, shape, jnp.float32)

    return {
        "x": jax.random.normal(ks[0], (BATCH, SEQ, D_MODEL), jnp.float32),
        "c": jax.random.normal(ks[1], (BATCH, D_MODEL), jnp.float32),
        "w_ada": nrm(ks[2], (DEPTH, D_MODEL, N_MOD * D_MODEL), D_MODEL) * 0.5,
        "b_ada": 0.02 * jax.random.normal(ks[3], (DEPTH, N_MOD * D_MODEL), jnp.float32),
        "norm_mix_g": gain(ks[4], (DEPTH, D_MODEL)),
        "w_in": nrm(ks[5], (DEPTH, D_MODEL, D_IN), D_MODEL),
        "conv_w": nrm(ks[6], (DEPTH, CONV_WIDTH, D_CONV), CONV_WIDTH),
        "lb_param": jax.random.normal(ks[7], (DEPTH + 1, D_HGRN_K), jnp.float32),
        "gnorm_g": gain(ks[8], (DEPTH, HGRN_DV)),
        "w_conv_out": nrm(ks[9], (DEPTH, D_CONV, D_MODEL), D_CONV),
        "w_hgrn_out": nrm(ks[10], (DEPTH, D_HGRN_V, D_MODEL), D_HGRN_V),
        "w_o": nrm(ks[11], (DEPTH, D_MODEL, D_MODEL), D_MODEL),
        "norm_ffn_g": gain(ks[12], (DEPTH, D_MODEL)),
        "w_ffn_gate": nrm(ks[13], (DEPTH, D_MODEL, D_FF_2), D_MODEL),
        "w_ffn_up": nrm(ks[14], (DEPTH, D_MODEL, D_FF_2), D_MODEL),
        "w_ffn_down": nrm(ks[15], (DEPTH, D_FF_2, D_MODEL), D_FF_2),
        "norm_final_g": gain(ks[16], (D_MODEL,)),
    }

def second_block(x, c, w_ada, b_ada, norm_mix_g, w_in, conv_w, lb_param, gnorm_g,
              w_conv_out, w_hgrn_out, w_o, norm_ffn_g, w_ffn_gate, w_ffn_up, w_ffn_down,
              norm_final_g):
    b, s, _ = x.shape
    lb_all = jnp.cumsum(jax.nn.softmax(lb_param.astype(jnp.float32), axis=0), axis=0)
    split_idx = list(np.cumsum(SPLITS)[:-1])
    c_act = jax.nn.silu(c)

    for l in range(DEPTH):
        mod = c_act @ w_ada[l] + b_ada[l]
        sh_m, sc_m, gt_m, sh_f, sc_f, gt_f = [m[:, None, :] for m in jnp.split(mod, N_MOD, axis=-1)]

        h = rmsnorm_2(x, norm_mix_g[l]) * (1.0 + sc_m) + sh_m
        proj = h @ w_in[l]
        a_b, a_c, a_x, q, f_logit, i_in, g_out, gate_a, gate_b = jnp.split(proj, split_idx, axis=-1)

        y_a = (a_b * causal_depthwise_conv(a_c * a_x, conv_w[l])) @ w_conv_out[l]

        lb = lb_all[l]
        f = lb + (1.0 - lb) * jax.nn.sigmoid(f_logit.astype(jnp.float32))
        qh = jax.nn.silu(q.astype(jnp.float32)).reshape(b, s, HGRN_HEADS, HGRN_DK)
        kh = (1.0 - f).reshape(b, s, HGRN_HEADS, HGRN_DK)
        log_f = jnp.log(f).reshape(b, s, HGRN_HEADS, HGRN_DK)
        vh = i_in.astype(jnp.float32).reshape(b, s, HGRN_HEADS, HGRN_DV)
        o = hgrn2_chunked(qh, kh, vh, log_f)
        o = rmsnorm_2(o, gnorm_g[l]) * jax.nn.silu(g_out.astype(jnp.float32)).reshape(b, s, HGRN_HEADS, HGRN_DV)
        y_b = o.reshape(b, s, D_HGRN_V).astype(x.dtype) @ w_hgrn_out[l]

        merged = jax.nn.sigmoid(gate_a) * y_a + jax.nn.sigmoid(gate_b) * y_b
        x = x + gt_m * (merged @ w_o[l])

        h2 = rmsnorm_2(x, norm_ffn_g[l]) * (1.0 + sc_f) + sh_f
        ff = (jax.nn.silu(h2 @ w_ffn_gate[l]) * (h2 @ w_ffn_up[l])) @ w_ffn_down[l]
        x = x + gt_f * ff

    return rmsnorm_2(x, norm_final_g)


def setup_inputs(seed=0):
    out = dict(first_inputs(seed))
    for name, value in second_inputs(seed + 1).items():
        if name != "x":
            out[name + "_2"] = value
    return out


def reference(
    x, meta_tokens, mix_norm_g, w_in, na_q_g, na_k_g, na_rpb, na_meta_bias, mla_cq_g, mla_ckv_g,
    w_q_up, w_kv_up, mla_q_g, mla_k_g, na_out_g, mla_out_g, w_out, ffn_norm_g, w_gate, w_up,
    conv_w, conv_b, w_down, c_2, w_ada_2, b_ada_2, norm_mix_g_2, w_in_2, conv_w_2, lb_param_2,
    gnorm_g_2, w_conv_out_2, w_hgrn_out_2, w_o_2, norm_ffn_g_2, w_ffn_gate_2, w_ffn_up_2,
    w_ffn_down_2, norm_final_g_2,
):
    x = first_block(
        x, meta_tokens, mix_norm_g, w_in, na_q_g, na_k_g, na_rpb, na_meta_bias, mla_cq_g,
        mla_ckv_g, w_q_up, w_kv_up, mla_q_g, mla_k_g, na_out_g, mla_out_g, w_out, ffn_norm_g,
        w_gate, w_up, conv_w, conv_b, w_down,
    )
    return second_block(
        x, c_2, w_ada_2, b_ada_2, norm_mix_g_2, w_in_2, conv_w_2, lb_param_2, gnorm_g_2,
        w_conv_out_2, w_hgrn_out_2, w_o_2, norm_ffn_g_2, w_ffn_gate_2, w_ffn_up_2, w_ffn_down_2,
        norm_final_g_2,
    )


_drawn_inputs = setup_inputs


def setup_inputs(seed=0):
    import zlib

    import numpy as np

    out = dict(_drawn_inputs(seed))
    spreads = {}
    factors = {'conv_b': 8.0,
     'b_ada_2': 3.462,
     'norm_mix_g_2': 8.0,
     'lb_param_2': 39.951,
     'gnorm_g_2': 200.0,
     'norm_ffn_g_2': 64.0,
     'norm_final_g_2': 21.337}
    for name, (base, spread) in spreads.items():
        noise = np.random.default_rng([zlib.crc32(name.encode()), seed]).standard_normal(out[name].shape)
        drawn = base * np.exp(spread * noise) if base else spread * noise
        out[name] = __import__('jax').numpy.asarray(drawn.astype(out[name].dtype))
    for name, factor in factors.items():
        out[name] = (out[name] * factor).astype(out[name].dtype)
    return out
```

```python
from contextlib import ExitStack

import numpy as np

import concourse.bass as bass
from concourse import mybir

F32 = mybir.dt.float32
F32R = mybir.dt.float32r
ALU = mybir.AluOpType
ACT = mybir.ActivationFunctionType
AX = mybir.AxisListType

P = 128
D = 2048
KD = D // P
META = 16
SEQ = 256
T = META + SEQ
HEADS = 8
FF = 5632
KF = FF // P
HALF = KF // 2
EPS = 1e-6
NEG = -1e30
WIN = 16
GRID = 64
SLAB = 2048
LEVELS = [1, 2, 4, 8, 16, 32, 64]

VEC_ROWS = [("mix_g", 16), ("na_q_g", 1), ("na_k_g", 1), ("cq_g", 4), ("ckv_g", 2), ("mq_g", 2), ("mk_g", 2),
            ("na_out_g", 8), ("mla_out_g", 8), ("ffn_g", 16), ("cw0", 44), ("cw1", 44), ("cw2", 44), ("cb", 44),
            ("b_ada", 96), ("mix2_g", 16), ("vw0", 8), ("vw1", 8), ("vw2", 8), ("lb0", 8), ("lb1", 8),
            ("gnorm_g", 1), ("ffn2_g", 16), ("fin_g", 16), ("c", 16)]
VEC = {}
NVEC = 0
for _name, _n in VEC_ROWS:
    VEC[_name] = NVEC
    NVEC += _n

CONST_COLS = [("ident", 128), ("ones", 128), ("rot", 64), ("cos", T), ("sin", T), ("namask", 256),
              ("lmask", 128 * (len(LEVELS) + 1)), ("eps", 1)]
CST = {}
NCONST = 0
for _name, _n in CONST_COLS:
    CST[_name] = NCONST
    NCONST += _n


def constants():
    out = np.zeros((P, NCONST), np.float32)

    def put(name, a):
        out[:a.shape[0], CST[name]:CST[name] + a.shape[1]] = a

    put("ident", np.eye(P, dtype=np.float32))
    put("ones", np.ones((P, P), np.float32))
    rot = np.zeros((64, 64), np.float32)
    for i in range(32):
        rot[32 + i, i] = -1.0
        rot[i, 32 + i] = 1.0
    put("rot", rot)
    inv = np.float32(10000.0) ** (-np.arange(0, 64, 2, dtype=np.float32) / np.float32(64))
    ang = np.arange(T, dtype=np.float32)[None, :] * inv[:, None]
    put("cos", np.concatenate([np.cos(ang), np.cos(ang)], 0).astype(np.float32))
    put("sin", np.concatenate([np.sin(ang), np.sin(ang)], 0).astype(np.float32))
    qc = np.arange(P) % GRID
    start = np.clip(qc - WIN // 2, 0, GRID - WIN)
    kc = np.arange(SEQ) % GRID
    ok = (kc[None, :] >= start[:, None]) & (kc[None, :] < start[:, None] + WIN)
    put("namask", np.where(ok, 0.0, NEG).astype(np.float32))
    s = np.arange(P)[:, None]
    t = np.arange(P)[None, :]
    masks = [(s == t)]
    for m in LEVELS:
        masks.append((s // (2 * m) == t // (2 * m)) & ((s // m) % 2 == 0) & ((t // m) % 2 == 1))
    put("lmask", np.concatenate(masks, 1).astype(np.float32))
    put("eps", np.full((P, 1), EPS, np.float32))
    return out


class Engine:

    def __init__(self, eng, sem):
        self.eng, self.sem, self.n, self.seen = eng, sem, 0, {}

    def need(self, toks):
        for t in toks:
            if t is None:
                continue
            if isinstance(t, list):
                self.need(t)
                continue
            sem, value = t
            if self.seen.get(id(sem), 0) < value:
                self.seen[id(sem)] = value
                self.eng.wait_ge(sem, value)

    def run(self, fn, *toks):
        self.need(toks)
        fn(self.eng)

    def do(self, fn, *toks):
        self.need(toks)
        self.n += 1
        fn(self.eng).then_inc(self.sem, 1)
        return (self.sem, self.n)

    def dma(self, fn, sem, value, *toks):
        self.need(toks)
        fn(self.eng).then_inc(sem, 16)
        return (sem, value)


class Ring:
    def __init__(self, aps):
        self.aps, self.free, self.i = aps, [[] for _ in aps], 0

    def take(self):
        k = self.i % len(self.aps)
        self.i += 1
        return k, self.aps[k], self.free[k]


class Operand:

    def __init__(self, h, l):
        self.h, self.l = h, l
        self.tok = [[] for _ in range(h.shape[1])]


def build(nc, A, out):
    ctx = ExitStack()
    with ctx:
        base = (nc.sbuf_base + 31) // 32 * 32
        limit = nc.sbuf_usable_end
        cursor = [base]

        def at(name, shape, dt, offset):
            size = 4 * int(np.prod(shape[1:]))
            assert offset + size <= limit, (name, offset, size, limit)
            return nc.alloc_sbuf_tensor_at(name, shape, dt, offset=offset), offset + size

        def sb(name, shape, dt=F32):
            t, cursor[0] = at(name, shape, dt, cursor[0])
            cursor[0] = (cursor[0] + 31) // 32 * 32
            return t

        sems = {}

        def sem(name):
            sems[name] = ctx.enter_context(nc.semaphore(name))
            return sems[name]

        pe, act, dve, pool, sp = (Engine(eng, sem(f"s_{n}")) for n, eng in (
            ("pe", nc.tensor), ("act", nc.scalar), ("dve", nc.vector), ("pool", nc.gpsimd), ("sp", nc.sync)))

        NR, NS = 3, 3
        raw = [sb(f"raw{i}", [P, SLAB]) for i in range(NR)]
        wh = [sb(f"wh{i}", [P, SLAB], F32R) for i in range(NS)]
        wl = [sb(f"wl{i}", [P, SLAB], F32R) for i in range(NS)]
        xh = sb("xh", [P, KD, T], F32R)
        xl = sb("xl", [P, KD, T], F32R)
        hoff = cursor[0]
        H = sb("H", [P, KD, T])
        cst = sb("cst", [P, NCONST])
        vec = sb("vec", [P, NVEC])
        small = sb("small", [P, 256])
        TMP = [sb(f"tmp{i}", [P, T]) for i in range(5)]
        ada_off = cursor[0]
        ada_raw = [sb(f"ada_raw{i}", [P, 2, 512]) for i in range(2)]
        ada_acc = sb("ada_acc", [P, 512])
        mod = sb("mod", [P, 96])
        arena = cursor[0]

        ps = [ctx.enter_context(nc.psum_tensor(f"ps{i}", [P, 512], F32)) for i in range(8)]
        main_free = [[] for _ in range(4)]
        x_free = [[] for _ in range(4)]
        PX = ps[4:8]

        def V(name, j=0, n=1):
            return vec[:, VEC[name] + j:VEC[name] + j + n]

        def C(name, n, rows=P):
            return cst[0:rows, CST[name]:CST[name] + n]

        ident, ones = C("ident", P), C("ones", P)
        eps = C("eps", 1)

        def lmask(i):
            return cst[:, CST["lmask"] + 128 * i:CST["lmask"] + 128 * (i + 1)]

        s_cst = sem("s_cst")
        s_vec = sem("s_vec")
        s_h = [sem(f"s_h{i}") for i in range(2)]
        hT = A["hT"].rearrange("(c p) t -> p c t", p=P)
        t_h = []
        for i in range(2):
            t_h.append(sp.dma(lambda e, i=i: e.dma_start(H[:, 8 * i:8 * i + 8, :], hT[:, 8 * i:8 * i + 8, :]), s_h[i], 16))
        t_vec = act.dma(lambda e: e.dma_start(vec[:, :], A["vecs"]), s_vec, 16)
        t_cst = act.dma(lambda e: e.dma_start(cst[:, :], A["consts"]), s_cst, 16)

        plan, loads, splits, peds = [], [], [], []
        s_raw = [sem(f"s_raw{i}") for i in range(NR)]

        def add(key, w, k0, nk, c0, ncols):
            step = min(SLAB // ncols, nk)
            view = w.rearrange("(c p) n -> p c n", p=P)
            for k in range(0, nk, step):
                n = min(step, nk - k)
                plan.append((key, view[:, k0 + k:k0 + k + n, c0:c0 + ncols], k, n, ncols, k + n == nk))

        def load(i):
            slot = i % NR
            _, view, _, n, ncols, _ = plan[i]
            dst = raw[slot][:, 0:n * ncols].rearrange("p (c n) -> p c n", c=n)
            loads.append(sp.dma(lambda e: e.dma_start(dst, view), s_raw[slot], 16 * (i // NR + 1),
                                splits[i - NR] if i >= NR else None))

        def split(i):
            while len(loads) <= i:
                load(len(loads))
            size = plan[i][3] * plan[i][4]
            src = raw[i % NR][:, 0:size]
            hi, lo = wh[i % NS][:, 0:size], wl[i % NS][:, 0:size]
            done = peds[i - NS] if i >= NS else None
            a = act.do(lambda e: e.activation(hi, src, ACT.Copy), loads[i], done)
            d = dve.do(lambda e: e.tensor_tensor(lo, src, hi.bitcast(F32), ALU.subtract), loads[i], a, done)
            splits.append([a, d])

        lanes = []

        def pump():
            for g in list(lanes):
                if next(g, "end") == "end":
                    lanes.remove(g)

        def drain(*gens):
            while any(g in lanes for g in gens):
                pump()

        at_slab = [0]

        def gemm(key, X, t0, t1, tiles, banks, kx=0):
            n = t1 - t0
            for b in banks:
                pe.need(main_free[b])
            while True:
                i = at_slab[0]
                assert plan[i][0] == key, (plan[i][0], key)
                while len(splits) < min(len(plan), i + NS):
                    split(len(splits))
                _, _, k0, nk, ncols, last = plan[i]
                pe.need(splits[i])
                w_h = wh[i % NS][:, 0:nk * ncols].rearrange("p (c n) -> p c n", c=nk)
                w_l = wl[i % NS][:, 0:nk * ncols].rearrange("p (c n) -> p c n", c=nk)
                for c in range(nk):
                    k = k0 + c
                    pe.need(X.tok[kx + k])
                    x_h, x_l = X.h[:, kx + k, t0:t1], X.l[:, kx + k, t0:t1]
                    end = last and c == nk - 1
                    for j, (o, w) in enumerate(tiles):
                        dst = ps[banks[j]][0:w, 0:n]
                        a, b = w_h[:, c, o:o + w], w_l[:, c, o:o + w]
                        pe.run(lambda e, d=dst, a=a, x=x_h, s=(k == 0): e.matmul(d, a, x, start=s, stop=False))
                        pe.run(lambda e, d=dst, a=a, x=x_l: e.matmul(d, a, x, start=False, stop=False))
                        f = lambda e, d=dst, a=b, x=x_h, s=end: e.matmul(d, a, x, start=False, stop=s)
                        if c == nk - 1 and j == len(tiles) - 1:
                            peds.append(pe.do(f))
                        else:
                            pe.run(f)
                    if c == nk // 2 - 1:
                        pump()
                at_slab[0] += 1
                pump()
                if last:
                    return peds[-1]

        PAIR = [(0, 128), (128, 128)]
        parity = [0]

        def two():
            parity[0] ^= 1
            return [0, 1] if parity[0] else [2, 3]

        tmp = Ring(TMP)
        rstd_buf = sb("rstd", [P, T])
        arena = cursor[0]
        rstd_free = [[]]

        def rstd_of(chunks, toks, n, t0, t1):
            m = t1 - t0
            bank = PX[0]
            pe.need([x_free[0], t_cst])
            last = None
            for i, (c, tk) in enumerate(zip(chunks, toks)):
                k, buf, free = tmp.take()
                a = act.do(lambda e, c=c, b=buf: e.activation(b[:, 0:m], c, ACT.Square), tk, free)
                last = pe.do(lambda e, b=buf, s=(i == 0), z=(i == len(chunks) - 1):
                             e.matmul(bank[:, 0:m], ones, b[:, 0:m], start=s, stop=z), a)
                tmp.free[k] = [last]
            r = rstd_buf[:, 0:m]
            a = act.do(lambda e: e.activation(r, bank[:, 0:m], ACT.Sqrt, bias=eps, scale=1.0 / n), last, rstd_free[0])
            x_free[0] = [a]
            return r, dve.do(lambda e: e.reciprocal(r, r), a)

        def norm_to(chunks, toks, n, t0, t1, gain, dst, d0, dst_free, shift=None):
            m = t1 - t0
            r, tr = rstd_of(chunks, toks, n, t0, t1)
            ends = []
            for i, c in enumerate(chunks):
                k, buf, free = tmp.take()
                x = buf[:, 0:m]
                h, l = dst.h[:, d0 + i, t0:t1], dst.l[:, d0 + i, t0:t1]
                b = dve.do(lambda e, x=x, c=c, i=i: e.scalar_tensor_tensor(
                    out=x, in0=c, scalar=gain(i), in1=r, op0=ALU.mult, op1=ALU.mult), tr, toks[i], free, t_vec)
                if shift is None:
                    a = act.do(lambda e, h=h, x=x: e.activation(h, x, ACT.Copy), b, dst_free)
                    s = dve.do(lambda e, l=l, x=x, h=h: e.tensor_tensor(l, x, h.bitcast(F32), ALU.subtract), a, b, dst_free)
                else:
                    a = act.do(lambda e, h=h, x=x, i=i: e.activation(h, x, ACT.Identity, bias=shift(i)), b, dst_free)
                    s = dve.do(lambda e, l=l, x=x, h=h, i=i: e.scalar_tensor_tensor(
                        out=l, in0=x, scalar=shift(i), in1=h.bitcast(F32), op0=ALU.add, op1=ALU.subtract), a, b, dst_free)
                tmp.free[k] = [a, s]
                dst.tok[d0 + i] = [a, s]
                ends = [a, s]
            rstd_free[0] = ends
            return ends

        def split_to(x, tok, dst, c, t0, t1, free):
            h, l = dst.h[:, c, t0:t1], dst.l[:, c, t0:t1]
            a = act.do(lambda e: e.activation(h, x, ACT.Copy), tok, free)
            s = dve.do(lambda e: e.tensor_tensor(l, x, h.bitcast(F32), ALU.subtract), a, tok, free)
            dst.tok[c] = [a, s]
            return [a, s]

        X = Operand(xh, xl)
        w_in, w_qup, w_kvup, w_out_, w_gate, w_up, w_down = (
            A[n] for n in ("w_in", "w_q_up", "w_kv_up", "w_out", "w_gate", "w_up", "w_down"))
        for g in range(2):
            add(("cq", g), w_in, 0, 16, 3072 + 256 * g, 256)
        add(("ckv", 0), w_in, 0, 16, 3584, 256)
        add(("kpe", 0), w_in, 0, 16, 3840, 64)
        for p in range(4):
            add(("qup", p), w_qup, 0, 4, 384 * p, 384)
            add(("kvup", p), w_kvup, 0, 2, 512 * p, 512)
            for n in range(3):
                add(("na", p, n), w_in, 0, 16, 1024 * n + 256 * p, 256)
        for g in range(8):
            add(("out", g), w_out_, 0, 16, 256 * g, 256)

        def plan_ffn(b, wg, wu, wd):
            for f in range(2):
                for g in range(HALF // 2):
                    add((b, "gate", f, g), wg, 0, 16, 128 * (HALF * f + 2 * g), 256)
                    add((b, "up", f, g), wu, 0, 16, 128 * (HALF * f + 2 * g), 256)
                for g in range(8):
                    add((b, "down", f, g), wd, HALF * f, HALF, 256 * g, 256)

        plan_ffn(1, w_gate, w_up, w_down)
        w_in2 = A["w_in_2"]
        for p in range(4):
            for n, c0 in (("q", 3072), ("f", 4096), ("i", 5120), ("g", 6144)):
                add((n, p), w_in2, 0, 16, c0 + 256 * p, 256)
        for p in range(4):
            for n, c0 in (("ac", 1024), ("ax", 2048), ("ab", 0)):
                add((n, p), w_in2, 0, 16, c0 + 256 * p, 256)
        for g in range(8):
            add(("ga", g), w_in2, 0, 16, 7168 + 256 * g, 256)
            add(("gb", g), w_in2, 0, 16, 9216 + 256 * g, 256)
            add(("ya", g), A["w_conv_out_2"], 0, 8, 256 * g, 256)
            add(("yb", g), A["w_hgrn_out_2"], 0, 8, 256 * g, 256)
        for g in range(8):
            add(("wo", g), A["w_o_2"], 0, 16, 256 * g, 256)
        plan_ffn(2, A["w_ffn_gate_2"], A["w_ffn_up_2"], A["w_ffn_down_2"])

        s_ada = [sem(f"s_ada{i}") for i in range(2)]
        cact = small[:, 0:16]
        sig_c = act.do(lambda e: e.activation(cact, V("c", 0, 16), ACT.Silu), t_vec)
        mod_tok = []

        def ada_lane():
            w = A["w_ada_2"].rearrange("(c p) n -> p c n", p=P)
            free = [None, None]
            acc_free = None
            i = 0
            for g in range(24):
                prev = None
                for k in range(0, 16, 2):
                    slot = i % 2
                    src = w[:, k:k + 2, 512 * g:512 * g + 512]
                    ld = sp.dma(lambda e, d=ada_raw[slot], s=src: e.dma_start(d[:, :, :], s), s_ada[slot],
                                16 * (i // 2 + 1), free[slot])
                    for c in range(2):
                        s = cact[:, k + c:k + c + 1]
                        r = ada_raw[slot][:, c, :]
                        if k + c == 0:
                            prev = pool.do(lambda e, r=r, s=s: e.tensor_scalar(ada_acc[:, :], r, s, None, ALU.mult),
                                           ld, sig_c, acc_free)
                        else:
                            t = pool.do(lambda e, r=r, s=s: e.tensor_scalar(r, r, s, None, ALU.mult), ld, sig_c)
                            prev = pool.do(lambda e, r=r: e.tensor_tensor(ada_acc[:, :], r, ada_acc[:, :], ALU.add), t, prev)
                    free[slot] = prev
                    i += 1
                    yield
                yield
                pe.need(x_free[3])
                for j in range(4):
                    last = pe.do(lambda e, j=j: e.matmul(PX[3][:, j:j + 1], ada_acc[:, 128 * j:128 * j + 128],
                                                         ones[:, 0:1], start=True, stop=True), prev, t_cst)
                acc_free = last
                m = dve.do(lambda e, g=g: e.tensor_tensor(mod[:, 4 * g:4 * g + 4], PX[3][:, 0:4],
                                                          V("b_ada", 4 * g, 4), ALU.add), last, t_vec)
                x_free[3] = [m]
                mod_tok[:] = [m]
                yield

        Hc = [H[:, c, :] for c in range(KD)]
        norm_to(Hc, [t_h[c // 8] for c in range(KD)], D, 0, T, lambda i: V("mix_g", i), X, 0, None)
        h0_read = [pe_tok for pe_tok in [rstd_free[0]]]

        cursor[0] = arena
        cqh = sb("cqh", [P, 4, T], F32R)
        cql = sb("cql", [P, 4, T], F32R)
        ckvh = sb("ckvh", [P, 2, T], F32R)
        ckvl = sb("ckvl", [P, 2, T], F32R)
        kpe = sb("kpe", [64, T])
        kpe2 = sb("kpe2", [64, T])
        shared = cursor[0]
        cq = sb("cq", [P, 4, T])
        ckv = sb("ckv", [P, 2, T])
        cursor[0] = shared
        mla_q = [sb(f"mla_q{i}", [P, T]) for i in range(2)]
        mla_qr = [sb(f"mla_qr{i}", [64, T]) for i in range(2)]
        mla_k = [sb(f"mla_k{i}", [P, T]) for i in range(2)]
        mla_kr = [sb(f"mla_kr{i}", [64, T]) for i in range(2)]
        mla_v = [sb(f"mla_v{i}", [P, T]) for i in range(2)]
        na_q = [[sb(f"na{n}{i}{j}", [P, T]) for n in "qkv"] for i in range(1) for j in range(2)]
        na_bias = [sb(f"na_bias{j}", [P, 2, T]) for j in range(2)]
        lane_vt = [sb(f"vt{j}", [P, 3, P]) for j in range(4)]
        lane_p = [sb(f"lp{j}", [P, T]) for j in range(4)]
        lane_pt = [sb(f"lpt{j}", [P, 3, P]) for j in range(4)]
        lane_r = [sb(f"lr{j}", [P, T]) for j in range(4)]
        lane_c = [sb(f"lc{j}", [P, 4]) for j in range(4)]
        out_a, _ = at("out_a", [P, 8, T], F32, hoff)
        out_b, _ = at("out_b", [P, 8, T], F32, hoff + 8 * T * 4)
        Xq, Xkv = Operand(cqh, cql), Operand(ckvh, ckvl)

        def evac(bank, w, n, dst, *toks):
            t = act.do(lambda e: e.activation(dst, ps[bank][0:w, 0:n], ACT.Copy), *toks)
            main_free[bank] = [t]
            return t

        cq_tok = []
        for g in range(2):
            b = two()
            t = gemm(("cq", g), X, 0, T, PAIR, b)
            cq_tok += [evac(b[j], P, T, cq[:, 2 * g + j, :], t) for j in range(2)]
        b = two()
        t = gemm(("ckv", 0), X, 0, T, PAIR, b)
        ckv_tok = [evac(b[j], P, T, ckv[:, j, :], t) for j in range(2)]
        b = two()
        t = gemm(("kpe", 0), X, 0, T, [(0, 64)], b)
        main_free[b[1]] = main_free[b[1]]
        kp = evac(b[0], 64, T, kpe[:, :], t)
        cq_read = norm_to([cq[:, c, :] for c in range(4)], cq_tok, 512, 0, T, lambda i: V("cq_g", i), Xq, 0, None)
        cq_read = cq_read + norm_to([ckv[:, c, :] for c in range(2)], ckv_tok, 256, 0, T, lambda i: V("ckv_g", i), Xkv, 0, None)
        kp2 = act.do(lambda e: e.activation(kpe2[:, :], kpe[:, :], ACT.Square), kp)
        gq = small[:, 32:36]
        sc_m = float(192) ** -0.5
        sc_n = float(128) ** -0.5
        t_g = [dve.do(lambda e: e.tensor_scalar(gq[:, 0:2], V("mq_g", 0, 2), sc_m, None, ALU.mult), t_vec),
               dve.do(lambda e: e.tensor_scalar(gq[:, 2:3], V("na_q_g"), sc_n, None, ALU.mult), t_vec)]
        cos, sin = C("cos", T, 64), C("sin", T, 64)

        def rope(x, tok, bank, bank_tok, buf, buf_tok):
            m = pe.do(lambda e: e.matmul(bank[0:64, 0:T], C("rot", 64, 64), x, start=True, stop=True), tok, bank_tok, t_cst)
            a = dve.do(lambda e: e.tensor_tensor(buf[0:64, 0:T], bank[0:64, 0:T], sin, ALU.mult), m, buf_tok)
            c = pool.do(lambda e: e.tensor_tensor(x, x, cos, ALU.mult), m, t_cst)
            return dve.do(lambda e: e.tensor_tensor(x, x, buf[0:64, 0:T], ALU.add), a, c), a

        g0 = dve.do(lambda e: e.tensor_scalar(kpe[:, :], kpe[:, :], vec[0:64, VEC["mk_g"] + 1:VEC["mk_g"] + 2], None, ALU.mult), kp2, kp)
        kpe_tok, t = rope(kpe[:, :], g0, PX[1], x_free[1], lane_r[1], None)
        x_free[1] = [t]
        lane_free = [None, None, None, None]
        QT = [(META, P), (META + P, P), (0, META)]

        def attend(lane, S_mms, bias, first_tok, v, v_tok, dst, keys_of):
            bank, pb, ptb, vt, cc = PX[lane], lane_p[lane], lane_pt[lane], lane_vt[lane], lane_c[lane]
            free = x_free[lane]
            for j, (o, n) in enumerate(QT):
                m = pe.do(lambda e, j=j, o=o, n=n: e.transpose(bank[0:n, P * j:P * j + P], v[:, o:o + n], ident), v_tok, free, t_cst)
            vt_tok = [act.do(lambda e: e.activation(vt[:, 0:2, :], bank[:, 0:256].rearrange("p (a b) -> p a b", a=2), ACT.Copy), m, lane_free[lane]),
                      act.do(lambda e: e.activation(vt[0:META, 2, :], bank[0:META, 256:384], ACT.Copy), m)]
            free = vt_tok
            outs = []
            pv_tok = None
            yield
            for j, (o, n) in enumerate(QT):
                nk = keys_of(j)
                k = len(S_mms)
                for i, (l, r, tk) in enumerate(S_mms):
                    m = pe.do(lambda e, l=l, r=r, i=i: e.matmul(bank[0:n, 0:nk], l[:, o:o + n], r[:, 0:nk],
                                                                start=(i == 0), stop=(i == k - 1)), free, first_tok, tk)
                src = bank[0:n, 0:nk]
                dep = m
                p_ = pb[0:n, 0:nk]
                if bias is not None:
                    ba, bt = bias(j)
                    dep = dve.do(lambda e: e.tensor_tensor(p_, src, ba, ALU.add), m, bt, outs[-3:], pv_tok)
                    free_s = dep
                    src = p_
                mx = dve.do(lambda e, src=src: e.tensor_reduce(cc[0:n, 0:1], src, AX.X, ALU.max, negate=True), dep, pv_tok)
                ex = act.do(lambda e, src=src: e.activation(p_, src, ACT.Exp, bias=cc[0:n, 0:1], accum_out=cc[0:n, 1:2]), mx, dep, pv_tok)
                rc = dve.do(lambda e: e.reciprocal(cc[0:n, 2:3], cc[0:n, 1:2]), ex)
                nm = pool.do(lambda e: e.tensor_scalar(p_, p_, cc[0:n, 2:3], None, ALU.mult), rc, ex)
                yield
                tiles = [t for t in range(3) if QT[t][0] < nk]
                for t in tiles:
                    ko, kn = QT[t]
                    m = pe.do(lambda e, t=t, ko=ko, kn=kn: e.transpose(bank[0:kn, P * t:P * t + n], p_[:, ko:ko + kn], ident[0:n, 0:n]), nm, ex, dep)
                pt_tok = []
                if len(tiles) == 3:
                    pt_tok.append(act.do(lambda e: e.activation(
                        ptb[:, 0:2, 0:n], bank[:, 0:256].rearrange("p (a b) -> p a b", a=2)[:, :, 0:n], ACT.Copy), m, pv_tok))
                pt_tok.append(act.do(lambda e: e.activation(ptb[0:META, 2, 0:n], bank[0:META, 256:256 + n], ACT.Copy), m, pv_tok))
                yield
                for i, t in enumerate(tiles):
                    kn = QT[t][1]
                    m = pe.do(lambda e, t=t, kn=kn, i=i: e.matmul(bank[:, 384:384 + n], vt[0:kn, t, :], ptb[0:kn, t, 0:n],
                                                                  start=(i == 0), stop=(i == len(tiles) - 1)), pt_tok, vt_tok)
                pv_tok = m
                w = act.do(lambda e: e.activation(dst[:, o:o + n], bank[:, 384:384 + n], ACT.Copy), m)
                outs.append(w)
                free = [w, pt_tok]
                yield
            x_free[lane] = [outs[-1]]
            lane_free[lane] = [outs[-1]]
            return outs

        def head_rstd(lane, mms, n, free_buf):
            bank, r = PX[lane], lane_r[lane]
            for i, (o, x, tk) in enumerate(mms):
                m = pe.do(lambda e, o=o, x=x, i=i: e.matmul(bank[:, 0:T], o, x, start=(i == 0), stop=(i == len(mms) - 1)),
                          tk, x_free[lane], t_cst)
            a = act.do(lambda e: e.activation(r[:, :], bank[:, 0:T], ACT.Sqrt, bias=eps, scale=1.0 / n), m, free_buf)
            x_free[lane] = [a]
            return dve.do(lambda e: e.reciprocal(r[:, :], r[:, :]), a)

        outa_tok, outb_tok = [None] * 8, [None] * 8
        mla_free = [None, None]
        na_free = [None, None]
        ones64 = cst[0:64, CST["ones"]:CST["ones"] + 128]

        def mla_lane(j, head, tq, tqr, tk, tv):
            lane = 2 + j
            q, qr, k, kr, v, r = mla_q[j], mla_qr[j], mla_k[j], mla_kr[j], mla_v[j], lane_r[lane]
            sqa, sqb = lane_p[lane], lane_pt[lane][0:64, :, :].rearrange("p a b -> p (a b)")[:, 0:T]
            a1 = act.do(lambda e: e.activation(sqa[:, :], q[:, :], ACT.Square), tq, lane_free[lane])
            a2 = act.do(lambda e: e.activation(sqb, qr[:, :], ACT.Square), tqr, lane_free[lane])
            yield
            rt = head_rstd(lane, [(ones, sqa[:, :], a1), (ones64, sqb, a2)], 192, [lane_free[lane], kpe_tok])
            m1 = pe_last = x_free[lane]
            a3 = act.do(lambda e: e.activation(sqa[:, :], k[:, :], ACT.Square), tk, rt)
            n1 = dve.do(lambda e: e.scalar_tensor_tensor(out=q[:, :], in0=q[:, :], scalar=gq[:, 0:1], in1=r[:, :], op0=ALU.mult, op1=ALU.mult), rt, t_g, a1)
            n2 = dve.do(lambda e: e.scalar_tensor_tensor(out=qr[:, :], in0=qr[:, :], scalar=gq[0:64, 1:2], in1=r[0:64, :], op0=ALU.mult, op1=ALU.mult), rt, t_g, a2)
            yield
            rt2 = head_rstd(lane, [(ones, sqa[:, :], a3), (ones64, kpe2[:, :], kp2)], 192, [n1, n2])
            n3 = dve.do(lambda e: e.scalar_tensor_tensor(out=k[:, :], in0=k[:, :], scalar=V("mk_g"), in1=r[:, :], op0=ALU.mult, op1=ALU.mult), rt2, a3)
            n4 = dve.do(lambda e: e.tensor_tensor(kr[:, :], kpe[:, :], r[0:64, :], ALU.mult), rt2, kpe_tok, mla_free[j])
            yield
            n5, t = rope(qr[:, :], n2, PX[lane], x_free[lane], sqa, a3)
            x_free[lane] = [t]
            yield
            toks = [n1, n3, n4, n5, a3]
            outs = yield from attend(lane, [(q, k, [n1, n3]), (qr, kr, [n4, n5])], None, toks, v, tv, out_b[:, head, :], lambda j: T)
            outb_tok[head] = outs
            mla_free[j] = outs

        def na_lane(j, head, tq, tk, tv, tb):
            lane = j
            (q, k, v), r, sqa, bias = na_q[j], lane_r[lane], lane_p[lane], na_bias[j]
            a1 = act.do(lambda e: e.activation(sqa[:, :], q[:, :], ACT.Square), tq, lane_free[lane])
            yield
            rt = head_rstd(lane, [(ones, sqa[:, :], a1)], 128, [lane_free[lane], kpe_tok])
            a3 = act.do(lambda e: e.activation(sqa[:, :], k[:, :], ACT.Square), tk, rt)
            n1 = dve.do(lambda e: e.scalar_tensor_tensor(out=q[:, :], in0=q[:, :], scalar=gq[:, 2:3], in1=r[:, :], op0=ALU.mult, op1=ALU.mult), rt, t_g, a1)
            yield
            rt2 = head_rstd(lane, [(ones, sqa[:, :], a3)], 128, n1)
            n3 = dve.do(lambda e: e.scalar_tensor_tensor(out=k[:, :], in0=k[:, :], scalar=V("na_k_g"), in1=r[:, :], op0=ALU.mult, op1=ALU.mult), rt2, a3)
            bt = pool.do(lambda e: e.tensor_tensor(bias[:, :, META:T], bias[:, :, META:T],
                                                   C("namask", 256).unsqueeze(1).to_broadcast([P, 2, 256]), ALU.add), tb, t_cst)
            yield

            def bias_of(t):
                return (bias[:, t, :], [bt, tb]) if t < 2 else (bias[0:META, 0, 0:META], [bt, tb])

            outs = yield from attend(lane, [(q, k, [n1, n3])], bias_of, a3, v, tv, out_a[:, head, :], lambda t: T if t < 2 else META)
            outa_tok[head] = outs
            na_free[j] = outs

        s_bias = [sem(f"s_bias{j}") for j in range(2)]
        rpb, mb = A["na_rpb"], A["na_meta_bias"]
        ROW = 7 * 31
        spread = nc.dram_tensor("spread", [HEADS, GRID * ROW], F32).ap()
        s_spread = sem("s_spread")
        for h in range(HEADS):
            src = bass.AP(tensor=rpb.tensor, offset=rpb.offset + h * 465 + 4 * 31, ap=[[0, GRID], [1, ROW]])
            t_spread = act.dma(lambda e: e.dma_start(spread[h].rearrange("(a b) -> a b", a=GRID), src), s_spread, 16 * (h + 1))
        bias_n = [0, 0]

        def load_bias(j, head):
            tok = None
            for r in range(4):
                src = bass.AP(tensor=spread.tensor, offset=spread.offset + head * GRID * ROW + (3 - r) * 31 + 15,
                              ap=[[ROW - 1, GRID], [31, 4], [1, GRID]])
                dst = na_bias[j][64 * (r % 2):64 * (r % 2) + 64, r // 2, META:T].rearrange("p (a b) -> p a b", a=4)
                bias_n[j] += 16
                tok = sp.dma(lambda e, d=dst, s=src: e.dma_start(d, s), s_bias[j], bias_n[j], na_free[j], t_spread)
            for t in range(2):
                src = bass.AP(tensor=mb.tensor, offset=mb.offset + head * META, ap=[[0, P], [1, META]])
                dst = na_bias[j][:, t, 0:META]
                bias_n[j] += 16
                tok = sp.dma(lambda e, d=dst, s=src: e.dma_start(d, s), s_bias[j], bias_n[j], na_free[j])
            return tok

        ada = ada_lane()
        na_gens, mla_gens = [], []
        tbs = None
        for p in range(4):
            drain(*mla_gens)
            t = gemm(("qup", p), Xq, 0, T, [(0, 128), (128, 64), (192, 128), (320, 64)], [0, 1, 2, 3])
            fr = [cq_read, mla_free]
            tq = [evac(2 * j, P, T, mla_q[j][:, :], t, fr) for j in range(2)]
            tqr = [evac(2 * j + 1, 64, T, mla_qr[j][:, :], t, fr) for j in range(2)]
            t = gemm(("kvup", p), Xkv, 0, T, [(128 * i, 128) for i in range(4)], [0, 1, 2, 3])
            tk = [evac(2 * j, P, T, mla_k[j][:, :], t, fr) for j in range(2)]
            tv = [evac(2 * j + 1, P, T, mla_v[j][:, :], t, fr) for j in range(2)]
            mla_gens = [mla_lane(j, 2 * p + j, tq[j], tqr[j], tk[j], tv[j]) for j in range(2)]
            lanes[0:0] = mla_gens
            drain(*na_gens)
            tbs = [load_bias(j, 2 * p + j) for j in range(2)]
            tn = []
            for n in range(3):
                b = two()
                t = gemm(("na", p, n), X, 0, T, PAIR, b)
                tn.append([evac(b[j], P, T, na_q[j][n][:, :], t, na_free[j], cq_read) for j in range(2)])
            na_gens = [na_lane(j, 2 * p + j, tn[0][j], tn[1][j], tn[2][j], tbs[j]) for j in range(2)]
            lanes[0:0] = na_gens
        w_in_done = peds[-1]
        drain(*mla_gens, *na_gens)
        lanes.append(ada)
        norm_to([out_b[:, c, :] for c in range(8)], outb_tok, 1024, 0, T, lambda i: V("mla_out_g", i), X, 8, w_in_done)
        norm_to([out_a[:, c, :] for c in range(8)], outa_tok, 1024, 0, T, lambda i: V("na_out_g", i), X, 0, w_in_done)
        t_read = [rstd_free[0], outa_tok[-1]]
        attn_end = [t_read, x_free, lane_free]
        t_h2 = []
        for i in range(2):
            t_h2.append(sp.dma(lambda e, i=i: e.dma_start(H[:, 8 * i:8 * i + 8, :], hT[:, 8 * i:8 * i + 8, :]), s_h[i], 32, t_read))
        htok = [t_h2[c // 8] for c in range(KD)]

        def residual(bank, c, t0, t1, tok, scale=None, stok=None):
            dst = H[:, c, t0:t1]
            src = ps[bank][:, 0:t1 - t0]
            if scale is None:
                t = dve.do(lambda e: e.tensor_tensor(dst, src, dst, ALU.add), tok, htok[c])
            else:
                t = dve.do(lambda e: e.scalar_tensor_tensor(out=dst, in0=src, scalar=scale, in1=dst, op0=ALU.mult, op1=ALU.add), tok, htok[c], stok)
            main_free[bank] = [t]
            htok[c] = t

        for g in range(8):
            b = two()
            t = gemm(("out", g), X, 14, T, PAIR, b)
            for j in range(2):
                residual(b[j], 2 * g + j, 14, T, t)

        cursor[0] = arena
        hidh = sb("hidh", [P, HALF, SEQ], F32R)
        hidl = sb("hidl", [P, HALF, SEQ], F32R)
        gct = [sb(f"gc{i}", [P, SEQ]) for i in range(3)]
        HID = Operand(hidh, hidl)

        def ffn(b, conv, x_done, scale=None):
            gc_ring = Ring(gct)
            gc_ring.free = [[x_done] for _ in gct]
            down_done = x_done
            t0 = 14 if conv else 16
            for f in range(2):
                for g in range(HALF // 2):
                    t = gemm((b, "gate", f, g), X, t0, T, PAIR, [0, 1])
                    gs = []
                    for j in range(2):
                        n = HALF * f + 2 * g + j
                        k, gc, free = gc_ring.take()
                        src = ps[j]
                        if conv:
                            a = act.do(lambda e, gc=gc, src=src, n=n: e.activation(gc[:, :], src[:, 2:258], ACT.Identity, bias=V("cb", n), scale=V("cw1", n)), t, free, t_vec)
                            d = dve.do(lambda e, gc=gc, src=src, n=n: e.scalar_tensor_tensor(
                                out=gc[:, :], in0=src[:, 1:257], scalar=V("cw0", n), in1=gc[:, :], op0=ALU.mult, op1=ALU.add), a)
                            d = dve.do(lambda e, gc=gc, src=src, n=n: e.scalar_tensor_tensor(
                                out=gc[:, 0:255], in0=src[:, 3:258], scalar=V("cw2", n), in1=gc[:, 0:255], op0=ALU.mult, op1=ALU.add), d)
                            s = act.do(lambda e, gc=gc: e.activation(gc[:, :], gc[:, :], ACT.Silu), d)
                            main_free[j] = [d]
                        else:
                            s = act.do(lambda e, gc=gc, src=src: e.activation(gc[:, :], src[:, 0:256], ACT.Silu), t, free)
                            main_free[j] = [s]
                        gs.append((k, gc, s))
                    t = gemm((b, "up", f, g), X, 16, T, PAIR, [2, 3])
                    for j in range(2):
                        k, gc, s = gs[j]
                        m = dve.do(lambda e, gc=gc, j=j: e.tensor_tensor(gc[:, :], ps[2 + j][:, 0:256], gc[:, :], ALU.mult), t, s)
                        main_free[2 + j] = [m]
                        gc_ring.free[k] = split_to(gc[:, :], m, HID, 2 * g + j, 0, SEQ, down_done)
                for g in range(8):
                    bk = two()
                    t = gemm((b, "down", f, g), HID, 0, SEQ, PAIR, bk)
                    for j in range(2):
                        c = 2 * g + j
                        residual(bk[j], c, 16, T, t, *(scale(c) if scale else ()))
                down_done = peds[-1]
            return down_done

        norm_to([H[:, c, 14:T] for c in range(KD)], htok, D, 14, T, lambda i: V("ffn_g", i), X, 0, peds[-1])
        down_done = ffn(1, True, [attn_end, peds[-1]])
        drain(ada)

        mx = small
        one_sc = mx[:, 48:80]
        sc = [dve.do(lambda e: e.tensor_scalar(one_sc[:, 0:16], mod[:, 16:32], 1.0, None, ALU.add), mod_tok),
              dve.do(lambda e: e.tensor_scalar(one_sc[:, 16:32], mod[:, 64:80], 1.0, None, ALU.add), mod_tok)]
        scg = [dve.do(lambda e: e.tensor_tensor(one_sc[:, 0:16], one_sc[:, 0:16], V("mix2_g", 0, 16), ALU.mult), sc),
               dve.do(lambda e: e.tensor_tensor(one_sc[:, 16:32], one_sc[:, 16:32], V("ffn2_g", 0, 16), ALU.mult), sc)]
        dve.need(scg)
        act.need(mod_tok)
        lbm, lbe0, lbe1, lbs, lb, oml = (mx[:, 80 + 8 * i:88 + 8 * i] for i in range(6))
        t = dve.do(lambda e: e.tensor_tensor(lbm, V("lb0", 0, 8), V("lb1", 0, 8), ALU.max), t_vec)
        t = [dve.do(lambda e: e.tensor_tensor(lbe0, V("lb0", 0, 8), lbm, ALU.subtract), t),
             dve.do(lambda e: e.tensor_tensor(lbe1, V("lb1", 0, 8), lbm, ALU.subtract), t)]
        t = [act.do(lambda e: e.activation(lbe0, lbe0, ACT.Exp), t), act.do(lambda e: e.activation(lbe1, lbe1, ACT.Exp), t)]
        t = dve.do(lambda e: e.tensor_tensor(lbs, lbe0, lbe1, ALU.add), t)
        t = dve.do(lambda e: e.reciprocal(lbs, lbs), t)
        t = dve.do(lambda e: e.tensor_tensor(lb, lbe0, lbs, ALU.mult), t)
        lb_tok = [t, dve.do(lambda e: e.tensor_scalar(oml, lb, -1.0, 1.0, ALU.mult, ALU.add), t)]

        cursor[0] = arena
        convh = sb("convh", [P, 8, SEQ], F32R)
        convl = sb("convl", [P, 8, SEQ], F32R)
        oh = sb("oh", [P, 8, SEQ], F32R)
        ol = sb("ol", [P, 8, SEQ], F32R)
        cu = sb("cu", [P, 2, SEQ])
        cy = sb("cy", [P, 2, SEQ])
        mid = cursor[0]
        hq, hf, hk, hi_, hg = (sb(f"hg_{n}", [P, 2, SEQ]) for n in "qfkig")
        hR = sb("hR", [P, 2, SEQ])
        hQ = sb("hQ", [P, 2, SEQ])
        hK = sb("hK", [P, 2, SEQ])
        hA = sb("hA", [P, 4, P])
        hB = sb("hB", [P, 2, P])
        hvt, _ = at("hvt", [P, 4, P], F32, ada_off)
        cursor[0] = mid
        merged = sb("merged", [P, KD, SEQ])
        OC, OH = Operand(convh, convl), Operand(oh, ol)

        norm_to([H[:, c, 16:T] for c in range(KD)], htok, D, 16, T, lambda i: one_sc[:, i:i + 1], X, 0, peds[-1],
                shift=lambda i: mod[:, i:i + 1])
        h_free = [down_done, mod_tok]
        hset = {"q": hq, "f": hf, "i": hi_, "g": hg}

        def hgrn_lane(p, tq, tf, ti, tg):
            bA, bB = PX[1], PX[2]
            for n in range(2):
                for b in range(2):
                    m = pe.do(lambda e, n=n, b=b: e.transpose(bA[:, 128 * (2 * n + b):128 * (2 * n + b) + 128],
                                                              hi_[:, n, 128 * b:128 * b + 128], ident), ti, x_free[1], t_cst)
            tvt = act.do(lambda e: e.activation(hvt[:, :, :], bA[:, :].rearrange("p (a b) -> p a b", a=4), ACT.Copy), m, h_free)
            tk = dve.do(lambda e: e.tensor_scalar(hk[:, :, :], hf[:, :, :], -1.0, 1.0, ALU.mult, ALU.add), tf, h_free)
            tR = dve.do(lambda e: e.memset(hR[:, :, :], 1.0), h_free)
            tP = tf
            yield
            acc = None
            bfree = [[tvt], x_free[2]]
            qsrc, ksrc, tqk = hq, hk, [tq, tk]
            prev = None
            for lv in range(len(LEVELS) + 1):
                bank = (bA, bB)[lv % 2]
                for n in range(2):
                    for b in range(2):
                        j = 2 * n + b
                        m = pe.do(lambda e, n=n, b=b, j=j, q=qsrc, k=ksrc, bank=bank: e.matmul(
                            bank[:, 128 * j:128 * j + 128], k[:, n, 128 * b:128 * b + 128], q[:, n, 128 * b:128 * b + 128],
                            start=True, stop=True), tqk, bfree[lv % 2])
                mk = lmask(lv).unsqueeze(1).to_broadcast([P, 4, P])
                bv = bank[:, :].rearrange("p (a b) -> p a b", a=4)
                if lv == 0:
                    acc = dve.do(lambda e, bv=bv, mk=mk: e.tensor_tensor(hA[:, :, :], bv, mk, ALU.mult), m, h_free, t_cst)
                    bfree[0] = [acc]
                else:
                    t1 = dve.do(lambda e, bv=bv, mk=mk: e.tensor_tensor(bv, bv, mk, ALU.mult), m)
                    acc = dve.do(lambda e, bv=bv: e.tensor_tensor(hA[:, :, :], bv, hA[:, :, :], ALU.add), t1, acc)
                    bfree[lv % 2] = [acc]
                if lv < len(LEVELS):
                    sz = LEVELS[lv]
                    if lv > 0:
                        tP, tR = grow(LEVELS[lv - 1], tP, tR, prev)
                    t2 = dve.do(lambda e: e.tensor_tensor(hQ[:, :, :], hq[:, :, :], hf[:, :, :], ALU.mult), tq, tP, m, h_free)
                    t3 = pool.do(lambda e: e.tensor_tensor(hK[:, :, :], hk[:, :, :], hR[:, :, :], ALU.mult), tk, tR, m, h_free)
                    qsrc, ksrc, tqk = hQ, hK, [t2, t3]
                    prev = [t2, t3]
                yield
            tP, tR = grow(64, tP, tR, prev)
            t2 = dve.do(lambda e: e.tensor_tensor(hQ[:, :, 128:256], hq[:, :, 128:256], hf[:, :, 128:256], ALU.mult), tP, m)
            t3 = pool.do(lambda e: e.tensor_tensor(hK[:, :, 0:128], hk[:, :, 0:128], hR[:, :, 0:128], ALU.mult), tR, m)
            yield
            for n in range(2):
                m = pe.do(lambda e, n=n: e.matmul(bA[:, 128 * n:128 * n + 128], hK[:, n, 0:128], hQ[:, n, 128:256],
                                                  start=True, stop=True), t2, t3, bfree)
            tB = act.do(lambda e: e.activation(hB[:, :, :], bA[:, 0:256].rearrange("p (a b) -> p a b", a=2), ACT.Copy), m, h_free)
            yield
            for n in range(2):
                o = 256 * n
                pe.run(lambda e, n=n, o=o: e.matmul(bB[:, o:o + 128], hvt[:, 2 * n, :], hA[:, 2 * n, :], start=True, stop=True), tB, acc, tvt, bfree)
                pe.run(lambda e, n=n, o=o: e.matmul(bB[:, o + 128:o + 256], hvt[:, 2 * n, :], hB[:, n, :], start=True, stop=False))
                m = pe.do(lambda e, n=n, o=o: e.matmul(bB[:, o + 128:o + 256], hvt[:, 2 * n + 1, :], hA[:, 2 * n + 1, :], start=False, stop=True))
            flat = lambda x: x[:, :, :].rearrange("p a b -> p (a b)")
            tO = act.do(lambda e: e.activation(flat(hQ), bB[:, :], ACT.Copy), m)
            tS = act.do(lambda e: e.activation(flat(hK), bB[:, :], ACT.Square), m)
            x_free[2] = [tS]
            yield
            m = pe.do(lambda e: e.matmul(bA[:, :], ones, flat(hK), start=True, stop=True), tS, tB)
            a = act.do(lambda e: e.activation(flat(hR), bA[:, :], ACT.Sqrt, bias=eps, scale=1.0 / 128), m, t3)
            x_free[1] = [a]
            d = dve.do(lambda e: e.reciprocal(flat(hR), flat(hR)), a)
            d = dve.do(lambda e: e.scalar_tensor_tensor(out=flat(hQ), in0=flat(hQ), scalar=V("gnorm_g"), in1=flat(hR), op0=ALU.mult, op1=ALU.mult), d, tO)
            d = pool.do(lambda e: e.tensor_tensor(flat(hQ), flat(hQ), flat(hg), ALU.mult), d, tg)
            yield
            ends = []
            for n in range(2):
                ends += split_to(hQ[:, n, :], d, OH, 2 * p + n, 0, SEQ, down_done)
            h_free[:] = ends
            yield

        def grow(m, tP, tR, used):
            Pv = hf[:, :, :].rearrange("p a (b c m) -> p (a b) c m", c=2, m=m)
            Rv = hR[:, :, :].rearrange("p a (b c m) -> p (a b) c m", c=2, m=m)
            nb = 2 * SEQ // (2 * m)
            r = dve.do(lambda e: e.tensor_tensor(Rv[:, :, 0, :], Rv[:, :, 0, :], Pv[:, :, 1, m - 1:m].to_broadcast([P, nb, m]), ALU.mult), tP, tR, used)
            q = dve.do(lambda e: e.tensor_tensor(Pv[:, :, 1, :], Pv[:, :, 1, :], Pv[:, :, 0, m - 1:m].to_broadcast([P, nb, m]), ALU.mult), r, tP, used)
            return q, r

        gen = None
        for p in range(4):
            if gen is not None:
                drain(gen)
            toks = {}
            for n in "qfig":
                b = two()
                t = gemm((n, p), X, 16, T, PAIR, b)
                o = []
                for j in range(2):
                    src, dst = ps[b[j]][:, 0:SEQ], hset[n][:, j, :]
                    c = 2 * p + j
                    if n == "i":
                        e1 = act.do(lambda e, d=dst, s=src: e.activation(d, s, ACT.Copy), t, h_free)
                    else:
                        e1 = act.do(lambda e, d=dst, s=src: e.activation(d, s, ACT.Sigmoid), t, h_free)
                        if n == "f":
                            e2 = dve.do(lambda e, d=dst, c=c: e.tensor_scalar(d, d, oml[:, c:c + 1], lb[:, c:c + 1], ALU.mult, ALU.add), e1, lb_tok)
                        else:
                            e2 = dve.do(lambda e, d=dst, s=src: e.tensor_tensor(d, s, d, ALU.mult), e1)
                            e1 = e2
                        o.append(e2)
                    main_free[b[j]] = [e1]
                    if n == "i":
                        o.append(e1)
                toks[n] = o
            gen = hgrn_lane(p, toks["q"], toks["f"], toks["i"], toks["g"])
            lanes.append(gen)
        cfree = down_done
        for p in range(4):
            b = two()
            t = gemm(("ac", p), X, 16, T, PAIR, b)
            ta = []
            for j in range(2):
                e1 = act.do(lambda e, j=j, s=b[j]: e.activation(cu[:, j, :], ps[s][:, 0:SEQ], ACT.Copy), t, cfree)
                main_free[b[j]] = [e1]
                ta.append(e1)
            b = two()
            t = gemm(("ax", p), X, 16, T, PAIR, b)
            ty = []
            for j in range(2):
                c = 2 * p + j
                u, y = cu[:, j, :], cy[:, j, :]
                d = dve.do(lambda e, u=u, s=b[j]: e.tensor_tensor(u, ps[s][:, 0:SEQ], u, ALU.mult), t, ta[j])
                main_free[b[j]] = [d]
                a = act.do(lambda e, u=u, y=y, c=c: e.activation(y, u, ACT.Copy, scale=V("vw2", c)), d, cfree)
                d = dve.do(lambda e, u=u, y=y, c=c: e.scalar_tensor_tensor(
                    out=y[:, 1:SEQ], in0=u[:, 0:SEQ - 1], scalar=V("vw1", c), in1=y[:, 1:SEQ], op0=ALU.mult, op1=ALU.add), a, d)
                d = dve.do(lambda e, u=u, y=y, c=c: e.scalar_tensor_tensor(
                    out=y[:, 2:SEQ], in0=u[:, 0:SEQ - 2], scalar=V("vw0", c), in1=y[:, 2:SEQ], op0=ALU.mult, op1=ALU.add), d)
                ty.append(d)
            b = two()
            t = gemm(("ab", p), X, 16, T, PAIR, b)
            cf = []
            for j in range(2):
                y = cy[:, j, :]
                d = dve.do(lambda e, y=y, s=b[j]: e.tensor_tensor(y, ps[s][:, 0:SEQ], y, ALU.mult), t, ty[j])
                main_free[b[j]] = [d]
                cf += split_to(y, d, OC, 2 * p + j, 0, SEQ, down_done)
            cfree = cf
        drain(gen)
        mtok = [None] * KD
        for g in range(8):
            sg = []
            for n, buf in (("ga", cu), ("gb", cy)):
                b = two()
                t = gemm((n, g), X, 16, T, PAIR, b)
                o = []
                for j in range(2):
                    e1 = act.do(lambda e, j=j, s=b[j], buf=buf: e.activation(buf[:, j, :], ps[s][:, 0:SEQ], ACT.Sigmoid), t, cfree)
                    main_free[b[j]] = [e1]
                    o.append(e1)
                sg.append(o)
            x_done = peds[-1]
            cf = []
            b = two()
            t = gemm(("ya", g), OC, 0, SEQ, PAIR, b)
            for j in range(2):
                c = 2 * g + j
                d = dve.do(lambda e, j=j, c=c, s=b[j]: e.tensor_tensor(merged[:, c, :], ps[s][:, 0:SEQ], cu[:, j, :], ALU.mult), t, sg[0][j], h_free)
                main_free[b[j]] = [d]
                mtok[c] = d
            b = two()
            t = gemm(("yb", g), OH, 0, SEQ, PAIR, b)
            for j in range(2):
                c = 2 * g + j
                d = dve.do(lambda e, j=j, s=b[j]: e.tensor_tensor(cy[:, j, :], ps[s][:, 0:SEQ], cy[:, j, :], ALU.mult), t, sg[1][j])
                main_free[b[j]] = [d]
                d = dve.do(lambda e, j=j, c=c: e.tensor_tensor(merged[:, c, :], merged[:, c, :], cy[:, j, :], ALU.add), d, mtok[c])
                mtok[c] = d
                cf.append(d)
            cfree = cf
        for c in range(KD):
            split_to(merged[:, c, :], mtok[c], X, c, 16, T, x_done)
        m_read = X.tok[KD - 1]
        for g in range(8):
            b = two()
            t = gemm(("wo", g), X, 16, T, PAIR, b)
            for j in range(2):
                c = 2 * g + j
                residual(b[j], c, 16, T, t, mod[:, 32 + c:33 + c], mod_tok)
        norm_to([H[:, c, 16:T] for c in range(KD)], htok, D, 16, T, lambda i: one_sc[:, 16 + i:17 + i], X, 0, peds[-1],
                shift=lambda i: mod[:, 48 + i:49 + i])
        ffn(2, False, [peds[-1], m_read], scale=lambda c: (mod[:, 80 + c:81 + c], mod_tok))

        r, tr = rstd_of([H[:, c, 16:T] for c in range(KD)], htok, D, 16, T)
        s_out = sem("s_out")
        oT = out.rearrange("(c p) t -> p c t", p=P)
        tot = 0
        for c in range(KD):
            d = dve.do(lambda e, c=c: e.scalar_tensor_tensor(out=H[:, c, 16:T], in0=H[:, c, 16:T], scalar=V("fin_g", c), in1=r,
                                                             op0=ALU.mult, op1=ALU.mult), tr, htok[c])
            if c % 4 == 3:
                tot += 16
                sp.dma(lambda e, c=c: e.dma_start(oT[:, c - 3:c + 1, :], H[:, c - 3:c + 1, 16:T]), s_out, tot, d)
        sp.need([(s_out, tot)])
        assert at_slab[0] == len(plan)


_WEIGHTS = ["w_in", "w_q_up", "w_kv_up", "w_out", "w_gate", "w_up", "w_down", "w_ada_2", "w_in_2", "w_conv_out_2",
            "w_hgrn_out_2", "w_o_2", "w_ffn_gate_2", "w_ffn_up_2", "w_ffn_down_2", "na_rpb", "na_meta_bias"]


def lay_out(inputs):
    a = {n: np.ascontiguousarray(inputs[n][0]) for n in _WEIGHTS}
    a["hT"] = np.ascontiguousarray(np.concatenate([inputs["meta_tokens"], inputs["x"][0]], 0).T)
    pad = np.zeros(64, np.float32)
    rows = {"mix_g": inputs["mix_norm_g"][0], "na_q_g": inputs["na_q_g"][0], "na_k_g": inputs["na_k_g"][0],
            "cq_g": inputs["mla_cq_g"][0], "ckv_g": inputs["mla_ckv_g"][0],
            "mq_g": np.concatenate([inputs["mla_q_g"][0], pad]), "mk_g": np.concatenate([inputs["mla_k_g"][0], pad]),
            "na_out_g": inputs["na_out_g"][0], "mla_out_g": inputs["mla_out_g"][0], "ffn_g": inputs["ffn_norm_g"][0],
            "cw0": inputs["conv_w"][0, 0], "cw1": inputs["conv_w"][0, 1], "cw2": inputs["conv_w"][0, 2],
            "cb": inputs["conv_b"][0], "b_ada": inputs["b_ada_2"][0], "mix2_g": inputs["norm_mix_g_2"][0],
            "vw0": inputs["conv_w_2"][0, 0], "vw1": inputs["conv_w_2"][0, 1], "vw2": inputs["conv_w_2"][0, 2],
            "lb0": inputs["lb_param_2"][0], "lb1": inputs["lb_param_2"][1], "gnorm_g": inputs["gnorm_g_2"][0],
            "ffn2_g": inputs["norm_ffn_g_2"][0], "fin_g": inputs["norm_final_g_2"], "c": inputs["c_2"][0]}
    flat = np.concatenate([np.asarray(rows[n]) for n, _ in VEC_ROWS])
    a["vecs"] = np.ascontiguousarray(flat.reshape(NVEC, P).T)
    a["consts"] = constants()
    return a


def program(nc, shapes):
    aps = {n: nc.dram_tensor(f"in_{n}", list(s), F32, kind="ExternalInput").ap() for n, s in shapes.items()}
    out = nc.dram_tensor("out_0", [D, SEQ], F32, kind="ExternalOutput").ap()
    build(nc, aps, out)


def kernel(**inputs):
    import concourse.bacc as _bacc
    from concourse.bass_utils import run_bass_kernel_spmd as _run

    inputs = {k: np.asarray(v) for k, v in inputs.items()}
    arrays = lay_out(inputs)
    nc = _bacc.Bacc("TRN2", target_bir_lowering=False, num_devices=1)
    program(nc, {n: a.shape for n, a in arrays.items()})
    r = _run(nc, [{f"in_{n}": a for n, a in arrays.items()}], core_ids=[0])
    got = r.results[0]["out_0"]
    return np.ascontiguousarray(got.T).reshape(1, SEQ, D)
```

```python
from contextlib import ExitStack

import numpy as np

import concourse.bass as bass
from concourse import mybir

F32 = mybir.dt.float32
F32R = mybir.dt.float32r
ALU = mybir.AluOpType
ACT = mybir.ActivationFunctionType
AX = mybir.AxisListType

P = 128
D = 2048
KD = D // P
META = 16
SEQ = 256
T = META + SEQ
HEADS = 8
FF = 5632
KF = FF // P
HALF = KF // 2
EPS = 1e-6
NEG = -1e30
WIN = 16
GRID = 64
SLAB = 2048
LEVELS = [1, 2, 4, 8, 16, 32, 64]

VEC_ROWS = [("mix_g", 16), ("na_q_g", 1), ("na_k_g", 1), ("cq_g", 4), ("ckv_g", 2), ("mq_g", 2), ("mk_g", 2),
            ("na_out_g", 8), ("mla_out_g", 8), ("ffn_g", 16), ("cw0", 44), ("cw1", 44), ("cw2", 44), ("cb", 44),
            ("b_ada", 96), ("mix2_g", 16), ("vw0", 8), ("vw1", 8), ("vw2", 8), ("lb0", 8), ("lb1", 8),
            ("gnorm_g", 1), ("ffn2_g", 16), ("fin_g", 16), ("c", 16)]
VEC = {}
NVEC = 0
for _name, _n in VEC_ROWS:
    VEC[_name] = NVEC
    NVEC += _n

CONST_COLS = [("ident", 128), ("ones", 128), ("rot", 64), ("cos", T), ("sin", T), ("namask", 256),
              ("eps", 1)]
CST = {}
NCONST = 0
for _name, _n in CONST_COLS:
    CST[_name] = NCONST
    NCONST += _n


def constants():
    out = np.zeros((P, NCONST), np.float32)

    def put(name, a):
        out[:a.shape[0], CST[name]:CST[name] + a.shape[1]] = a

    put("ident", np.eye(P, dtype=np.float32))
    put("ones", np.ones((P, P), np.float32))
    rot = np.zeros((64, 64), np.float32)
    for i in range(32):
        rot[32 + i, i] = -1.0
        rot[i, 32 + i] = 1.0
    put("rot", rot)
    inv = np.float32(10000.0) ** (-np.arange(0, 64, 2, dtype=np.float32) / np.float32(64))
    ang = np.arange(T, dtype=np.float32)[None, :] * inv[:, None]
    put("cos", np.concatenate([np.cos(ang), np.cos(ang)], 0).astype(np.float32))
    put("sin", np.concatenate([np.sin(ang), np.sin(ang)], 0).astype(np.float32))
    qc = np.arange(P) % GRID
    start = np.clip(qc - WIN // 2, 0, GRID - WIN)
    kc = np.arange(SEQ) % GRID
    ok = (kc[None, :] >= start[:, None]) & (kc[None, :] < start[:, None] + WIN)
    put("namask", np.where(ok, 0.0, NEG).astype(np.float32))
    put("eps", np.full((P, 1), EPS, np.float32))
    return out


def level_masks():
    s = np.arange(P)[:, None]
    t = np.arange(P)[None, :]
    masks = [(s == t)]
    for m in LEVELS:
        masks.append((s // (2 * m) == t // (2 * m)) & ((s // m) % 2 == 0) & ((t // m) % 2 == 1))
    return np.concatenate(masks, 1).astype(np.float32)


class Engine:

    def __init__(self, eng, sem):
        self.eng, self.sem, self.n, self.seen = eng, sem, 0, {}

    def need(self, toks):
        for t in toks:
            if t is None:
                continue
            if isinstance(t, list):
                self.need(t)
                continue
            sem, value = t
            if self.seen.get(id(sem), 0) < value:
                self.seen[id(sem)] = value
                self.eng.wait_ge(sem, value)

    def run(self, fn, *toks):
        self.need(toks)
        fn(self.eng)

    def do(self, fn, *toks):
        self.need(toks)
        self.n += 1
        fn(self.eng).then_inc(self.sem, 1)
        return (self.sem, self.n)

    def dma(self, fn, sem, value, *toks):
        self.need(toks)
        fn(self.eng).then_inc(sem, 16)
        return (sem, value)


class Ring:
    def __init__(self, aps):
        self.aps, self.free, self.i = aps, [[] for _ in aps], 0

    def take(self):
        k = self.i % len(self.aps)
        self.i += 1
        return k, self.aps[k], self.free[k]


class Operand:

    def __init__(self, h, l):
        self.h, self.l = h, l
        self.tok = [[] for _ in range(h.shape[1])]


def build(nc, A, out):
    ctx = ExitStack()
    with ctx:
        base = (nc.sbuf_base + 31) // 32 * 32
        limit = nc.sbuf_usable_end
        cursor = [base]

        def at(name, shape, dt, offset):
            size = 4 * int(np.prod(shape[1:]))
            assert offset + size <= limit, (name, offset, size, limit)
            return nc.alloc_sbuf_tensor_at(name, shape, dt, offset=offset), offset + size

        def sb(name, shape, dt=F32):
            t, cursor[0] = at(name, shape, dt, cursor[0])
            cursor[0] = (cursor[0] + 31) // 32 * 32
            return t

        sems = {}

        def sem(name):
            sems[name] = ctx.enter_context(nc.semaphore(name))
            return sems[name]

        pe, act, dve, pool, sp = (Engine(eng, sem(f"s_{n}")) for n, eng in (
            ("pe", nc.tensor), ("act", nc.scalar), ("dve", nc.vector), ("pool", nc.gpsimd), ("sp", nc.sync)))

        NR, NS = 3, 3
        raw = [sb(f"raw{i}", [P, SLAB]) for i in range(NR)]
        wh = [sb(f"wh{i}", [P, SLAB], F32R) for i in range(NS)]
        wl = [sb(f"wl{i}", [P, SLAB], F32R) for i in range(NS)]
        xh = sb("xh", [P, KD, T], F32R)
        xl = sb("xl", [P, KD, T], F32R)
        hoff = cursor[0]
        H = sb("H", [P, KD, T])
        cst = sb("cst", [P, NCONST])
        vec = sb("vec", [P, NVEC])
        masks, cursor[0] = nc.alloc_sbuf_tensor_at("masks", [P, 128 * (len(LEVELS) + 1)], mybir.dt.uint8, offset=cursor[0]), cursor[0] + 128 * (len(LEVELS) + 1)
        small = sb("small", [P, 256])
        tmp_off = cursor[0]
        TMP = [sb(f"tmp{i}", [P, T]) for i in range(5)]
        NA_SLOTS, AHEAD = 4, 3
        ada_off = cursor[0]
        ada_raw = [sb(f"ada_raw{i}", [P, 512]) for i in range(NA_SLOTS)]
        ada_acc = sb("ada_acc", [P, 512])
        mod = sb("mod", [P, 96])
        arena = cursor[0]

        ps = [ctx.enter_context(nc.psum_tensor(f"ps{i}", [P, 512], F32)) for i in range(8)]
        main_free = [[] for _ in range(4)]
        x_free = [[] for _ in range(4)]
        PX = ps[4:8]

        def V(name, j=0, n=1):
            return vec[:, VEC[name] + j:VEC[name] + j + n]

        def C(name, n, rows=P):
            return cst[0:rows, CST[name]:CST[name] + n]

        ident, ones = C("ident", P), C("ones", P)
        eps = C("eps", 1)

        def lmask(i):
            return masks[:, 128 * i:128 * (i + 1)]

        s_cst = sem("s_cst")
        s_vec = sem("s_vec")
        s_h = [sem(f"s_h{i}") for i in range(2)]
        hT = A["hT"].rearrange("(c p) t -> p c t", p=P)
        t_h = []
        for i in range(2):
            t_h.append(sp.dma(lambda e, i=i: e.dma_start(H[:, 8 * i:8 * i + 8, :], hT[:, 8 * i:8 * i + 8, :]), s_h[i], 16))
        t_vec = act.dma(lambda e: e.dma_start(vec[:, :], A["vecs"]), s_vec, 16)
        t_cst = act.dma(lambda e: e.dma_start(cst[:, :], A["consts"]), s_cst, 16)

        plan, loads, splits, peds = [], [], [], []
        s_raw = [sem(f"s_raw{i}") for i in range(NR)]

        def add(key, w, k0, nk, c0, ncols):
            step = min(SLAB // ncols, nk)
            view = w.rearrange("(c p) n -> p c n", p=P)
            for k in range(0, nk, step):
                n = min(step, nk - k)
                plan.append((key, view[:, k0 + k:k0 + k + n, c0:c0 + ncols], k, n, ncols, k + n == nk))

        def load(i):
            slot = i % NR
            _, view, _, n, ncols, _ = plan[i]
            dst = raw[slot][:, 0:n * ncols].rearrange("p (c n) -> p c n", c=n)
            loads.append(sp.dma(lambda e: e.dma_start(dst, view), s_raw[slot], 16 * (i // NR + 1),
                                splits[i - NR] if i >= NR else None))

        def split(i):
            while len(loads) <= i:
                load(len(loads))
            nk, ncols = plan[i][3:5]
            done = peds[i - NS] if i >= NS else None
            toks = []
            for k0, k1 in ((0, nk // 2), (nk // 2, nk)):
                part = slice(k0 * ncols, k1 * ncols)
                src, hi, lo = raw[i % NR][:, part], wh[i % NS][:, part], wl[i % NS][:, part]
                a = act.do(lambda e: e.activation(hi, src, ACT.Copy), loads[i], done)
                d = dve.do(lambda e: e.tensor_tensor(lo, src, hi.bitcast(F32), ALU.subtract), loads[i], a, done)
                toks.append([a, d])
            splits.append(toks)

        lanes = []

        def later(fn):
            def lane():
                yield
                fn()
            lanes.insert(0, lane())

        def pump():
            for g in list(lanes):
                if next(g, "end") == "end":
                    lanes.remove(g)

        def drain(*gens):
            while any(g in lanes for g in gens):
                pump()

        at_slab = [0]

        def gemm(key, X, t0, t1, tiles, banks, kx=0):
            n = t1 - t0
            for b in banks:
                pe.need(main_free[b])
            while True:
                i = at_slab[0]
                assert plan[i][0] == key, (plan[i][0], key)
                while len(splits) < min(len(plan), i + NS):
                    split(len(splits))
                _, _, k0, nk, ncols, last = plan[i]
                w_h = wh[i % NS][:, 0:nk * ncols].rearrange("p (c n) -> p c n", c=nk)
                w_l = wl[i % NS][:, 0:nk * ncols].rearrange("p (c n) -> p c n", c=nk)
                for c in range(nk):
                    k = k0 + c
                    pe.need([splits[i][0 if c < nk // 2 else 1], X.tok[kx + k]])
                    x_h, x_l = X.h[:, kx + k, t0:t1], X.l[:, kx + k, t0:t1]
                    end = last and c == nk - 1
                    for j, (o, w) in enumerate(tiles):
                        dst = ps[banks[j]][0:w, 0:n]
                        a, b = w_h[:, c, o:o + w], w_l[:, c, o:o + w]
                        pe.run(lambda e, d=dst, a=a, x=x_h, s=(k == 0): e.matmul(d, a, x, start=s, stop=False))
                        pe.run(lambda e, d=dst, a=a, x=x_l: e.matmul(d, a, x, start=False, stop=False))
                        f = lambda e, d=dst, a=b, x=x_h, s=end: e.matmul(d, a, x, start=False, stop=s)
                        if c == nk - 1 and j == len(tiles) - 1:
                            peds.append(pe.do(f))
                        else:
                            pe.run(f)
                    if c == nk // 2 - 1:
                        pump()
                at_slab[0] += 1
                pump()
                if last:
                    return peds[-1]

        PAIR = [(0, 128), (128, 128)]
        parity = [0]

        def two():
            parity[0] ^= 1
            return [0, 1] if parity[0] else [2, 3]

        tmp = Ring(TMP)
        rstd_buf = sb("rstd", [P, T])
        ssq = {n: sb(f"ssq_{n}", [P, T]) for n in "hab"}
        arena = cursor[0]
        rstd_free = [[]]

        class Squares:

            def __init__(self, name, t0, t1, count):
                self.acc, self.m, self.count, self.i, self.tok = ssq[name][:, 0:t1 - t0], t1 - t0, count, 0, None
                self.last = None

            def add(self, c, tok, free=None):
                self.i += 1
                if self.i == 1:
                    self.tok = act.do(lambda e: e.activation(self.acc, c, ACT.Square), tok, free)
                    return
                k, buf, fr = tmp.take()
                x = buf[:, 0:self.m]
                a = act.do(lambda e: e.activation(x, c, ACT.Square), tok, fr)
                if self.i < self.count:
                    self.tok = pool.do(lambda e: e.tensor_tensor(self.acc, self.acc, x, ALU.add), a, self.tok)
                    tmp.free[k] = [self.tok]
                else:
                    self.last = (k, x, a)

            def rstd(self, n):
                assert self.i == self.count
                k, x, a = self.last
                bank, r, m = PX[2], rstd_buf[:, 0:self.m], self.m
                pe.run(lambda e: e.matmul(bank[:, 0:m], ones, self.acc, start=True, stop=False), self.tok, x_free[2], t_cst)
                last = pe.do(lambda e: e.matmul(bank[:, 0:m], ones, x, start=False, stop=True), a)
                tmp.free[k] = [last]
                a = act.do(lambda e: e.activation(r, bank[:, 0:m], ACT.Sqrt, bias=eps, scale=1.0 / n), last, rstd_free[0])
                x_free[2] = [a]
                return r, dve.do(lambda e: e.reciprocal(r, r), a)

        def rstd_of(chunks, toks, n, t0, t1):
            m = t1 - t0
            bank = PX[2]
            pe.need([x_free[2], t_cst])
            last = None
            for i, (c, tk) in enumerate(zip(chunks, toks)):
                k, buf, free = tmp.take()
                a = act.do(lambda e: e.activation(buf[:, 0:m], c, ACT.Square), tk, free)
                last = pe.do(lambda e: e.matmul(bank[:, 0:m], ones, buf[:, 0:m], start=(i == 0), stop=(i == len(chunks) - 1)), a)
                tmp.free[k] = [last]
            r = rstd_buf[:, 0:m]
            a = act.do(lambda e: e.activation(r, bank[:, 0:m], ACT.Sqrt, bias=eps, scale=1.0 / n), last, rstd_free[0])
            x_free[2] = [a]
            return r, dve.do(lambda e: e.reciprocal(r, r), a)

        def norm_to(chunks, toks, n, t0, t1, gain, dst, d0, dst_free, shift=None, squares=None, deps=None):
            m = t1 - t0
            r, tr = squares.rstd(n) if squares else rstd_of(chunks, toks, n, t0, t1)
            ends = []
            for i, c in enumerate(chunks):
                k, buf, free = tmp.take()
                x = buf[:, 0:m]
                h, l = dst.h[:, d0 + i, t0:t1], dst.l[:, d0 + i, t0:t1]
                b = dve.do(lambda e: e.scalar_tensor_tensor(
                    out=x, in0=c, scalar=gain(i), in1=r, op0=ALU.mult, op1=ALU.mult), tr, toks[i], free, t_vec, deps)
                if shift is None:
                    a = act.do(lambda e: e.activation(h, x, ACT.Copy), b, dst_free)
                    low = pool if i % 3 == 2 else dve
                    s = low.do(lambda e: e.tensor_tensor(l, x, h.bitcast(F32), ALU.subtract), a, b, dst_free)
                else:
                    a = act.do(lambda e: e.activation(h, x, ACT.Identity, bias=shift(i)), b, dst_free, deps)
                    s = dve.do(lambda e: e.scalar_tensor_tensor(
                        out=l, in0=x, scalar=shift(i), in1=h.bitcast(F32), op0=ALU.add, op1=ALU.subtract), a, b, dst_free, deps)
                tmp.free[k] = [a, s]
                dst.tok[d0 + i] = [a, s]
                ends.append([a, s])
            rstd_free[0] = ends
            return ends

        def ready_sqrt():
            sqrt_tok[:] = [act.do(lambda e: e.activation(small[:, 250:251], eps, ACT.Sqrt), t_cst, sqrt_tok)]

        sqrt_tok = []

        def split_to(x, tok, dst, c, t0, t1, free):
            h, l = dst.h[:, c, t0:t1], dst.l[:, c, t0:t1]
            a = act.do(lambda e: e.activation(h, x, ACT.Copy), tok, free)
            s = dve.do(lambda e: e.tensor_tensor(l, x, h.bitcast(F32), ALU.subtract), a, tok, free)
            dst.tok[c] = [a, s]
            return [a, s]

        X = Operand(xh, xl)
        w_in, w_qup, w_kvup, w_out_, w_gate, w_up, w_down = (
            A[n] for n in ("w_in", "w_q_up", "w_kv_up", "w_out", "w_gate", "w_up", "w_down"))
        for g in range(2):
            add(("cq", g), w_in, 0, 16, 3072 + 256 * g, 256)
        add(("ckv", 0), w_in, 0, 16, 3584, 256)
        add(("kpe", 0), w_in, 0, 16, 3840, 64)
        for p in range(4):
            add(("qup", p), w_qup, 0, 4, 384 * p, 384)
            add(("kvup", p), w_kvup, 0, 2, 512 * p, 512)
            for n in range(3):
                add(("na", p, n), w_in, 0, 16, 1024 * n + 256 * p, 256)
        for n, k0 in (("outb", 8), ("outa", 0)):
            for g in range(8):
                add((n, g), w_out_, k0, 8, 256 * g, 256)

        def plan_ffn(b, wg, wu, wd):
            for f in range(2):
                for g in range(HALF // 2):
                    add((b, "gate", f, g), wg, 0, 16, 128 * (HALF * f + 2 * g), 256)
                    add((b, "up", f, g), wu, 0, 16, 128 * (HALF * f + 2 * g), 256)
                for g in range(8):
                    add((b, "down", f, g), wd, HALF * f, HALF, 256 * g, 256)

        plan_ffn(1, w_gate, w_up, w_down)
        w_in2 = A["w_in_2"]
        for p in range(4):
            for n, c0 in (("q", 3072), ("f", 4096), ("i", 5120), ("g", 6144)):
                add((n, p), w_in2, 0, 16, c0 + 256 * p, 256)
        for p in range(4):
            for n, c0 in (("ac", 1024), ("ax", 2048), ("ab", 0)):
                add((n, p), w_in2, 0, 16, c0 + 256 * p, 256)
        for g in range(8):
            add(("ga", g), w_in2, 0, 16, 7168 + 256 * g, 256)
            add(("gb", g), w_in2, 0, 16, 9216 + 256 * g, 256)
            add(("ya", g), A["w_conv_out_2"], 0, 8, 256 * g, 256)
            add(("yb", g), A["w_hgrn_out_2"], 0, 8, 256 * g, 256)
        for g in range(8):
            add(("wo", g), A["w_o_2"], 0, 16, 256 * g, 256)
        plan_ffn(2, A["w_ffn_gate_2"], A["w_ffn_up_2"], A["w_ffn_down_2"])

        s_ada = [sem(f"s_ada{i}") for i in range(NA_SLOTS)]
        cact = small[:, 0:16]
        sig_c = act.do(lambda e: e.activation(cact, V("c", 0, 16), ACT.Silu), t_vec)
        mod_tok = [None] * 24

        def ada_lane():
            w = A["w_ada_2"].rearrange("(c p) n -> p c n", p=P)
            free = [na_set_free[0]] * NA_SLOTS
            got = []

            def fetch(i):
                g, k = divmod(i, 16)
                src = w[:, k, 512 * g:512 * g + 512]
                got.append(pool.dma(lambda e: e.dma_start(ada_raw[i % NA_SLOTS][:, :], src), s_ada[i % NA_SLOTS],
                                  16 * (i // NA_SLOTS + 1), free[i % NA_SLOTS]))

            for i in range(AHEAD):
                fetch(i)
            yield
            acc_free = na_set_free[0]
            for i in range(24 * 16):
                g, k = divmod(i, 16)
                if i + AHEAD < 24 * 16:
                    fetch(i + AHEAD)
                s, r = cact[:, k:k + 1], ada_raw[i % NA_SLOTS][:, :]
                if k == 0:
                    prev = dve.do(lambda e: e.tensor_scalar(ada_acc[:, :], r, s, None, ALU.mult), got[i], sig_c, acc_free)
                else:
                    prev = dve.do(lambda e: e.scalar_tensor_tensor(
                        out=ada_acc[:, :], in0=r, scalar=s, in1=ada_acc[:, :], op0=ALU.mult, op1=ALU.add), got[i], prev)
                free[i % NA_SLOTS] = prev
                yield
                if k == 15:
                    pe.need([x_free[3]])
                    for j in range(4):
                        last = pe.do(lambda e, j=j: e.matmul(PX[3][:, j:j + 1], ada_acc[:, 128 * j:128 * j + 128],
                                                             ones[:, 0:1], start=True, stop=True), prev, t_cst)
                    acc_free = last
                    m = dve.do(lambda e: e.tensor_tensor(mod[:, 4 * g:4 * g + 4], PX[3][:, 0:4],
                                                         V("b_ada", 4 * g, 4), ALU.add), last, t_vec)
                    x_free[3] = [m]
                    mod_tok[g] = m

        def mod_until(g):
            while mod_tok[g - 1] is None:
                pump()
            return mod_tok[0:g]

        Hc = [H[:, c, :] for c in range(KD)]
        for i in range(NS):
            split(i)
        norm_to(Hc, [t_h[c // 8] for c in range(KD)], D, 0, T, lambda i: V("mix_g", i), X, 0, None)
        h0_read = [pe_tok for pe_tok in [rstd_free[0]]]

        cursor[0] = arena
        attn_off = arena
        cqh = sb("cqh", [P, 4, T], F32R)
        cql = sb("cql", [P, 4, T], F32R)
        ckvh = sb("ckvh", [P, 2, T], F32R)
        ckvl = sb("ckvl", [P, 2, T], F32R)
        kpe = sb("kpe", [64, T])
        kpe2 = sb("kpe2", [64, T])
        shared = cursor[0]
        cq = sb("cq", [P, 4, T])
        ckv = sb("ckv", [P, 2, T])
        cursor[0] = shared
        mla_q = [sb(f"mla_q{i}", [P, T]) for i in range(2)]
        mla_qr = [sb(f"mla_qr{i}", [64, T]) for i in range(2)]
        mla_k = [sb(f"mla_k{i}", [P, T]) for i in range(2)]
        mla_kr = [sb(f"mla_kr{i}", [64, T]) for i in range(2)]
        mla_v = [sb(f"mla_v{i}", [P, T]) for i in range(2)]
        mla_end = cursor[0]
        na_sets = [None, [[sb(f"na1{n}{j}", [P, T]) for n in "qkv"] for j in range(2)]]
        keep, cursor[0] = cursor[0], ada_off
        na_sets[0] = [[sb(f"na0{n}{j}", [P, T]) for n in "qkv"] for j in range(2)]
        assert cursor[0] <= ada_off + 4 * 512 * (NA_SLOTS + 1)
        cursor[0] = keep
        na_bias = [sb(f"na_bias{j}", [P, 2, T]) for j in range(2)]
        lane_vt = [sb(f"vt{j}", [P, 3, P]) for j in range(4)]
        lane_p = [sb(f"lp{j}", [P, T]) for j in range(4)]
        lane_pt = [sb(f"lpt{j}", [P, 3, P]) for j in range(4)]
        lane_r = [sb(f"lr{j}", [P, T]) for j in range(4)]
        lane_c = [sb(f"lc{j}", [P, 4]) for j in range(4)]
        out_a, _ = at("out_a", [P, 8, T], F32, hoff)
        out_b, _ = at("out_b", [P, 8, T], F32, hoff + 8 * T * 4)
        Xq, Xkv = Operand(cqh, cql), Operand(ckvh, ckvl)

        def evac(bank, w, n, dst, *toks):
            t = act.do(lambda e: e.activation(dst, ps[bank][0:w, 0:n], ACT.Copy), *toks)
            main_free[bank] = [t]
            return t

        cq_tok = []
        for g in range(2):
            b = two()
            t = gemm(("cq", g), X, 0, T, PAIR, b)
            cq_tok += [evac(b[j], P, T, cq[:, 2 * g + j, :], t) for j in range(2)]
        b = two()
        t = gemm(("ckv", 0), X, 0, T, PAIR, b)
        ckv_tok = [evac(b[j], P, T, ckv[:, j, :], t) for j in range(2)]
        b = two()
        t = gemm(("kpe", 0), X, 0, T, [(0, 64)], b)
        main_free[b[1]] = main_free[b[1]]
        kp = evac(b[0], 64, T, kpe[:, :], t)
        cq_read = norm_to([cq[:, c, :] for c in range(4)], cq_tok, 512, 0, T, lambda i: V("cq_g", i), Xq, 0, None)
        cq_read = cq_read + norm_to([ckv[:, c, :] for c in range(2)], ckv_tok, 256, 0, T, lambda i: V("ckv_g", i), Xkv, 0, None)
        kp2 = act.do(lambda e: e.activation(kpe2[:, :], kpe[:, :], ACT.Square), kp)
        gq = small[:, 32:36]
        sc_m = float(192) ** -0.5
        sc_n = float(128) ** -0.5
        t_g = [dve.do(lambda e: e.tensor_scalar(gq[:, 0:2], V("mq_g", 0, 2), sc_m, None, ALU.mult), t_vec),
               dve.do(lambda e: e.tensor_scalar(gq[:, 2:3], V("na_q_g"), sc_n, None, ALU.mult), t_vec)]
        cos, sin = C("cos", T, 64), C("sin", T, 64)

        def rope(x, tok, bank, bank_tok, buf, buf_tok):
            m = pe.do(lambda e: e.matmul(bank[0:64, 0:T], C("rot", 64, 64), x, start=True, stop=True), tok, bank_tok, t_cst)
            a = dve.do(lambda e: e.tensor_tensor(buf[0:64, 0:T], bank[0:64, 0:T], sin, ALU.mult), m, buf_tok)
            c = dve.do(lambda e: e.tensor_tensor(x, x, cos, ALU.mult), m, t_cst)
            return dve.do(lambda e: e.tensor_tensor(x, x, buf[0:64, 0:T], ALU.add), a, c), a

        g0 = dve.do(lambda e: e.tensor_scalar(kpe[:, :], kpe[:, :], vec[0:64, VEC["mk_g"] + 1:VEC["mk_g"] + 2], None, ALU.mult), kp2, kp)
        kpe_tok, t = rope(kpe[:, :], g0, PX[1], x_free[1], lane_r[1], None)
        x_free[1] = [t]
        lane_free = [None, None, None, None]
        QT = [(META, P), (META + P, P), (0, META)]

        def attend(lane, S_mms, bias, first_tok, v, v_tok, dst, keys_of):
            bank, pb, ptb, vt, cc = PX[lane], lane_p[lane], lane_pt[lane], lane_vt[lane], lane_c[lane]
            free = x_free[lane]
            for j, (o, n) in enumerate(QT):
                m = pe.do(lambda e, j=j, o=o, n=n: e.transpose(bank[0:n, P * j:P * j + P], v[:, o:o + n], ident), v_tok, free, t_cst)
            vt_tok = [act.do(lambda e: e.activation(vt[:, 0:2, :], bank[:, 0:256].rearrange("p (a b) -> p a b", a=2), ACT.Copy), m, lane_free[lane]),
                      act.do(lambda e: e.activation(vt[0:META, 2, :], bank[0:META, 256:384], ACT.Copy), m)]
            free = vt_tok
            outs = []
            yield
            for j, (o, n) in enumerate(QT):
                nk = keys_of(j)
                k = len(S_mms)
                for i, (l, r, tk) in enumerate(S_mms):
                    m = pe.do(lambda e: e.matmul(bank[0:n, 0:nk], l[:, o:o + n], r[:, 0:nk],
                                                 start=(i == 0), stop=(i == k - 1)), free, first_tok, tk)
                src, p_ = bank[0:n, 0:nk], pb[0:n, 0:nk]
                if bias is not None:
                    ba, bt = bias(j)
                    dep = dve.do(lambda e: e.tensor_tensor_reduce(p_, src, ba, 1.0, -3.0e38, ALU.add, ALU.max, cc[0:n, 3:4]), m, bt, free)
                    src = p_
                    mx = dve.do(lambda e: e.tensor_scalar(cc[0:n, 0:1], cc[0:n, 3:4], -1.0, None, ALU.mult), dep)
                else:
                    dep = mx = dve.do(lambda e: e.tensor_reduce(cc[0:n, 0:1], src, AX.X, ALU.max, negate=True), m, free)
                ex = act.do(lambda e: e.activation(p_, src, ACT.Exp, bias=cc[0:n, 0:1], accum_out=cc[0:n, 1:2]), mx, dep, free)
                rc = dve.do(lambda e: e.reciprocal(cc[0:n, 2:3], cc[0:n, 1:2]), ex)
                nm = dve.do(lambda e: e.tensor_scalar(p_, p_, cc[0:n, 2:3], None, ALU.mult), rc, ex)
                yield
                tiles = [t for t in range(3) if QT[t][0] < nk]
                for t in tiles:
                    ko, kn = QT[t]
                    m = pe.do(lambda e: e.transpose(bank[0:kn, P * t:P * t + n], p_[:, ko:ko + kn], ident[0:n, 0:n]), nm, ex, dep)
                pt_tok = []
                if len(tiles) == 3:
                    pt_tok.append(act.do(lambda e: e.activation(
                        ptb[:, 0:2, 0:n], bank[:, 0:256].rearrange("p (a b) -> p a b", a=2)[:, :, 0:n], ACT.Copy), m, outs))
                pt_tok.append(act.do(lambda e: e.activation(ptb[0:META, 2, 0:n], bank[0:META, 256:256 + n], ACT.Copy), m, outs))
                yield
                for i, t in enumerate(tiles):
                    kn = QT[t][1]
                    m = pe.do(lambda e: e.matmul(bank[:, 384:384 + n], vt[0:kn, t, :], ptb[0:kn, t, 0:n],
                                                 start=(i == 0), stop=(i == len(tiles) - 1)), pt_tok, vt_tok)
                outs.append(act.do(lambda e: e.activation(dst[:, o:o + n], bank[:, 384:384 + n], ACT.Copy), m))
                free = [outs[-1], pt_tok, nm]
                yield
            x_free[lane] = [outs[-1]]
            lane_free[lane] = [outs[-1]]
            return outs

        def head_rstd(lane, mms, n, free_buf):
            bank, r = PX[lane], lane_r[lane]
            for i, (o, x, tk) in enumerate(mms):
                m = pe.do(lambda e, o=o, x=x, i=i: e.matmul(bank[:, 0:T], o, x, start=(i == 0), stop=(i == len(mms) - 1)),
                          tk, x_free[lane], t_cst)
            a = act.do(lambda e: e.activation(r[:, :], bank[:, 0:T], ACT.Sqrt, bias=eps, scale=1.0 / n), m, free_buf)
            x_free[lane] = [a]
            return dve.do(lambda e: e.reciprocal(r[:, :], r[:, :]), a)

        outa_tok, outb_tok = [None] * 8, [None] * 8
        sq_a, sq_b = Squares("a", 0, T, 8), Squares("b", 0, T, 8)
        mla_free = [None, None]
        na_free = [None, None]
        na_set_free = [[], []]
        ones64 = cst[0:64, CST["ones"]:CST["ones"] + 128]

        def mla_lane(j, head, tq, tqr, tk, tv):
            lane = 2 + j
            q, qr, k, kr, v, r = mla_q[j], mla_qr[j], mla_k[j], mla_kr[j], mla_v[j], lane_r[lane]
            sqa, sqb = lane_p[lane], lane_pt[lane][0:64, :, :].rearrange("p a b -> p (a b)")[:, 0:T]
            a1 = act.do(lambda e: e.activation(sqa[:, :], q[:, :], ACT.Square), tq, lane_free[lane])
            a2 = act.do(lambda e: e.activation(sqb, qr[:, :], ACT.Square), tqr, lane_free[lane])
            rt = head_rstd(lane, [(ones, sqa[:, :], a1), (ones64, sqb, a2)], 192, [lane_free[lane], kpe_tok])
            m1 = pe_last = x_free[lane]
            a3 = act.do(lambda e: e.activation(sqa[:, :], k[:, :], ACT.Square), tk, rt)
            n1 = dve.do(lambda e: e.scalar_tensor_tensor(out=q[:, :], in0=q[:, :], scalar=gq[:, 0:1], in1=r[:, :], op0=ALU.mult, op1=ALU.mult), rt, t_g, a1)
            n2 = dve.do(lambda e: e.scalar_tensor_tensor(out=qr[:, :], in0=qr[:, :], scalar=gq[0:64, 1:2], in1=r[0:64, :], op0=ALU.mult, op1=ALU.mult), rt, t_g, a2)
            yield
            rt2 = head_rstd(lane, [(ones, sqa[:, :], a3), (ones64, kpe2[:, :], kp2)], 192, [n1, n2])
            n3 = dve.do(lambda e: e.scalar_tensor_tensor(out=k[:, :], in0=k[:, :], scalar=V("mk_g"), in1=r[:, :], op0=ALU.mult, op1=ALU.mult), rt2, a3)
            n4 = dve.do(lambda e: e.tensor_tensor(kr[:, :], kpe[:, :], r[0:64, :], ALU.mult), rt2, kpe_tok, mla_free[j])
            yield
            n5, t = rope(qr[:, :], n2, PX[lane], x_free[lane], sqa, a3)
            x_free[lane] = [t]
            yield
            toks = [n1, n3, n4, n5, a3]
            outs = yield from attend(lane, [(q, k, [n1, n3]), (qr, kr, [n4, n5])], None, toks, v, tv, out_b[:, head, :], lambda j: T)
            outb_tok[head] = outs
            mla_free[j] = outs
            sq_b.add(out_b[:, head, :], outs)

        def na_lane(j, head, tq, tk, tv, tb):
            lane = j
            (q, k, v), r, sqa, bias = na_sets[head // 2 % 2][j], lane_r[lane], lane_p[lane], na_bias[j]
            a1 = act.do(lambda e: e.activation(sqa[:, :], q[:, :], ACT.Square), tq, lane_free[lane])
            yield
            rt = head_rstd(lane, [(ones, sqa[:, :], a1)], 128, [lane_free[lane], kpe_tok])
            a3 = act.do(lambda e: e.activation(sqa[:, :], k[:, :], ACT.Square), tk, rt)
            n1 = dve.do(lambda e: e.scalar_tensor_tensor(out=q[:, :], in0=q[:, :], scalar=gq[:, 2:3], in1=r[:, :], op0=ALU.mult, op1=ALU.mult), rt, t_g, a1)
            yield
            rt2 = head_rstd(lane, [(ones, sqa[:, :], a3)], 128, n1)
            n3 = dve.do(lambda e: e.scalar_tensor_tensor(out=k[:, :], in0=k[:, :], scalar=V("na_k_g"), in1=r[:, :], op0=ALU.mult, op1=ALU.mult), rt2, a3)
            bt = pool.do(lambda e: e.tensor_tensor(bias[:, :, META:T], bias[:, :, META:T],
                                                   C("namask", 256).unsqueeze(1).to_broadcast([P, 2, 256]), ALU.add), tb, t_cst)
            yield

            def bias_of(t):
                return (bias[:, t, :], [bt, tb]) if t < 2 else (bias[0:META, 0, 0:META], [bt, tb])

            outs = yield from attend(lane, [(q, k, [n1, n3])], bias_of, a3, v, tv, out_a[:, head, :], lambda t: T if t < 2 else META)
            outa_tok[head] = outs
            na_free[j] = outs
            na_set_free[head // 2 % 2] += outs
            sq_a.add(out_a[:, head, :], outs)

        s_bias = [sem(f"s_bias{j}") for j in range(2)]
        rpb, mb = A["na_rpb"], A["na_meta_bias"]
        ROW = 7 * 31
        spread = nc.dram_tensor("spread", [HEADS, GRID * ROW], F32).ap()
        s_spread = sem("s_spread")
        for h in range(HEADS):
            src = bass.AP(tensor=rpb.tensor, offset=rpb.offset + h * 465 + 4 * 31, ap=[[0, GRID], [1, ROW]])
            t_spread = act.dma(lambda e: e.dma_start(spread[h].rearrange("(a b) -> a b", a=GRID), src), s_spread, 16 * (h + 1))
        bias_n = [0, 0]

        def load_bias(j, head):
            tok = None
            for r in range(4):
                src = bass.AP(tensor=spread.tensor, offset=spread.offset + head * GRID * ROW + (3 - r) * 31 + 15,
                              ap=[[ROW - 1, GRID], [31, 4], [1, GRID]])
                dst = na_bias[j][64 * (r % 2):64 * (r % 2) + 64, r // 2, META:T].rearrange("p (a b) -> p a b", a=4)
                bias_n[j] += 16
                tok = sp.dma(lambda e, d=dst, s=src: e.dma_start(d, s), s_bias[j], bias_n[j], na_free[j], t_spread)
            for t in range(2):
                src = bass.AP(tensor=mb.tensor, offset=mb.offset + head * META, ap=[[0, P], [1, META]])
                dst = na_bias[j][:, t, 0:META]
                bias_n[j] += 16
                tok = sp.dma(lambda e, d=dst, s=src: e.dma_start(d, s), s_bias[j], bias_n[j], na_free[j])
            return tok

        ada = ada_lane()
        na_gens, mla_gens = [], []
        tbs = None
        for p in range(4):
            drain(*mla_gens)
            t = gemm(("qup", p), Xq, 0, T, [(0, 128), (128, 64), (192, 128), (320, 64)], [0, 1, 2, 3])
            fr = [cq_read, mla_free]
            tq = [evac(2 * j, P, T, mla_q[j][:, :], t, fr) for j in range(2)]
            tqr = [evac(2 * j + 1, 64, T, mla_qr[j][:, :], t, fr) for j in range(2)]
            t = gemm(("kvup", p), Xkv, 0, T, [(128 * i, 128) for i in range(4)], [0, 1, 2, 3])
            tk = [evac(2 * j, P, T, mla_k[j][:, :], t, fr) for j in range(2)]
            tv = [evac(2 * j + 1, P, T, mla_v[j][:, :], t, fr) for j in range(2)]
            mla_gens = [mla_lane(j, 2 * p + j, tq[j], tqr[j], tk[j], tv[j]) for j in range(2)]
            lanes[0:0] = mla_gens
            tn = []
            for n in range(3):
                b = two()
                t = gemm(("na", p, n), X, 0, T, PAIR, b)
                tn.append([evac(b[j], P, T, na_sets[p % 2][j][n][:, :], t, na_set_free[p % 2], cq_read) for j in range(2)])
            drain(*na_gens)
            tbs = [load_bias(j, 2 * p + j) for j in range(2)]
            na_gens = [na_lane(j, 2 * p + j, tn[0][j], tn[1][j], tn[2][j], tbs[j]) for j in range(2)]
            lanes[0:0] = na_gens
        w_in_done = peds[-1]
        drain(*mla_gens)
        norm_to([out_b[:, c, :] for c in range(8)], outb_tok, 1024, 0, T, lambda i: V("mla_out_g", i), X, 8, w_in_done, squares=sq_b)
        b_read = rstd_free[0]
        s_h2 = sem("s_h2")
        h2, _ = at("h2", [P, KD, T], F32, attn_off)
        assert attn_off + KD * T * 4 <= mla_end
        t_h2 = sp.dma(lambda e: e.dma_start(h2[:, :, :], hT), s_h2, 16, outb_tok, b_read)
        lanes.append(ada)

        def residual(bank, c, t0, t1, tok, scale=None, stok=None, src=None, free=None):
            dst = H[:, c, t0:t1]
            old = dst if src is None else src[:, c, t0:t1]
            new = ps[bank][:, 0:t1 - t0]
            if scale is None:
                t = dve.do(lambda e: e.tensor_tensor(dst, new, old, ALU.add), tok, htok[c], free)
            else:
                t = dve.do(lambda e: e.scalar_tensor_tensor(out=dst, in0=new, scalar=scale, in1=old, op0=ALU.mult, op1=ALU.add), tok, htok[c], stok)
            main_free[bank] = [t]
            htok[c] = t

        for g in range(8):
            b = two()
            t = gemm(("outb", g), X, 14, T, PAIR, b, kx=8)
            for j in range(2):
                c = 2 * g + j
                new, old = ps[b[j]][:, 0:T - 14], h2[:, c, 14:T]
                main_free[b[j]] = [dve.do(lambda e: e.tensor_tensor(old, new, old, ALU.add), t, t_h2)]
        drain(*na_gens)
        norm_to([out_a[:, c, :] for c in range(8)], outa_tok, 1024, 0, T, lambda i: V("na_out_g", i), X, 0, w_in_done, squares=sq_a)
        a_read = [rstd_free[0], b_read, outa_tok]
        htok = [None] * KD
        sq = Squares("h", 14, T, KD)
        for g in range(8):
            b = two()
            t = gemm(("outa", g), X, 14, T, PAIR, b)
            for j in range(2):
                residual(b[j], 2 * g + j, 14, T, t, src=h2, free=a_read)
                sq.add(H[:, 2 * g + j, 14:T], htok[2 * g + j])
        ready_sqrt()
        attn_end = [a_read, x_free, lane_free, htok]

        cursor[0] = arena
        hidh = sb("hidh", [P, HALF, SEQ], F32R)
        hidl = sb("hidl", [P, HALF, SEQ], F32R)
        gct = [sb(f"gc{i}", [P, SEQ]) for i in range(3)]
        HID = Operand(hidh, hidl)

        def ffn(b, conv, x_done, sq, scale=None):
            gc_ring = Ring(gct)
            gc_ring.free = [[x_done] for _ in gct]
            down_done = x_done
            t0 = 14 if conv else 16
            for f in range(2):
                for g in range(HALF // 2):
                    t = gemm((b, "gate", f, g), X, t0, T, PAIR, [0, 1])
                    gs = []
                    for j in range(2):
                        n = HALF * f + 2 * g + j
                        k, gc, free = gc_ring.take()
                        src = ps[j]
                        if conv:
                            a = act.do(lambda e, gc=gc, src=src, n=n: e.activation(gc[:, :], src[:, 2:258], ACT.Identity, bias=V("cb", n), scale=V("cw1", n)), t, free, t_vec)
                            d = dve.do(lambda e, gc=gc, src=src, n=n: e.scalar_tensor_tensor(
                                out=gc[:, :], in0=src[:, 1:257], scalar=V("cw0", n), in1=gc[:, :], op0=ALU.mult, op1=ALU.add), a)
                            d = dve.do(lambda e, gc=gc, src=src, n=n: e.scalar_tensor_tensor(
                                out=gc[:, 0:255], in0=src[:, 3:258], scalar=V("cw2", n), in1=gc[:, 0:255], op0=ALU.mult, op1=ALU.add), d)
                            s = []
                            later(lambda gc=gc, d=d, s=s: s.append(act.do(lambda e: e.activation(gc[:, :], gc[:, :], ACT.Silu), d)))
                            main_free[j] = [d]
                        else:
                            s = act.do(lambda e, gc=gc, src=src: e.activation(gc[:, :], src[:, 0:256], ACT.Silu), t, free)
                            main_free[j] = [s]
                        gs.append((k, gc, s))
                    t = gemm((b, "up", f, g), X, 16, T, PAIR, [2, 3])
                    for j in range(2):
                        k, gc, s = gs[j]
                        assert s
                        m = dve.do(lambda e, gc=gc, j=j: e.tensor_tensor(gc[:, :], ps[2 + j][:, 0:256], gc[:, :], ALU.mult), t, s)
                        main_free[2 + j] = [m]
                        gc_ring.free[k] = split_to(gc[:, :], m, HID, 2 * g + j, 0, SEQ, down_done)
                for g in range(8):
                    bk = two()
                    t = gemm((b, "down", f, g), HID, 0, SEQ, PAIR, bk)
                    for j in range(2):
                        c = 2 * g + j
                        residual(bk[j], c, 16, T, t, *(scale(c) if scale else ()))
                        if f == 1:
                            sq.add(H[:, c, 16:T], htok[c])
                    if f == 1 and g == 0:
                        ready_sqrt()
                down_done = peds[-1]
            return down_done

        norm_to([H[:, c, 14:T] for c in range(KD)], htok, D, 14, T, lambda i: V("ffn_g", i), X, 0, peds[-1], squares=sq)
        sq = Squares("h", 16, T, KD)
        down_done = ffn(1, True, [attn_end, peds[-1]], sq)
        mod_mix = mod_until(8)

        mx = small
        one_sc = mx[:, 48:80]

        def gain_of(k, name, toks):
            dst = one_sc[:, 16 * k:16 * k + 16]
            t = dve.do(lambda e: e.tensor_scalar(dst, mod[:, 16 + 48 * k:32 + 48 * k], 1.0, None, ALU.add), toks)
            return dve.do(lambda e: e.tensor_tensor(dst, dst, V(name, 0, 16), ALU.mult), t)

        sc_mix = gain_of(0, "mix2_g", mod_mix)
        lbm, lbe0, lbe1, lbs, lb, oml = (mx[:, 80 + 8 * i:88 + 8 * i] for i in range(6))
        t = dve.do(lambda e: e.tensor_tensor(lbm, V("lb0", 0, 8), V("lb1", 0, 8), ALU.max), t_vec)
        t = [dve.do(lambda e: e.tensor_tensor(lbe0, V("lb0", 0, 8), lbm, ALU.subtract), t),
             dve.do(lambda e: e.tensor_tensor(lbe1, V("lb1", 0, 8), lbm, ALU.subtract), t)]
        t = [act.do(lambda e: e.activation(lbe0, lbe0, ACT.Exp), t), act.do(lambda e: e.activation(lbe1, lbe1, ACT.Exp), t)]
        t = dve.do(lambda e: e.tensor_tensor(lbs, lbe0, lbe1, ALU.add), t)
        t = dve.do(lambda e: e.reciprocal(lbs, lbs), t)
        t = dve.do(lambda e: e.tensor_tensor(lb, lbe0, lbs, ALU.mult), t)
        lb_tok = [t, dve.do(lambda e: e.tensor_scalar(oml, lb, -1.0, 1.0, ALU.mult, ALU.add), t)]

        cursor[0] = arena
        convh = sb("convh", [P, 8, SEQ], F32R)
        convl = sb("convl", [P, 8, SEQ], F32R)
        oh = sb("oh", [P, 8, SEQ], F32R)
        ol = sb("ol", [P, 8, SEQ], F32R)
        cu = sb("cu", [P, 2, SEQ])
        cy = sb("cy", [P, 2, SEQ])
        mid = cursor[0]
        hsets = [None, {n: sb(f"hg1_{n}", [P, 2, SEQ]) for n in "qfkig"}]
        keep, cursor[0] = cursor[0], arena
        hsets[0] = {n: sb(f"hg0_{n}", [P, 2, SEQ]) for n in "qfkig"}
        cursor[0] = keep
        hR = sb("hR", [P, 2, SEQ])
        masks32, _ = at("masks32", [P, 128 * (len(LEVELS) + 1)], F32, cursor[0])
        hQs = [sb(f"hQ{i}", [P, 2, SEQ]) for i in range(2)]
        hKs = [sb(f"hK{i}", [P, 2, SEQ]) for i in range(2)]
        hB, off = at("hB", [P, 2, P], F32, tmp_off)
        hvt, off = at("hvt", [P, 4, P], F32, off)
        assert off <= tmp_off + 5 * T * 4
        cursor[0] = mid
        merged = sb("merged", [P, KD, SEQ])
        OC, OH = Operand(convh, convl), Operand(oh, ol)

        norm_to([H[:, c, 16:T] for c in range(KD)], htok, D, 16, T, lambda i: one_sc[:, i:i + 1], X, 0, peds[-1],
                shift=lambda i: mod[:, i:i + 1], squares=sq, deps=[sc_mix, mod_mix])
        t_masks = sp.dma(lambda e: e.dma_start(masks32[:, :], A["masks"]), sem("s_masks"), 16, down_done)
        t_masks = dve.do(lambda e: e.tensor_copy(masks[:, :], masks32[:, :]), t_masks)
        h_free = [down_done, t_masks]
        hset_free = [[down_done], [down_done]]

        def hgrn_lane(p, tq, tf, ti, tg):
            bA, bB = PX[1], PX[2]
            hq, hf, hk, hi_, hg = (hsets[p % 2][n] for n in "qfkig")
            hA = hi_[:, :, :].rearrange("p a (b c) -> p (a b) c", b=2)
            for n in range(2):
                for b in range(2):
                    m = pe.do(lambda e, n=n, b=b: e.transpose(bA[:, 128 * (2 * n + b):128 * (2 * n + b) + 128],
                                                              hi_[:, n, 128 * b:128 * b + 128], ident), ti, x_free[1], t_cst)
            tvt = act.do(lambda e: e.activation(hvt[:, :, :], bA[:, :].rearrange("p (a b) -> p a b", a=4), ACT.Copy), m, h_free)
            tk = dve.do(lambda e: e.tensor_scalar(hk[:, :, :], hf[:, :, :], -1.0, 1.0, ALU.mult, ALU.add), tf, h_free)
            tR = dve.do(lambda e: e.memset(hR[:, :, :], 1.0), h_free)
            tP = tf
            yield
            acc = dve.do(lambda e: e.memset(hA, 0.0), m)
            bfree = [[tvt], x_free[2]]
            half = lambda x, m, c: x[:, :, :].rearrange("p a (b c m) -> p (a b) c m", c=2, m=m)[:, :, c, :]
            used = [None, None]
            ready = [tq, tk]
            for lv in range(len(LEVELS) + 1):
                bank = (bA, bB)[lv % 2]
                q, k = (hq, hk) if lv == 0 else (hQs[lv % 2], hKs[lv % 2])
                for n in range(2):
                    for b in range(2):
                        j = 2 * n + b
                        m = pe.do(lambda e: e.matmul(
                            bank[:, 128 * j:128 * j + 128], k[:, n, 128 * b:128 * b + 128], q[:, n, 128 * b:128 * b + 128],
                            start=True, stop=True), ready, bfree[lv % 2])
                used[lv % 2] = m
                if lv < len(LEVELS):
                    sz = LEVELS[lv]
                    q2, k2 = hQs[(lv + 1) % 2], hKs[(lv + 1) % 2]
                    if lv > 0:
                        tP, tR = grow(hf, LEVELS[lv - 1], tP, tR, ready)
                    if lv < 2:
                        parts = [(q2[:, :, :], hq[:, :, :], hf[:, :, :]), (k2[:, :, :], hk[:, :, :], hR[:, :, :])]
                    else:
                        parts = [(half(q2, sz, 1), half(hq, sz, 1), half(hf, sz, 1)),
                                 (half(k2, sz, 0), half(hk, sz, 0), half(hR, sz, 0))]
                    ready = [dve.do(lambda e: e.tensor_tensor(o, x, y, ALU.mult), tq, tk, tP, tR, used[(lv + 1) % 2], h_free)
                             for o, x, y in parts]
                bv = bank[:, :].rearrange("p (a b) -> p a b", a=4)
                mk = lmask(lv).unsqueeze(1).to_broadcast([P, 4, P])
                acc = dve.do(lambda e: e.copy_predicated(hA, mk, bv), m, acc, t_masks)
                bfree[lv % 2] = [acc]
                yield
            tP, tR = grow(hf, 64, tP, tR, ready)
            hQ, hK = hQs[0], hKs[0]
            t2 = dve.do(lambda e: e.tensor_tensor(hQ[:, :, 128:256], hq[:, :, 128:256], hf[:, :, 128:256], ALU.mult), tP, used)
            t3 = dve.do(lambda e: e.tensor_tensor(hK[:, :, 0:128], hk[:, :, 0:128], hR[:, :, 0:128], ALU.mult), tR, used)
            yield
            for n in range(2):
                m = pe.do(lambda e: e.matmul(bA[:, 128 * n:128 * n + 128], hK[:, n, 0:128], hQ[:, n, 128:256],
                                             start=True, stop=True), t2, t3, bfree)
            tB = act.do(lambda e: e.activation(hB[:, :, :], bA[:, 0:256].rearrange("p (a b) -> p a b", a=2), ACT.Copy), m, h_free)
            yield
            for n in range(2):
                o = 256 * n
                pe.run(lambda e: e.matmul(bB[:, o:o + 128], hvt[:, 2 * n, :], hA[:, 2 * n, :], start=True, stop=True), tB, acc, tvt, bfree)
                pe.run(lambda e: e.matmul(bB[:, o + 128:o + 256], hvt[:, 2 * n, :], hB[:, n, :], start=True, stop=False))
                m = pe.do(lambda e: e.matmul(bB[:, o + 128:o + 256], hvt[:, 2 * n + 1, :], hA[:, 2 * n + 1, :], start=False, stop=True))
            flat = lambda x: x[:, :, :].rearrange("p a b -> p (a b)")
            tO = act.do(lambda e: e.activation(flat(hQ), bB[:, :], ACT.Copy), m)
            tS = act.do(lambda e: e.activation(flat(hK), bB[:, :], ACT.Square), m)
            x_free[2] = [tS]
            yield
            m = pe.do(lambda e: e.matmul(bA[:, :], ones, flat(hK), start=True, stop=True), tS, tB)
            a = act.do(lambda e: e.activation(flat(hR), bA[:, :], ACT.Sqrt, bias=eps, scale=1.0 / 128), m, t3)
            x_free[1] = [a]
            d = dve.do(lambda e: e.reciprocal(flat(hR), flat(hR)), a)
            d = dve.do(lambda e: e.scalar_tensor_tensor(out=flat(hQ), in0=flat(hQ), scalar=V("gnorm_g"), in1=flat(hR), op0=ALU.mult, op1=ALU.mult), d, tO)
            d = dve.do(lambda e: e.tensor_tensor(flat(hQ), flat(hQ), flat(hg), ALU.mult), d, tg)
            yield
            ends = []
            for n in range(2):
                ends += split_to(hQ[:, n, :], d, OH, 2 * p + n, 0, SEQ, down_done)
            h_free[:] = ends
            hset_free[p % 2] = ends
            yield

        def grow(hf, m, tP, tR, used):
            Pv = hf[:, :, :].rearrange("p a (b c m) -> p (a b) c m", c=2, m=m)
            Rv = hR[:, :, :].rearrange("p a (b c m) -> p (a b) c m", c=2, m=m)
            nb = 2 * SEQ // (2 * m)
            r = dve.do(lambda e: e.tensor_tensor(Rv[:, :, 0, :], Rv[:, :, 0, :], Pv[:, :, 1, m - 1:m].to_broadcast([P, nb, m]), ALU.mult), tP, tR, used)
            q = dve.do(lambda e: e.tensor_tensor(Pv[:, :, 1, :], Pv[:, :, 1, :], Pv[:, :, 0, m - 1:m].to_broadcast([P, nb, m]), ALU.mult), r, tP, used)
            return q, r

        gen = None
        if ada in lanes:
            lanes.remove(ada)
        for p in range(4):
            toks = {}
            for n in "qfig":
                b = two()
                t = gemm((n, p), X, 16, T, PAIR, b)
                o = []
                for j in range(2):
                    src, dst = ps[b[j]][:, 0:SEQ], hsets[p % 2][n][:, j, :]
                    c = 2 * p + j
                    if n == "i":
                        e1 = act.do(lambda e, d=dst, s=src: e.activation(d, s, ACT.Copy), t, hset_free[p % 2])
                    else:
                        e1 = act.do(lambda e, d=dst, s=src: e.activation(d, s, ACT.Sigmoid), t, hset_free[p % 2])
                        if n == "f":
                            e2 = dve.do(lambda e, d=dst, c=c: e.tensor_scalar(d, d, oml[:, c:c + 1], lb[:, c:c + 1], ALU.mult, ALU.add), e1, lb_tok)
                        else:
                            e2 = dve.do(lambda e, d=dst, s=src: e.tensor_tensor(d, s, d, ALU.mult), e1)
                            e1 = e2
                        o.append(e2)
                    main_free[b[j]] = [e1]
                    if n == "i":
                        o.append(e1)
                toks[n] = o
            if gen is not None:
                drain(gen)
            gen = hgrn_lane(p, toks["q"], toks["f"], toks["i"], toks["g"])
            lanes.append(gen)
        cfree = [down_done, hset_free[0]]
        for p in range(4):
            b = two()
            t = gemm(("ac", p), X, 16, T, PAIR, b)
            ta = []
            for j in range(2):
                e1 = act.do(lambda e, j=j, s=b[j]: e.activation(cu[:, j, :], ps[s][:, 0:SEQ], ACT.Copy), t, cfree)
                main_free[b[j]] = [e1]
                ta.append(e1)
            b = two()
            t = gemm(("ax", p), X, 16, T, PAIR, b)
            ty = []
            for j in range(2):
                c = 2 * p + j
                u, y = cu[:, j, :], cy[:, j, :]
                d = dve.do(lambda e, u=u, s=b[j]: e.tensor_tensor(u, ps[s][:, 0:SEQ], u, ALU.mult), t, ta[j])
                main_free[b[j]] = [d]
                a = act.do(lambda e, u=u, y=y, c=c: e.activation(y, u, ACT.Copy, scale=V("vw2", c)), d, cfree)
                d = dve.do(lambda e, u=u, y=y, c=c: e.scalar_tensor_tensor(
                    out=y[:, 1:SEQ], in0=u[:, 0:SEQ - 1], scalar=V("vw1", c), in1=y[:, 1:SEQ], op0=ALU.mult, op1=ALU.add), a, d)
                d = dve.do(lambda e, u=u, y=y, c=c: e.scalar_tensor_tensor(
                    out=y[:, 2:SEQ], in0=u[:, 0:SEQ - 2], scalar=V("vw0", c), in1=y[:, 2:SEQ], op0=ALU.mult, op1=ALU.add), d)
                ty.append(d)
            b = two()
            t = gemm(("ab", p), X, 16, T, PAIR, b)
            cf = []
            for j in range(2):
                y = cy[:, j, :]
                d = dve.do(lambda e, y=y, s=b[j]: e.tensor_tensor(y, ps[s][:, 0:SEQ], y, ALU.mult), t, ty[j])
                main_free[b[j]] = [d]
                cf += split_to(y, d, OC, 2 * p + j, 0, SEQ, [down_done, hset_free[0]])
            cfree = cf
        drain(gen)
        lanes.append(ada)
        mtok = [None] * KD
        for g in range(8):
            sg = []
            for n, buf in (("ga", cu), ("gb", cy)):
                b = two()
                t = gemm((n, g), X, 16, T, PAIR, b)
                o = []
                for j in range(2):
                    e1 = act.do(lambda e, j=j, s=b[j], buf=buf: e.activation(buf[:, j, :], ps[s][:, 0:SEQ], ACT.Sigmoid), t, cfree)
                    main_free[b[j]] = [e1]
                    o.append(e1)
                sg.append(o)
            x_done = peds[-1]
            cf = []
            b = two()
            t = gemm(("ya", g), OC, 0, SEQ, PAIR, b)
            for j in range(2):
                c = 2 * g + j
                d = dve.do(lambda e, j=j, c=c, s=b[j]: e.tensor_tensor(merged[:, c, :], ps[s][:, 0:SEQ], cu[:, j, :], ALU.mult), t, sg[0][j], h_free)
                main_free[b[j]] = [d]
                mtok[c] = d
            b = two()
            t = gemm(("yb", g), OH, 0, SEQ, PAIR, b)
            for j in range(2):
                c = 2 * g + j
                d = dve.do(lambda e, j=j, s=b[j]: e.tensor_tensor(cy[:, j, :], ps[s][:, 0:SEQ], cy[:, j, :], ALU.mult), t, sg[1][j])
                main_free[b[j]] = [d]
                d = dve.do(lambda e, j=j, c=c: e.tensor_tensor(merged[:, c, :], merged[:, c, :], cy[:, j, :], ALU.add), d, mtok[c])
                mtok[c] = d
                cf.append(d)
            cfree = cf
        for c in range(KD):
            split_to(merged[:, c, :], mtok[c], X, c, 16, T, x_done)
        m_read = X.tok[KD - 1]
        sq = Squares("h", 16, T, KD)
        mod_gt = mod_until(12)
        for g in range(8):
            b = two()
            t = gemm(("wo", g), X, 16, T, PAIR, b)
            for j in range(2):
                c = 2 * g + j
                residual(b[j], c, 16, T, t, mod[:, 32 + c:33 + c], mod_gt)
                sq.add(H[:, c, 16:T], htok[c])
            if g == 0:
                ready_sqrt()
        mod_ffn = mod_until(20)
        sc_ffn = gain_of(1, "ffn2_g", mod_ffn)
        norm_to([H[:, c, 16:T] for c in range(KD)], htok, D, 16, T, lambda i: one_sc[:, 16 + i:17 + i], X, 0, peds[-1],
                shift=lambda i: mod[:, 48 + i:49 + i], squares=sq, deps=[sc_ffn, mod_ffn])
        sq = Squares("h", 16, T, KD)
        mod_end = mod_until(24)
        ffn(2, False, [peds[-1], m_read], sq, scale=lambda c: (mod[:, 80 + c:81 + c], mod_end))

        r, tr = sq.rstd(D)
        s_out = sem("s_out")
        oT = out.rearrange("(c p) t -> p c t", p=P)
        tot = 0
        for c in range(KD):
            d = dve.do(lambda e, c=c: e.scalar_tensor_tensor(out=H[:, c, 16:T], in0=H[:, c, 16:T], scalar=V("fin_g", c), in1=r,
                                                             op0=ALU.mult, op1=ALU.mult), tr, htok[c])
            if c % 4 == 3:
                tot += 16
                sp.dma(lambda e, c=c: e.dma_start(oT[:, c - 3:c + 1, :], H[:, c - 3:c + 1, 16:T]), s_out, tot, d)
        sp.need([(s_out, tot)])
        assert at_slab[0] == len(plan)


_WEIGHTS = ["w_in", "w_q_up", "w_kv_up", "w_out", "w_gate", "w_up", "w_down", "w_ada_2", "w_in_2", "w_conv_out_2",
            "w_hgrn_out_2", "w_o_2", "w_ffn_gate_2", "w_ffn_up_2", "w_ffn_down_2", "na_rpb", "na_meta_bias"]


def lay_out(inputs):
    a = {n: np.ascontiguousarray(inputs[n][0]) for n in _WEIGHTS}
    a["hT"] = np.ascontiguousarray(np.concatenate([inputs["meta_tokens"], inputs["x"][0]], 0).T)
    pad = np.zeros(64, np.float32)
    rows = {"mix_g": inputs["mix_norm_g"][0], "na_q_g": inputs["na_q_g"][0], "na_k_g": inputs["na_k_g"][0],
            "cq_g": inputs["mla_cq_g"][0], "ckv_g": inputs["mla_ckv_g"][0],
            "mq_g": np.concatenate([inputs["mla_q_g"][0], pad]), "mk_g": np.concatenate([inputs["mla_k_g"][0], pad]),
            "na_out_g": inputs["na_out_g"][0], "mla_out_g": inputs["mla_out_g"][0], "ffn_g": inputs["ffn_norm_g"][0],
            "cw0": inputs["conv_w"][0, 0], "cw1": inputs["conv_w"][0, 1], "cw2": inputs["conv_w"][0, 2],
            "cb": inputs["conv_b"][0], "b_ada": inputs["b_ada_2"][0], "mix2_g": inputs["norm_mix_g_2"][0],
            "vw0": inputs["conv_w_2"][0, 0], "vw1": inputs["conv_w_2"][0, 1], "vw2": inputs["conv_w_2"][0, 2],
            "lb0": inputs["lb_param_2"][0], "lb1": inputs["lb_param_2"][1], "gnorm_g": inputs["gnorm_g_2"][0],
            "ffn2_g": inputs["norm_ffn_g_2"][0], "fin_g": inputs["norm_final_g_2"], "c": inputs["c_2"][0]}
    flat = np.concatenate([np.asarray(rows[n]) for n, _ in VEC_ROWS])
    a["vecs"] = np.ascontiguousarray(flat.reshape(NVEC, P).T)
    a["consts"] = constants()
    a["masks"] = level_masks()
    return a


def program(nc, arrays):
    aps = {n: nc.dram_tensor(f"in_{n}", list(a.shape), mybir.dt.from_np(a.dtype), kind="ExternalInput").ap()
           for n, a in arrays.items()}
    out = nc.dram_tensor("out_0", [D, SEQ], F32, kind="ExternalOutput").ap()
    build(nc, aps, out)


def kernel(**inputs):
    import concourse.bacc as _bacc
    from concourse.bass_utils import run_bass_kernel_spmd as _run

    inputs = {k: np.asarray(v) for k, v in inputs.items()}
    arrays = lay_out(inputs)
    nc = _bacc.Bacc("TRN2", target_bir_lowering=False, num_devices=1)
    program(nc, arrays)
    r = _run(nc, [{f"in_{n}": a for n, a in arrays.items()}], core_ids=[0])
    got = r.results[0]["out_0"]
    return np.ascontiguousarray(got.T).reshape(1, SEQ, D)
```

```python
from contextlib import ExitStack

import numpy as np

import concourse.bass as bass
from concourse import mybir

F32 = mybir.dt.float32
F32R = mybir.dt.float32r
ALU = mybir.AluOpType
ACT = mybir.ActivationFunctionType
AX = mybir.AxisListType

P = 128
D = 2048
KD = D // P
META = 16
SEQ = 256
T = META + SEQ
HEADS = 8
FF = 5632
KF = FF // P
HALF = KF // 2
EPS = 1e-6
NEG = -1e30
WIN = 16
GRID = 64
SLAB = 2048
ORDER = "q0 m0 k0 v0 q1 m1 k1 v1 m2 q2 k2 v2 m3 q3 k3 v3".split()
PAUSES = [1, 3, 2, 1, 2, 3, 2]
FINE = 4
LEVELS = [1, 2, 4, 8, 16, 32, 64]

VEC_ROWS = [("mix_g", 16), ("na_q_g", 1), ("na_k_g", 1), ("cq_g", 4), ("ckv_g", 2), ("mq_g", 2), ("mk_g", 2),
            ("na_out_g", 8), ("mla_out_g", 8), ("ffn_g", 16), ("cw0", 44), ("cw1", 44), ("cw2", 44), ("cb", 44),
            ("b_ada", 96), ("mix2_g", 16), ("vw0", 8), ("vw1", 8), ("vw2", 8), ("lb0", 8), ("lb1", 8),
            ("gnorm_g", 1), ("ffn2_g", 16), ("fin_g", 16), ("c", 16)]
VEC = {}
NVEC = 0
for _name, _n in VEC_ROWS:
    VEC[_name] = NVEC
    NVEC += _n

CONST_COLS = [("ident", 128), ("ones", 128), ("rot", 64), ("cos", T), ("sin", T), ("namask", 256),
              ("eps", 1)]
CST = {}
NCONST = 0
for _name, _n in CONST_COLS:
    CST[_name] = NCONST
    NCONST += _n


def constants():
    out = np.zeros((P, NCONST), np.float32)

    def put(name, a):
        out[:a.shape[0], CST[name]:CST[name] + a.shape[1]] = a

    put("ident", np.eye(P, dtype=np.float32))
    put("ones", np.ones((P, P), np.float32))
    rot = np.zeros((64, 64), np.float32)
    for i in range(32):
        rot[32 + i, i] = -1.0
        rot[i, 32 + i] = 1.0
    put("rot", rot)
    inv = np.float32(10000.0) ** (-np.arange(0, 64, 2, dtype=np.float32) / np.float32(64))
    ang = np.arange(T, dtype=np.float32)[None, :] * inv[:, None]
    put("cos", np.concatenate([np.cos(ang), np.cos(ang)], 0).astype(np.float32))
    put("sin", np.concatenate([np.sin(ang), np.sin(ang)], 0).astype(np.float32))
    qc = np.arange(P) % GRID
    start = np.clip(qc - WIN // 2, 0, GRID - WIN)
    kc = np.arange(SEQ) % GRID
    ok = (kc[None, :] >= start[:, None]) & (kc[None, :] < start[:, None] + WIN)
    put("namask", np.where(ok, 0.0, NEG).astype(np.float32))
    put("eps", np.full((P, 1), EPS, np.float32))
    return out


def level_masks():
    s = np.arange(P)[:, None]
    t = np.arange(P)[None, :]
    masks = [(s == t)]
    for m in LEVELS:
        masks.append((s // (2 * m) == t // (2 * m)) & ((s // m) % 2 == 0) & ((t // m) % 2 == 1))
    return np.concatenate(masks, 1).astype(np.float32)


class Engine:

    def __init__(self, eng, sem):
        self.eng, self.sem, self.n, self.seen = eng, sem, 0, {}

    def need(self, toks):
        for t in toks:
            if t is None:
                continue
            if isinstance(t, list):
                self.need(t)
                continue
            sem, value = t
            if self.seen.get(id(sem), 0) < value:
                self.seen[id(sem)] = value
                self.eng.wait_ge(sem, value)

    def run(self, fn, *toks):
        self.need(toks)
        fn(self.eng)

    def do(self, fn, *toks):
        self.need(toks)
        self.n += 1
        fn(self.eng).then_inc(self.sem, 1)
        return (self.sem, self.n)

    def do_last(self, last, fn, *toks):
        return self.do(fn, *toks) if last else self.run(fn, *toks)

    def dma(self, fn, sem, value, *toks):
        self.need(toks)
        fn(self.eng).then_inc(sem, 16)
        return (sem, value)


class Ring:
    def __init__(self, aps):
        self.aps, self.free, self.i = aps, [[] for _ in aps], 0

    def take(self):
        k = self.i % len(self.aps)
        self.i += 1
        return k, self.aps[k], self.free[k]


class Operand:

    def __init__(self, h, l):
        self.h, self.l = h, l
        self.tok = [[] for _ in range(h.shape[1])]


def build(nc, A, out):
    ctx = ExitStack()
    with ctx:
        base = (nc.sbuf_base + 31) // 32 * 32
        limit = nc.sbuf_usable_end
        cursor = [base]

        def at(name, shape, dt, offset):
            size = 4 * int(np.prod(shape[1:]))
            assert offset + size <= limit, (name, offset, size, limit)
            return nc.alloc_sbuf_tensor_at(name, shape, dt, offset=offset), offset + size

        def sb(name, shape, dt=F32):
            t, cursor[0] = at(name, shape, dt, cursor[0])
            cursor[0] = (cursor[0] + 31) // 32 * 32
            return t

        sems = {}

        def sem(name):
            sems[name] = ctx.enter_context(nc.semaphore(name))
            return sems[name]

        pe, act, dve, pool, sp = (Engine(eng, sem(f"s_{n}")) for n, eng in (
            ("pe", nc.tensor), ("act", nc.scalar), ("dve", nc.vector), ("pool", nc.gpsimd), ("sp", nc.sync)))

        NR, NS = 3, 3
        raw = [sb(f"raw{i}", [P, SLAB]) for i in range(NR)]
        wh = [sb(f"wh{i}", [P, SLAB], F32R) for i in range(NS)]
        wl = [sb(f"wl{i}", [P, SLAB], F32R) for i in range(NS)]
        xh = sb("xh", [P, KD, T], F32R)
        xl = sb("xl", [P, KD, T], F32R)
        hoff = cursor[0]
        H = sb("H", [P, KD, T])
        cst = sb("cst", [P, NCONST])
        vec = sb("vec", [P, NVEC])
        masks, cursor[0] = nc.alloc_sbuf_tensor_at("masks", [P, 128 * (len(LEVELS) + 1)], mybir.dt.uint8, offset=cursor[0]), cursor[0] + 128 * (len(LEVELS) + 1)
        small = sb("small", [P, 256])
        tmp_off = cursor[0]
        TMP = [sb(f"tmp{i}", [P, T]) for i in range(5)]
        NA_SLOTS, AHEAD = 4, 3
        ada_off = cursor[0]
        ada_raw = [sb(f"ada_raw{i}", [P, 512]) for i in range(NA_SLOTS)]
        ada_acc = sb("ada_acc", [P, 512])
        mod = sb("mod", [P, 96])
        arena = cursor[0]

        ps = [ctx.enter_context(nc.psum_tensor(f"ps{i}", [P, 512], F32)) for i in range(8)]
        main_free = [[] for _ in range(4)]
        x_free = [[] for _ in range(4)]
        PX = ps[4:8]

        def V(name, j=0, n=1):
            return vec[:, VEC[name] + j:VEC[name] + j + n]

        def C(name, n, rows=P):
            return cst[0:rows, CST[name]:CST[name] + n]

        ident, ones = C("ident", P), C("ones", P)
        eps = C("eps", 1)

        def lmask(i):
            return masks[:, 128 * i:128 * (i + 1)]

        s_cst = sem("s_cst")
        s_vec = sem("s_vec")
        s_h = [sem(f"s_h{i}") for i in range(4)]
        hT = A["hT"].rearrange("(c p) t -> p c t", p=P)
        t_h = []
        for i in range(4):
            t_h.append(sp.dma(lambda e, i=i: e.dma_start(H[:, 4 * i:4 * i + 4, :], hT[:, 4 * i:4 * i + 4, :]), s_h[i], 16))
        t_vec = act.dma(lambda e: e.dma_start(vec[:, :], A["vecs"]), s_vec, 16)
        t_cst = act.dma(lambda e: e.dma_start(cst[:, :], A["consts"]), s_cst, 16)

        plan, loads, splits, peds = [], [], [], []
        s_raw = [sem(f"s_raw{i}") for i in range(NR)]

        def add(key, w, k0, nk, c0, ncols):
            step = min(SLAB // ncols, nk)
            view = w.rearrange("(c p) n -> p c n", p=P)
            for k in range(0, nk, step):
                n = min(step, nk - k)
                plan.append((key, view[:, k0 + k:k0 + k + n, c0:c0 + ncols], k, n, ncols, k + n == nk))

        def load(i):
            slot = i % NR
            _, view, _, n, ncols, _ = plan[i]
            dst = raw[slot][:, 0:n * ncols].rearrange("p (c n) -> p c n", c=n)
            loads.append(sp.dma(lambda e: e.dma_start(dst, view), s_raw[slot], 16 * (i // NR + 1),
                                splits[i - NR] if i >= NR else t_h[1]))

        def split(i, whole=True):
            split_rest()
            while len(loads) <= i:
                load(len(loads))
            splits.append([split_half(i, 0)])
            if whole:
                split_rest()

        def split_half(i, h):
            nk, ncols = plan[i][3:5]
            done = peds[i - NS] if i >= NS else None
            k0, k1 = ((0, nk // 2), (nk // 2, nk))[h]
            part = slice(k0 * ncols, k1 * ncols)
            src, hi, lo = raw[i % NR][:, part], wh[i % NS][:, part], wl[i % NS][:, part]
            a = act.do(lambda e: e.activation(hi, src, ACT.Copy), loads[i], done)
            d = dve.do(lambda e: e.tensor_tensor(lo, src, hi.bitcast(F32), ALU.subtract), loads[i], a, done)
            return [a, d]

        def split_rest():
            if splits and len(splits[-1]) == 1:
                splits[-1].append(split_half(len(splits) - 1, 1))

        lanes = []

        def later(fn):
            def lane():
                yield
                fn()
            lanes.insert(0, lane())

        quick = []
        MORE = "more"

        def step(queue):
            active = list(queue)
            while active:
                for g in list(active):
                    got = next(g, "end")
                    if got == "end":
                        queue.remove(g)
                    if got != MORE:
                        active.remove(g)

        def pump(all_of_them=True):
            if all_of_them:
                step(lanes)
            step(quick)

        def drain(*gens):
            while any(g in lanes or g in quick for g in gens):
                pump()

        def emit(gen):
            for _ in gen:
                pass

        def pause(n):
            for _ in range(n):
                yield

        at_slab = [0]

        def split_ahead():
            split_rest()
            while len(splits) < min(len(plan), at_slab[0] + NS):
                split(len(splits), len(splits) < at_slab[0] + NS - 1)

        def gemm(key, X, t0, t1, tiles, banks, hold=False):
            n = t1 - t0
            for b in banks:
                pe.need(main_free[b])
            while True:
                i = at_slab[0]
                assert plan[i][0] == key, (plan[i][0], key)
                _, _, k0, nk, ncols, last = plan[i]
                if len(splits) <= i or not (hold and last):
                    split_ahead()
                if len(splits) <= i + 1:
                    split_rest()
                w_h = wh[i % NS][:, 0:nk * ncols].rearrange("p (c n) -> p c n", c=nk)
                w_l = wl[i % NS][:, 0:nk * ncols].rearrange("p (c n) -> p c n", c=nk)
                for c in range(nk):
                    k = k0 + c
                    pe.need([splits[i][0 if c < nk // 2 else 1], X.tok[k]])
                    x_h, x_l = X.h[:, k, t0:t1], X.l[:, k, t0:t1]
                    end = last and c == nk - 1
                    for j, (o, w) in enumerate(tiles):
                        dst = ps[banks[j]][0:w, 0:n]
                        a, b = w_h[:, c, o:o + w], w_l[:, c, o:o + w]
                        pe.run(lambda e, d=dst, a=a, x=x_h, s=(k == 0): e.matmul(d, a, x, start=s, stop=False))
                        pe.run(lambda e, d=dst, a=a, x=x_l: e.matmul(d, a, x, start=False, stop=False))
                        f = lambda e, d=dst, a=b, x=x_h, s=end: e.matmul(d, a, x, start=False, stop=s)
                        if c == nk - 1 and j == len(tiles) - 1:
                            peds.append(pe.do(f))
                        else:
                            pe.run(f)
                    if c != nk - 1 and (c + 1) * FINE % nk == 0 and not (hold and last):
                        pump(c == nk // 2 - 1)
                    if c == nk // 2 - 1:
                        split_rest()
                at_slab[0] += 1
                if not (hold and last):
                    pump()
                if last:
                    return peds[-1]

        PAIR = [(0, 128), (128, 128)]
        parity = [0]

        def two():
            parity[0] ^= 1
            return [0, 1] if parity[0] else [2, 3]

        tmp = Ring(TMP)
        rstd_buf = sb("rstd", [P, T])
        ssq = {n: sb(f"ssq_{n}", [P, T]) for n in "hab"}
        arena = cursor[0]
        rstd_free = [[]]

        class Squares:

            def __init__(self, name, t0, t1, count):
                self.acc, self.m, self.count, self.i, self.tok = ssq[name][:, 0:t1 - t0], t1 - t0, count, 0, None
                self.last = []

            def add(self, c, tok, free=None):
                self.i += 1
                if self.i == 1:
                    self.tok = act.do(lambda e: e.activation(self.acc, c, ACT.Square), tok, free)
                    return
                k, buf, fr = tmp.take()
                x = buf[:, 0:self.m]
                a = act.do(lambda e: e.activation(x, c, ACT.Square), tok, fr)
                if self.i < self.count - 1:
                    self.tok = pool.do(lambda e: e.tensor_tensor(self.acc, self.acc, x, ALU.add), a, self.tok)
                    tmp.free[k] = [self.tok]
                else:
                    self.last.append((k, x, a))

            def rstd(self, n, ahead):
                assert self.i == self.count
                bank, r, m = PX[2], rstd_buf[:, 0:self.m], self.m
                pe.run(lambda e: e.matmul(bank[:, 0:m], ones, self.acc, start=True, stop=False), self.tok, x_free[2], t_cst)
                for i, (k, x, a) in enumerate(self.last):
                    last = pe.do(lambda e: e.matmul(bank[:, 0:m], ones, x, start=False, stop=(i == 1)), a)
                    tmp.free[k] = [last]
                if ahead and len(splits) < min(len(plan), at_slab[0] + NS):
                    split(len(splits))
                a = act.do(lambda e: e.activation(r, bank[:, 0:m], ACT.Sqrt, bias=eps, scale=1.0 / n), last, rstd_free[0])
                x_free[2] = [a]
                return r, dve.do(lambda e: e.reciprocal(r, r), a)

        def rstd_of(chunks, toks, n, t0, t1, ring=None):
            m = t1 - t0
            bank = PX[2]
            pe.need([x_free[2], t_cst])
            last = None
            ring = ring or tmp

            def add(i, k, x, k1, x1, a, d):
                d = dve.do(lambda e: e.tensor_tensor(x, x, x1, ALU.add), a, d)
                m = pe.do(lambda e: e.matmul(bank[:, 0:m_], ones, x, start=(i == 0), stop=(i + 2 == len(chunks))), d)
                ring.free[k], ring.free[k1] = [m], [d]
                return m

            m_, late = m, None
            for i in range(0, len(chunks), 2):
                (k, x, free), (k1, x1, free1) = ring.take(), ring.take()
                x, x1 = x[:, 0:m], x1[:, 0:m]
                a = act.do(lambda e: e.activation(x, chunks[i], ACT.Square), toks[i], free)
                d = dve.do(lambda e: e.tensor_tensor(x1, chunks[i + 1], chunks[i + 1], ALU.mult), toks[i + 1], free1)
                if late:
                    add(*late)
                late = (i, k, x, k1, x1, a, d)
            last = add(*late)
            if ring is not tmp:
                split(len(splits), False)
            r = rstd_buf[:, 0:m]
            a = act.do(lambda e: e.activation(r, bank[:, 0:m], ACT.Sqrt, bias=eps, scale=1.0 / n), last, rstd_free[0])
            x_free[2] = [a]
            return r, dve.do(lambda e: e.reciprocal(r, r), a)

        def norm_steps(chunks, toks, n, t0, t1, gain, dst, d0, dst_free, shift=None, squares=None, deps=None, split_at=None,
                       first=0, ring=None):
            m = t1 - t0
            yield from pause(first)
            r, tr = squares.rstd(n, len(chunks) > 8) if squares else rstd_of(chunks, toks, n, t0, t1, ring)
            yield
            ends = []

            def low(i, k, x, h, l, a, b):
                if shift is None:
                    eng = pool if i % 2 else dve
                    s = eng.do(lambda e: e.tensor_tensor(l, x, h.bitcast(F32), ALU.subtract), a, b, dst_free)
                elif i % 2:
                    y = act.do(lambda e: e.activation(x, x, ACT.Identity, bias=shift(i)), a)
                    s = pool.do(lambda e: e.tensor_tensor(l, x, h.bitcast(F32), ALU.subtract), y, dst_free)
                else:
                    s = dve.do(lambda e: e.scalar_tensor_tensor(
                        out=l, in0=x, scalar=shift(i), in1=h.bitcast(F32), op0=ALU.add, op1=ALU.subtract), a, b, dst_free, deps)
                tmp.free[k] = [a, s]
                dst.tok[d0 + i] = [a, s]
                ends.append([a, s])

            late = []
            for i, c in enumerate(chunks):
                if split_at and i == 3:
                    split_rest()
                if split_at and i in split_at:
                    split(len(splits))
                k, buf, free = tmp.take()
                x = buf[:, 0:m]
                h, l = dst.h[:, d0 + i, t0:t1], dst.l[:, d0 + i, t0:t1]
                b = dve.do(lambda e: e.scalar_tensor_tensor(
                    out=x, in0=c, scalar=gain(i), in1=r, op0=ALU.mult, op1=ALU.mult), tr, toks[i], free, t_vec, deps)
                if shift is None:
                    a = act.do(lambda e: e.activation(h, x, ACT.Copy), b, dst_free)
                else:
                    a = act.do(lambda e: e.activation(h, x, ACT.Identity, bias=shift(i)), b, dst_free, deps)
                late.append((i, k, x, h, l, a, b))
                if len(late) > 2:
                    low(*late.pop(0))
                if i == 11 and not split_at and len(chunks) > 8 and len(splits) < min(len(plan), at_slab[0] + NS):
                    split(len(splits))
                if i % 4 == 3:
                    yield
            for one in late:
                low(*one)
            rstd_free[0] = ends

        def norm_to(*args, **kw):
            emit(norm_steps(*args, **kw))
            return rstd_free[0]

        def ready_sqrt():
            sqrt_tok[:] = [act.do(lambda e: e.activation(small[:, 250:251], small[:, 251:252], ACT.Sqrt), t_one, sqrt_tok)]

        sqrt_tok = []
        t_one = pool.do(lambda e: e.memset(small[:, 251:252], 1.0))

        def split_to(x, tok, dst, c, t0, t1, free):
            h, l = dst.h[:, c, t0:t1], dst.l[:, c, t0:t1]
            a = act.do(lambda e: e.activation(h, x, ACT.Copy), tok, free)
            s = dve.do(lambda e: e.tensor_tensor(l, x, h.bitcast(F32), ALU.subtract), a, tok, free)
            dst.tok[c] = [a, s]
            return [a, s]

        X = Operand(xh, xl)
        w_in, w_qup, w_kvup, w_out_, w_gate, w_up, w_down = (
            A[n] for n in ("w_in", "w_q_up", "w_kv_up", "w_out", "w_gate", "w_up", "w_down"))
        for g in range(2):
            add(("cq", g), w_in, 0, 16, 3072 + 256 * g, 256)
        add(("ckv", 0), w_in, 0, 16, 3584, 256)
        add(("kpe", 0), w_in, 0, 16, 3840, 64)
        for o in ORDER:
            if o[0] == "m":
                p = int(o[1])
                add(("qup", p), w_qup, 0, 4, 384 * p, 384)
                add(("kvup", p), w_kvup, 0, 2, 512 * p, 512)
            else:
                p, n = int(o[1]), "qkv".index(o[0])
                add(("na", p, n), w_in, 0, 16, 1024 * n + 256 * p, 256)
        for n, k0 in (("outb", 8), ("outa", 0)):
            for g in range(8):
                add((n, g), w_out_, k0, 8, 256 * g, 256)

        def plan_ffn(b, wg, wu, wd):
            for f in range(2):
                for g in range(HALF // 2):
                    add((b, "gate", f, g), wg, 0, 16, 128 * (HALF * f + 2 * g), 256)
                    add((b, "up", f, g), wu, 0, 16, 128 * (HALF * f + 2 * g), 256)
                for g in range(8):
                    add((b, "down", f, g), wd, HALF * f, HALF, 256 * g, 256)

        plan_ffn(1, w_gate, w_up, w_down)
        w_in2 = A["w_in_2"]
        for p in range(4):
            for n, c0 in (("q", 3072), ("f", 4096), ("i", 5120), ("g", 6144)):
                add((n, p), w_in2, 0, 16, c0 + 256 * p, 256)
        for p in range(4):
            for n, c0 in (("ac", 1024), ("ax", 2048), ("ab", 0)):
                add((n, p), w_in2, 0, 16, c0 + 256 * p, 256)
        for gs, ys in [((g,), (g,)) for g in range(6)] + [((6, 7), (6, 7))]:
            for g in gs:
                add(("ga", g), w_in2, 0, 16, 7168 + 256 * g, 256)
                add(("gb", g), w_in2, 0, 16, 9216 + 256 * g, 256)
            for g in ys:
                add(("ya", g), A["w_conv_out_2"], 0, 8, 256 * g, 256)
                add(("yb", g), A["w_hgrn_out_2"], 0, 8, 256 * g, 256)
        for g in range(8):
            add(("wo", g), A["w_o_2"], 0, 16, 256 * g, 256)
        plan_ffn(2, A["w_ffn_gate_2"], A["w_ffn_up_2"], A["w_ffn_down_2"])

        s_ada = [sem(f"s_ada{i}") for i in range(NA_SLOTS)]
        cact = small[:, 0:16]
        mod_tok = [None] * 24

        def ada_lane():
            w = A["w_ada_2"].rearrange("(c p) n -> p c n", p=P)
            free = [[na_set_free[0], outb_tok]] * NA_SLOTS
            got = []

            def fetch(i):
                g, k = divmod(i, 16)
                src = w[:, k, 512 * g:512 * g + 512]
                got.append(pool.dma(lambda e: e.dma_start(ada_raw[i % NA_SLOTS][:, :], src), s_ada[i % NA_SLOTS],
                                  16 * (i // NA_SLOTS + 1), free[i % NA_SLOTS]))

            sig_c = act.do(lambda e: e.activation(cact, V("c", 0, 16), ACT.Silu), t_vec)
            for i in range(AHEAD):
                fetch(i)
            yield
            acc_free = [na_set_free[0], outb_tok]
            for i in range(24 * 16):
                g, k = divmod(i, 16)
                if i + AHEAD < 24 * 16:
                    fetch(i + AHEAD)
                s, r = cact[:, k:k + 1], ada_raw[i % NA_SLOTS][:, :]
                if k == 0:
                    prev = dve.do(lambda e: e.tensor_scalar(ada_acc[:, :], r, s, None, ALU.mult), got[i], sig_c, acc_free)
                else:
                    prev = dve.do(lambda e: e.scalar_tensor_tensor(
                        out=ada_acc[:, :], in0=r, scalar=s, in1=ada_acc[:, :], op0=ALU.mult, op1=ALU.add), got[i], prev)
                free[i % NA_SLOTS] = prev
                yield
                if k == 15:
                    pe.need([x_free[3]])
                    for j in range(4):
                        last = pe.do_last(j == 3, lambda e, j=j: e.matmul(PX[3][:, j:j + 1], ada_acc[:, 128 * j:128 * j + 128],
                                                             ones[:, 0:1], start=True, stop=True), prev, t_cst)
                    acc_free = last
                    m = dve.do(lambda e: e.tensor_tensor(mod[:, 4 * g:4 * g + 4], PX[3][:, 0:4],
                                                         V("b_ada", 4 * g, 4), ALU.add), last, t_vec)
                    x_free[3] = [m]
                    mod_tok[g] = m

        def mod_until(g):
            while mod_tok[g - 1] is None:
                pump()
            return mod_tok[0:g]

        Hc = [H[:, c, :] for c in range(KD)]
        ready_sqrt()
        emit(norm_steps(Hc, [t_h[c // 4] for c in range(KD)], D, 0, T, lambda i: V("mix_g", i), X, 0, None, split_at=(6, 11),
                        ring=Ring([at(f"first{i}", [P, T], F32, arena + 4 * T * i)[0] for i in range(10)])))

        cursor[0] = arena
        attn_off = arena
        cqh = sb("cqh", [P, 4, T], F32R)
        cql = sb("cql", [P, 4, T], F32R)
        ckvh = sb("ckvh", [P, 2, T], F32R)
        ckvl = sb("ckvl", [P, 2, T], F32R)
        kpe = sb("kpe", [64, T])
        kpe2 = sb("kpe2", [64, T])
        shared = cursor[0]
        cq = sb("cq", [P, 4, T])
        ckv = sb("ckv", [P, 2, T])
        cursor[0] = shared
        mla_q = [sb(f"mla_q{i}", [P, T]) for i in range(2)]
        mla_qr = [sb(f"mla_qr{i}", [64, T]) for i in range(2)]
        mla_k = [sb(f"mla_k{i}", [P, T]) for i in range(2)]
        mla_kr = [sb(f"mla_kr{i}", [64, T]) for i in range(2)]
        mla_v = [sb(f"mla_v{i}", [P, T]) for i in range(2)]
        mla_end = cursor[0]
        na_sets = [None, [[sb(f"na1{n}{j}", [P, T]) for n in "qkv"] for j in range(2)]]
        keep, cursor[0] = cursor[0], ada_off
        na_sets[0] = [[sb(f"na0{n}{j}", [P, T]) for n in "qkv"] for j in range(2)]
        assert cursor[0] <= ada_off + 4 * 512 * (NA_SLOTS + 1)
        cursor[0] = keep
        na_bias = [sb(f"na_bias{j}", [P, 2, T]) for j in range(2)]
        lane_vt = [sb(f"vt{j}", [P, 3, P]) for j in range(4)]
        lane_p = [sb(f"lp{j}", [P, T]) for j in range(4)]
        lane_pt = [sb(f"lpt{j}", [P, 3, P]) for j in range(4)]
        lane_r = [sb(f"lr{j}", [P, T]) for j in range(4)]
        lane_c = [sb(f"lc{j}", [P, 8]) for j in range(4)]
        dg_off = ada_off + 6 * T * 4
        lane_d = [ssq["h"][:, 0:P], ssq["h"][:, P:2 * P]] + [at(f"ld{j}", [P, P], F32, dg_off + 512 * j)[0] for j in range(2)]
        out_a, _ = at("out_a", [P, 8, T], F32, hoff)
        out_b, _ = at("out_b", [P, 8, T], F32, hoff + 8 * T * 4)
        Xq, Xkv = Operand(cqh, cql), Operand(ckvh, ckvl)

        def evac(bank, w, n, dst, *toks):
            t = act.do(lambda e: e.activation(dst, ps[bank][0:w, 0:n], ACT.Copy), *toks)
            main_free[bank] = [t]
            return t

        cq_tok = []
        for g in range(2):
            b = two()
            t = gemm(("cq", g), X, 0, T, PAIR, b)
            cq_tok += [evac(b[j], P, T, cq[:, 2 * g + j, :], t) for j in range(2)]
        b = two()
        t = gemm(("ckv", 0), X, 0, T, PAIR, b)
        ckv_tok = [evac(b[j], P, T, ckv[:, j, :], t) for j in range(2)]
        b = two()
        t = gemm(("kpe", 0), X, 0, T, [(0, 64)], b)
        kp = evac(b[0], 64, T, kpe[:, :], t)
        cq_read = []

        def latent():
            yield from norm_steps([cq[:, c, :] for c in range(4)], cq_tok, 512, 0, T, lambda i: V("cq_g", i), Xq, 0, None, first=1)
            cq_read.extend(rstd_free[0])
            yield from norm_steps([ckv[:, c, :] for c in range(2)], ckv_tok, 256, 0, T, lambda i: V("ckv_g", i), Xkv, 0, None)
            cq_read.extend(rstd_free[0])

        kp2 = act.do(lambda e: e.activation(kpe2[:, :], kpe[:, :], ACT.Square), kp)
        gq = small[:, 32:40]
        sc_m = float(192) ** -0.5
        sc_n = float(128) ** -0.5
        t_g = [dve.do(lambda e: e.tensor_scalar(gq[:, 0:2], V("mq_g", 0, 2), sc_m, None, ALU.mult), t_vec),
               dve.do(lambda e: e.tensor_scalar(gq[:, 2:3], V("na_q_g"), sc_n, None, ALU.mult), t_vec)]
        t_g += [dve.do(lambda e: e.tensor_tensor(gq[:, 4:5], gq[:, 0:1], V("mk_g"), ALU.mult), t_g),
                dve.do(lambda e: e.tensor_tensor(gq[:, 5:6], gq[:, 2:3], V("na_k_g"), ALU.mult), t_g)]
        cos, sin = C("cos", T, 64), C("sin", T, 64)

        def rope(x, tok, bank, bank_tok, buf, buf_tok):
            m = pe.do(lambda e: e.matmul(bank[0:64, 0:T], C("rot", 64, 64), x, start=True, stop=True), tok, bank_tok, t_cst)
            a = dve.do(lambda e: e.tensor_tensor(buf[0:64, 0:T], bank[0:64, 0:T], sin, ALU.mult), m, buf_tok)
            c = dve.do(lambda e: e.tensor_tensor(x, x, cos, ALU.mult), m, t_cst)
            return dve.do(lambda e: e.tensor_tensor(x, x, buf[0:64, 0:T], ALU.add), a, c), a

        kpe_tok = []

        def key_rope():
            g0 = dve.do(lambda e: e.tensor_scalar(kpe[:, :], kpe[:, :], vec[0:64, VEC["mk_g"] + 1:VEC["mk_g"] + 2], None, ALU.mult), kp2, kp)
            yield from pause(2)
            tok, t = rope(kpe[:, :], g0, PX[1], x_free[1], lane_r[1], None)
            kpe_tok.append(tok)
            x_free[1] = [t]

        start = [latent(), key_rope()]
        quick.extend(start)
        lane_free = [None, None, None, None]
        QT = [(META, P), (META + P, P), (0, META)]

        def attend(lane, S_mms, bias, first_tok, v, v_tok, dst, keys_of, rq, rq_tok):
            bank, pb, ptb, vt, cc = PX[lane], lane_p[lane], lane_pt[lane], lane_vt[lane], lane_c[lane]
            dg = lane_d[lane]
            free = x_free[lane]
            for j, (o, n) in enumerate(QT):
                m = pe.do_last(j == 2, lambda e, j=j, o=o, n=n: e.transpose(bank[0:n, P * j:P * j + P], v[:, o:o + n], ident), v_tok, free, t_cst)
            yield MORE
            vt_tok = [act.do(lambda e: e.activation(vt[:, 0:2, :], bank[:, 0:256].rearrange("p (a b) -> p a b", a=2), ACT.Copy), m, lane_free[lane]),
                      act.do(lambda e: e.activation(vt[0:META, 2, :], bank[0:META, 256:384], ACT.Copy), m)]
            free = vt_tok
            outs = []
            yield from pause(PAUSES[0])

            def scores(j, *toks):
                o, n = QT[j]
                k = len(S_mms)
                for i, (l, r, tk) in enumerate(S_mms):
                    m = pe.do_last(i == k - 1, lambda e: e.matmul(bank[0:n, 0:keys_of(j)], l[:, o:o + n], r[:, 0:keys_of(j)],
                                                 start=(i == 0), stop=(i == k - 1)), list(toks), first_tok, tk)
                return m

            s_tok = scores(0, free)
            for j, (o, n) in enumerate(QT):
                nk, m = keys_of(j), s_tok
                yield MORE
                src, p_, sc = bank[0:n, 0:nk], pb[0:n, 0:nk], rq[0:n, j:j + 1]
                if bias is not None:
                    ba, bt = bias(j)
                    dep = dve.do(lambda e: e.scalar_tensor_tensor(out=p_, in0=src, scalar=sc, in1=ba, op0=ALU.mult, op1=ALU.add), m, bt, rq_tok, free)
                    src, sc = p_, 1.0
                    yield MORE
                    mx = dve.do(lambda e: e.tensor_reduce(cc[0:n, 0:1], p_, AX.X, ALU.max, negate=True), dep, free)
                else:
                    dep = dve.do(lambda e: e.tensor_reduce(cc[0:n, 3:4], src, AX.X, ALU.max, negate=True), m, free)
                    yield MORE
                    mx = dve.do(lambda e: e.tensor_tensor(cc[0:n, 0:1], cc[0:n, 3:4], sc, ALU.mult), dep, rq_tok, free)
                yield MORE
                ex = act.do(lambda e: e.activation(p_, src, ACT.Exp, bias=cc[0:n, 0:1], scale=sc, accum_out=cc[0:n, 1:2]), mx, dep, free)
                yield MORE
                rc = dve.do(lambda e: e.reciprocal(cc[0:n, 2:3], cc[0:n, 1:2]), ex)
                yield MORE
                nm = dve.do(lambda e: e.tensor_scalar(dg[0:n, 0:n], ident[0:n, 0:n], cc[0:n, 2:3], None, ALU.mult), rc, free)
                yield from pause(PAUSES[1] if j < 2 else PAUSES[2])
                tiles = [t for t in range(3) if QT[t][0] < nk]
                for t in tiles:
                    ko, kn = QT[t]
                    m = pe.do_last(t == tiles[-1], lambda e: e.matmul(bank[0:kn, P * t:P * t + n], p_[:, ko:ko + kn], dg[0:n, 0:n], start=True, stop=True), nm, ex, dep)
                yield MORE
                pt_tok = []
                if len(tiles) == 3:
                    pt_tok.append(act.do(lambda e: e.activation(
                        ptb[:, 0:2, 0:n], bank[:, 0:256].rearrange("p (a b) -> p a b", a=2)[:, :, 0:n], ACT.Copy), m, outs))
                pt_tok.append(act.do(lambda e: e.activation(ptb[0:META, 2, 0:n], bank[0:META, 256:256 + n], ACT.Copy), m, outs))
                yield from pause(PAUSES[3])
                for i, t in enumerate(tiles):
                    kn = QT[t][1]
                    m = pe.do_last(i == len(tiles) - 1, lambda e: e.matmul(bank[:, 384:384 + n], vt[0:kn, t, :], ptb[0:kn, t, 0:n],
                                                 start=(i == 0), stop=(i == len(tiles) - 1)), pt_tok, vt_tok)
                s_tok = scores(j + 1, pt_tok) if j < 2 else m
                yield MORE
                outs.append(act.do(lambda e: e.activation(dst[:, o:o + n], bank[:, 384:384 + n], ACT.Copy), s_tok))
                free = [outs[-1], pt_tok, nm, m]
                yield MORE
            x_free[lane] = [outs[-1]]
            lane_free[lane] = [outs[-1], m]
            return outs

        def head_rstd(lane, kmms, qmms, n):
            bank, r, rq = PX[lane], lane_r[lane], lane_c[lane][:, 4:7]
            for i, (o, x, tk) in enumerate(kmms):
                pe.run(lambda e, o=o, x=x, i=i: e.matmul(bank[:, 0:T], o, x, start=(i == 0), stop=(i == len(kmms) - 1)),
                          tk, x_free[lane], t_cst)
            for j, (t, _) in enumerate(QT):
                for i, (o, x, tk) in enumerate(qmms):
                    m = pe.do_last(j == 2 and i == len(qmms) - 1, lambda e, o=o, x=x, i=i: e.matmul(bank[:, 400 + j:401 + j], x[:, t:t + P], o[:, 0:1], start=(i == 0), stop=(i == len(qmms) - 1)),
                              tk, x_free[lane], t_cst)
            yield MORE
            a = act.do(lambda e: e.activation(r[:, :], bank[:, 0:T], ACT.Sqrt, bias=eps, scale=1.0 / n), m, lane_free[lane], kpe_tok)
            aq = act.do(lambda e: e.activation(rq, bank[:, 400:403], ACT.Sqrt, bias=eps, scale=1.0 / n), m, lane_free[lane])
            x_free[lane] = [a, aq]
            yield MORE
            return dve.do(lambda e: e.reciprocal(r[:, :], r[:, :]), a), dve.do(lambda e: e.reciprocal(rq, rq), aq), m, rq

        outa_tok, outb_tok = [None] * 8, [None] * 8
        sq_a, sq_b = Squares("a", 0, T, 8), Squares("b", 0, T, 8)
        mla_free = [None, None]
        na_free = [None, None]
        na_set_free = [[], []]
        ones64 = cst[0:64, CST["ones"]:CST["ones"] + 128]

        def mla_lane(j, head, tq, tqr, tk, tv):
            lane = 2 + j
            q, qr, k, kr, v, r = mla_q[j], mla_qr[j], mla_k[j], mla_kr[j], mla_v[j], lane_r[lane]
            sqa, sqb = lane_p[lane], lane_pt[lane][0:64, :, :].rearrange("p a b -> p (a b)")[:, 0:T]
            a1 = act.do(lambda e: e.activation(sqa[:, :], q[:, :], ACT.Square), tq, lane_free[lane])
            a2 = act.do(lambda e: e.activation(sqb, qr[:, :], ACT.Square), tqr, lane_free[lane])
            a3 = act.do(lambda e: e.activation(r[:, :], k[:, :], ACT.Square), tk, lane_free[lane])
            n2 = dve.do(lambda e: e.tensor_scalar(qr[:, :], qr[:, :], gq[0:64, 1:2], None, ALU.mult), a2, t_g)
            yield from pause(PAUSES[4])
            rt, rqt, m1, rq = yield from head_rstd(lane, [(ones, r[:, :], a3), (ones64, kpe2[:, :], kp2)],
                                        [(ones, sqa[:, :], a1), (ones64, sqb, a2)], 192)
            yield MORE
            n3 = dve.do(lambda e: e.scalar_tensor_tensor(out=k[:, :], in0=k[:, :], scalar=gq[:, 4:5], in1=r[:, :], op0=ALU.mult, op1=ALU.mult), rt, a3, t_g)
            n4 = dve.do(lambda e: e.tensor_tensor(kr[:, :], kpe[:, :], r[0:64, :], ALU.mult), rt, kpe_tok, mla_free[j])
            yield from pause(PAUSES[5])
            n5, t = rope(qr[:, :], n2, PX[lane], x_free[lane], sqa, m1)
            x_free[lane] = [t]
            yield from pause(PAUSES[6])
            toks = [tq, n3, n4, n5, a3]
            outs = yield from attend(lane, [(q, k, [tq, n3]), (qr, kr, [n4, n5])], None, toks, v, tv, out_b[:, head, :], lambda j: T, rq, rqt)
            outb_tok[head] = outs
            mla_free[j] = outs
            sq_b.add(out_b[:, head, :], outs)

        def na_lane(j, head, tq, tk, tv, tb):
            lane = j
            (q, k, v), r, sqa, bias = na_sets[head // 2 % 2][j], lane_r[lane], lane_p[lane], na_bias[j]
            a1 = act.do(lambda e: e.activation(sqa[:, :], q[:, :], ACT.Square), tq, lane_free[lane])
            a3 = act.do(lambda e: e.activation(r[:, :], k[:, :], ACT.Square), tk, lane_free[lane], kpe_tok)
            bt = pool.do(lambda e: e.tensor_tensor(bias[:, :, META:T], bias[:, :, META:T],
                                                   C("namask", 256).unsqueeze(1).to_broadcast([P, 2, 256]), ALU.add), tb, t_cst)
            yield from pause(PAUSES[4])
            rt, rqt, m1, rq = yield from head_rstd(lane, [(ones, r[:, :], a3)], [(ones, sqa[:, :], a1)], 128)
            yield MORE
            n3 = dve.do(lambda e: e.scalar_tensor_tensor(out=k[:, :], in0=k[:, :], scalar=gq[:, 5:6], in1=r[:, :], op0=ALU.mult, op1=ALU.mult), rt, a3, t_g)
            yield from pause(PAUSES[5])

            def bias_of(t):
                return (bias[:, t, :], [bt, tb]) if t < 2 else (bias[0:META, 0, 0:META], [bt, tb])

            outs = yield from attend(lane, [(q, k, [tq, n3])], bias_of, [a3, m1], v, tv, out_a[:, head, :], lambda t: T if t < 2 else META, rq, rqt)
            outa_tok[head] = outs
            na_free[j] = outs
            na_set_free[head // 2 % 2] += outs
            sq_a.add(out_a[:, head, :], outs)

        s_bias = [sem(f"s_bias{j}") for j in range(2)]
        rpb, mb = A["na_rpb"], A["na_meta_bias"]
        ROW = 7 * 31
        spread = nc.dram_tensor("spread", [HEADS, GRID * ROW], F32).ap()
        s_spread = sem("s_spread")
        for h in range(HEADS):
            src = bass.AP(tensor=rpb.tensor, offset=rpb.offset + h * 465 + 4 * 31, ap=[[0, GRID], [1, ROW]])
            t_spread = pool.dma(lambda e: e.dma_start(spread[h].rearrange("(a b) -> a b", a=GRID), src), s_spread, 16 * (h + 1))
        bias_n = [0, 0]

        def load_bias(j, head):
            tok = None
            for r in range(4):
                src = bass.AP(tensor=spread.tensor, offset=spread.offset + head * GRID * ROW + (3 - r) * 31 + 15,
                              ap=[[ROW - 1, GRID], [31, 4], [1, GRID]])
                dst = na_bias[j][64 * (r % 2):64 * (r % 2) + 64, r // 2, META:T].rearrange("p (a b) -> p a b", a=4)
                bias_n[j] += 16
                tok = sp.dma(lambda e, d=dst, s=src: e.dma_start(d, s), s_bias[j], bias_n[j], na_free[j], t_spread)
            for t in range(2):
                src = bass.AP(tensor=mb.tensor, offset=mb.offset + head * META, ap=[[0, P], [1, META]])
                dst = na_bias[j][:, t, 0:META]
                bias_n[j] += 16
                tok = sp.dma(lambda e, d=dst, s=src: e.dma_start(d, s), s_bias[j], bias_n[j], na_free[j])
            return tok

        mx = small
        one_sc = mx[:, 48:80]

        def gain_of(k, name, toks):
            dst = one_sc[:, 16 * k:16 * k + 16]
            t = dve.do(lambda e: e.tensor_scalar(dst, mod[:, 16 + 48 * k:32 + 48 * k], 1.0, None, ALU.add), toks)
            return dve.do(lambda e: e.tensor_tensor(dst, dst, V(name, 0, 16), ALU.mult), t)

        ada = ada_lane()
        na_gens, mla_gens = [], []
        tn = {}
        mla_end_tok = None
        xbh, off = at("xbh", [P, 8, T], F32R, attn_off)
        xbl, off = at("xbl", [P, 8, T], F32R, off)
        h2, off = at("h2", [P, 8, T], F32, off)
        assert off <= mla_end
        XB = Operand(xbh, xbl)
        b_end = []

        def finish_b(gens):
            while any(g in quick for g in gens):
                yield
            yield from norm_steps([out_b[:, c, :] for c in range(8)], outb_tok, 1024, 0, T, lambda i: V("mla_out_g", i), XB, 0,
                                  [xkv_done, outb_tok], squares=sq_b, first=2)
            b_end.append(rstd_free[0])

        def finish_a(gens):
            while any(g in quick for g in gens):
                yield
            yield from norm_steps([out_a[:, c, :] for c in range(8)], outa_tok, 1024, 0, T, lambda i: V("na_out_g", i), X, 0,
                                  w_in_done, squares=sq_a, first=2)

        for o in ORDER:
            p = int(o[1])
            if o[0] == "m":
                drain(*start)
                t = gemm(("qup", p), Xq, 0, T, [(0, 128), (128, 64), (192, 128), (320, 64)], [0, 1, 2, 3])
                drain(*mla_gens)
                fr = [cq_read, mla_free]
                tq = [evac(2 * j, P, T, mla_q[j][:, :], t, fr) for j in range(2)]
                tqr = [evac(2 * j + 1, 64, T, mla_qr[j][:, :], t, fr) for j in range(2)]
                t = gemm(("kvup", p), Xkv, 0, T, [(128 * i, 128) for i in range(4)], [0, 1, 2, 3])
                tk = [evac(2 * j, P, T, mla_k[j][:, :], t, fr) for j in range(2)]
                tv = [evac(2 * j + 1, P, T, mla_v[j][:, :], t, fr) for j in range(2)]
                mla_gens = [mla_lane(j, 2 * p + j, tq[j], tqr[j], tk[j], tv[j]) for j in range(2)]
                quick[0:0] = mla_gens
                if p == 3:
                    xkv_done = peds[-1]
                    fin_b = finish_b(mla_gens)
                    quick.append(fin_b)
                continue
            n = "qkv".index(o[0])
            b = two()
            t = gemm(("na", p, n), X, 0, T, PAIR, b)
            tn[n] = [evac(b[j], P, T, na_sets[p % 2][j][n][:, :], t, na_set_free[p % 2]) for j in range(2)]
            if o[0] == "v":
                drain(*na_gens)
                tbs = [load_bias(j, 2 * p + j) for j in range(2)]
                na_gens = [na_lane(j, 2 * p + j, tn[0][j], tn[1][j], tn[2][j], tbs[j]) for j in range(2)]
                quick[0:0] = na_gens
        w_in_done = peds[-1]
        fin_a = finish_a(na_gens)
        quick.append(fin_a)
        drain(fin_b)
        s_h2 = [sem(f"s_h2{i}") for i in range(2)]
        t_h2 = [pool.dma(lambda e: e.dma_start(h2[:, :, :], hT[:, 0:8, :]), s_h2[0], 16, outb_tok),
                pool.dma(lambda e: e.dma_start(H[:, 8:16, :], hT[:, 8:16, :]), s_h2[1], 16, b_end)]
        lanes.append(ada)

        lbm, lbe0, lbe1, lbs, lb, oml = (mx[:, 80 + 8 * i:88 + 8 * i] for i in range(6))

        def bounds():
            t = dve.do(lambda e: e.tensor_tensor(lbm, V("lb0", 0, 8), V("lb1", 0, 8), ALU.max), t_vec)
            t = [dve.do(lambda e: e.tensor_tensor(lbe0, V("lb0", 0, 8), lbm, ALU.subtract), t),
                 dve.do(lambda e: e.tensor_tensor(lbe1, V("lb1", 0, 8), lbm, ALU.subtract), t)]
            t = [act.do(lambda e: e.activation(lbe0, lbe0, ACT.Exp), t), act.do(lambda e: e.activation(lbe1, lbe1, ACT.Exp), t)]
            t = dve.do(lambda e: e.tensor_tensor(lbs, lbe0, lbe1, ALU.add), t)
            t = dve.do(lambda e: e.reciprocal(lbs, lbs), t)
            t = dve.do(lambda e: e.tensor_tensor(lb, lbe0, lbs, ALU.mult), t)
            return [t, dve.do(lambda e: e.tensor_scalar(oml, lb, -1.0, 1.0, ALU.mult, ALU.add), t)]

        def residual(bank, c, t0, t1, tok, scale=None, stok=None, src=None, free=None):
            dst = H[:, c, t0:t1]
            old = dst if src is None else src[:, c, t0:t1]
            new = ps[bank][:, 0:t1 - t0]
            if scale is None:
                t = dve.do(lambda e: e.tensor_tensor(dst, new, old, ALU.add), tok, htok[c], free)
            else:
                t = dve.do(lambda e: e.scalar_tensor_tensor(out=dst, in0=new, scalar=scale, in1=old, op0=ALU.mult, op1=ALU.add), tok, htok[c], stok)
            main_free[bank] = [t]
            htok[c] = t

        def old_of(c):
            return h2[:, c, 14:T] if c < 8 else H[:, c, 14:T]

        for g in range(8):
            b = two()
            t = gemm(("outb", g), XB, 14, T, PAIR, b)
            for j in range(2):
                c = 2 * g + j
                new, old = ps[b[j]][:, 0:T - 14], old_of(c)
                main_free[b[j]] = [dve.do(lambda e: e.tensor_tensor(old, new, old, ALU.add), t, t_h2)]
            if g == 2:
                lb_tok = bounds()
        outb_done = peds[-1]
        drain(fin_a)
        a_read = [rstd_free[0], b_end, outa_tok, outb_done]
        htok = [None] * KD
        sq = Squares("h", 14, T, KD)
        for g in range(8):
            b = two()
            t = gemm(("outa", g), X, 14, T, PAIR, b, hold=(g == 7))
            for j in range(2):
                c = 2 * g + j
                residual(b[j], c, 14, T, t, src=h2 if c < 8 else None, free=a_read)
                sq.add(H[:, c, 14:T], htok[c], outa_tok)
        ready_sqrt()
        attn_end = [a_read, x_free, lane_free, htok]

        cursor[0] = arena
        hidh = sb("hidh", [P, HALF, SEQ], F32R)
        hidl = sb("hidl", [P, HALF, SEQ], F32R)
        gct = [sb(f"gc{i}", [P, SEQ]) for i in range(3)]
        HID = Operand(hidh, hidl)

        def ffn(b, conv, x_done, sq, scale=None, then=None):
            gc_ring = Ring(gct)
            gc_ring.free = [[x_done] for _ in gct]
            down_done = x_done
            t0 = 14 if conv else 16
            for f in range(2):
                for g in range(HALF // 2):
                    t = gemm((b, "gate", f, g), X, t0, T, PAIR, [0, 1])
                    gs = []
                    for j in range(2):
                        n = HALF * f + 2 * g + j
                        k, gc, free = gc_ring.take()
                        src = ps[j]
                        if conv:
                            a = act.do(lambda e, gc=gc, src=src, n=n: e.activation(gc[:, :], src[:, 2:258], ACT.Identity, bias=V("cb", n), scale=V("cw1", n)), t, free, t_vec)
                            d = dve.do(lambda e, gc=gc, src=src, n=n: e.scalar_tensor_tensor(
                                out=gc[:, :], in0=src[:, 1:257], scalar=V("cw0", n), in1=gc[:, :], op0=ALU.mult, op1=ALU.add), a)
                            d = dve.do(lambda e, gc=gc, src=src, n=n: e.scalar_tensor_tensor(
                                out=gc[:, 0:255], in0=src[:, 3:258], scalar=V("cw2", n), in1=gc[:, 0:255], op0=ALU.mult, op1=ALU.add), d)
                            s = []
                            later(lambda gc=gc, d=d, s=s: s.append(act.do(lambda e: e.activation(gc[:, :], gc[:, :], ACT.Silu), d)))
                            main_free[j] = [d]
                        else:
                            s = act.do(lambda e, gc=gc, src=src: e.activation(gc[:, :], src[:, 0:256], ACT.Silu), t, free)
                            main_free[j] = [s]
                        gs.append((k, gc, s))
                    t = gemm((b, "up", f, g), X, 16, T, PAIR, [2, 3])
                    for j in range(2):
                        k, gc, s = gs[j]
                        assert s
                        m = dve.do(lambda e, gc=gc, j=j: e.tensor_tensor(gc[:, :], ps[2 + j][:, 0:256], gc[:, :], ALU.mult), t, s)
                        main_free[2 + j] = [m]
                        gc_ring.free[k] = split_to(gc[:, :], m, HID, 2 * g + j, 0, SEQ, down_done)
                for g in range(8):
                    bk = two()
                    t = gemm((b, "down", f, g), HID, 0, SEQ, PAIR, bk, hold=(f == 1 and g == 7))
                    for j in range(2):
                        c = 2 * g + j
                        residual(bk[j], c, 16, T, t, *(scale(c) if scale else ()))
                        if f == 1:
                            sq.add(H[:, c, 16:T], htok[c])
                    if f == 1 and g == 0:
                        ready_sqrt()
                        if then is not None:
                            then()
                down_done = peds[-1]
            return down_done

        norm_to([H[:, c, 14:T] for c in range(KD)], htok, D, 14, T, lambda i: V("ffn_g", i), X, 0, peds[-1], squares=sq)
        sq = Squares("h", 16, T, KD)
        before = []

        def before_mix():
            before.append(mod_until(8))
            before.append(gain_of(0, "mix2_g", before[0]))

        down_done = ffn(1, True, [attn_end, peds[-1]], sq, then=before_mix)
        mod_mix, sc_mix = before

        cursor[0] = arena
        convh = sb("convh", [P, 8, SEQ], F32R)
        convl = sb("convl", [P, 8, SEQ], F32R)
        oh = sb("oh", [P, 8, SEQ], F32R)
        ol = sb("ol", [P, 8, SEQ], F32R)
        cu = sb("cu", [P, 2, SEQ])
        cy = sb("cy", [P, 2, SEQ])
        mid = cursor[0]
        hsets = [None, {n: sb(f"hg1_{n}", [P, 2, SEQ]) for n in "qfkig"}]
        keep, cursor[0] = cursor[0], arena
        hsets[0] = {n: sb(f"hg0_{n}", [P, 2, SEQ]) for n in "qfkig"}
        cursor[0] = keep
        hR = sb("hR", [P, 2, SEQ])
        masks32, _ = at("masks32", [P, 128 * (len(LEVELS) + 1)], F32, cursor[0])
        hQs = [sb(f"hQ{i}", [P, 2, SEQ]) for i in range(2)]
        hKs = [sb(f"hK{i}", [P, 2, SEQ]) for i in range(2)]
        hB, off = at("hB", [P, 2, P], F32, tmp_off)
        hvt, off = at("hvt", [P, 4, P], F32, off)
        assert off <= tmp_off + 5 * T * 4
        cursor[0] = mid
        merged = sb("merged", [P, KD, SEQ])
        cu2 = sb("cu2", [P, 2, SEQ])
        cy2 = sb("cy2", [P, 2, SEQ])
        OC, OH = Operand(convh, convl), Operand(oh, ol)

        norm_to([H[:, c, 16:T] for c in range(KD)], htok, D, 16, T, lambda i: one_sc[:, i:i + 1], X, 0, peds[-1],
                shift=lambda i: mod[:, i:i + 1], squares=sq, deps=[sc_mix, mod_mix])
        t_masks = sp.dma(lambda e: e.dma_start(masks32[:, :], A["masks"]), sem("s_masks"), 16, down_done)
        t_masks = pool.do(lambda e: e.tensor_copy(masks[:, :], masks32[:, :]), t_masks)
        h_free = [down_done, t_masks]
        hset_free = [[down_done], [down_done]]

        def hgrn_lane(p, tq, tf, ti, tg):
            bA, bB = PX[1], PX[2]
            hq, hf, hk, hi_, hg = (hsets[p % 2][n] for n in "qfkig")
            hA = hi_[:, :, :].rearrange("p a (b c) -> p (a b) c", b=2)
            for n in range(2):
                for b in range(2):
                    m = pe.do_last(n and b, lambda e, n=n, b=b: e.transpose(bA[:, 128 * (2 * n + b):128 * (2 * n + b) + 128],
                                                              hi_[:, n, 128 * b:128 * b + 128], ident), ti, x_free[1], t_cst)
            tvt = act.do(lambda e: e.activation(hvt[:, :, :], bA[:, :].rearrange("p (a b) -> p a b", a=4), ACT.Copy), m, h_free)
            tk = dve.do(lambda e: e.tensor_scalar(hk[:, :, :], hf[:, :, :], -1.0, 1.0, ALU.mult, ALU.add), tf, h_free)
            tR = dve.do(lambda e: e.memset(hR[:, :, :], 1.0), h_free)
            tP = tf
            yield
            acc = dve.do(lambda e: e.memset(hA, 0.0), m)
            bfree = [[tvt], x_free[2]]
            half = lambda x, m, c: x[:, :, :].rearrange("p a (b c m) -> p (a b) c m", c=2, m=m)[:, :, c, :]
            used = [None, None]
            ready = [tq, tk]
            for lv in range(len(LEVELS) + 1):
                bank = (bA, bB)[lv % 2]
                q, k = (hq, hk) if lv == 0 else (hQs[lv % 2], hKs[lv % 2])
                for n in range(2):
                    for b in range(2):
                        j = 2 * n + b
                        m = pe.do_last(j == 3, lambda e: e.matmul(
                            bank[:, 128 * j:128 * j + 128], k[:, n, 128 * b:128 * b + 128], q[:, n, 128 * b:128 * b + 128],
                            start=True, stop=True), ready, bfree[lv % 2])
                used[lv % 2] = m
                if lv < len(LEVELS):
                    sz = LEVELS[lv]
                    q2, k2 = hQs[(lv + 1) % 2], hKs[(lv + 1) % 2]
                    if lv > 0:
                        tP, tR = grow(hf, LEVELS[lv - 1], tP, tR, ready)
                    if lv < 2:
                        parts = [(q2[:, :, :], hq[:, :, :], hf[:, :, :]), (k2[:, :, :], hk[:, :, :], hR[:, :, :])]
                    else:
                        parts = [(half(q2, sz, 1), half(hq, sz, 1), half(hf, sz, 1)),
                                 (half(k2, sz, 0), half(hk, sz, 0), half(hR, sz, 0))]
                    ready = [dve.do(lambda e: e.tensor_tensor(o, x, y, ALU.mult), tq, tk, tP, tR, used[(lv + 1) % 2], h_free)
                             for o, x, y in parts]
                bv = bank[:, :].rearrange("p (a b) -> p a b", a=4)
                mk = lmask(lv).unsqueeze(1).to_broadcast([P, 4, P])
                acc = dve.do(lambda e: e.copy_predicated(hA, mk, bv), m, acc, t_masks)
                bfree[lv % 2] = [acc]
                yield
            tP, tR = grow(hf, 64, tP, tR, ready)
            hQ, hK = hQs[0], hKs[0]
            t2 = dve.do(lambda e: e.tensor_tensor(hQ[:, :, 128:256], hq[:, :, 128:256], hf[:, :, 128:256], ALU.mult), tP, used)
            t3 = dve.do(lambda e: e.tensor_tensor(hK[:, :, 0:128], hk[:, :, 0:128], hR[:, :, 0:128], ALU.mult), tR, used)
            yield
            for n in range(2):
                m = pe.do(lambda e: e.matmul(bA[:, 128 * n:128 * n + 128], hK[:, n, 0:128], hQ[:, n, 128:256],
                                             start=True, stop=True), t2, t3, bfree)
            tB = act.do(lambda e: e.activation(hB[:, :, :], bA[:, 0:256].rearrange("p (a b) -> p a b", a=2), ACT.Copy), m, h_free)
            yield
            for n in range(2):
                o = 256 * n
                pe.run(lambda e: e.matmul(bB[:, o:o + 128], hvt[:, 2 * n, :], hA[:, 2 * n, :], start=True, stop=True), tB, acc, tvt, bfree)
                pe.run(lambda e: e.matmul(bB[:, o + 128:o + 256], hvt[:, 2 * n, :], hB[:, n, :], start=True, stop=False))
                m = pe.do(lambda e: e.matmul(bB[:, o + 128:o + 256], hvt[:, 2 * n + 1, :], hA[:, 2 * n + 1, :], start=False, stop=True))
            flat = lambda x: x[:, :, :].rearrange("p a b -> p (a b)")
            tO = act.do(lambda e: e.activation(flat(hQ), bB[:, :], ACT.Copy), m)
            tS = act.do(lambda e: e.activation(flat(hK), bB[:, :], ACT.Square), m)
            x_free[2] = [tS]
            yield
            m = pe.do(lambda e: e.matmul(bA[:, :], ones, flat(hK), start=True, stop=True), tS, tB)
            a = act.do(lambda e: e.activation(flat(hR), bA[:, :], ACT.Sqrt, bias=eps, scale=1.0 / 128), m, t3)
            x_free[1] = [a]
            d = dve.do(lambda e: e.reciprocal(flat(hR), flat(hR)), a)
            d = dve.do(lambda e: e.scalar_tensor_tensor(out=flat(hQ), in0=flat(hQ), scalar=V("gnorm_g"), in1=flat(hR), op0=ALU.mult, op1=ALU.mult), d, tO)
            d = dve.do(lambda e: e.tensor_tensor(flat(hQ), flat(hQ), flat(hg), ALU.mult), d, tg)
            yield
            ends = []
            for n in range(2):
                ends += split_to(hQ[:, n, :], d, OH, 2 * p + n, 0, SEQ, down_done)
            h_free[:] = ends
            hset_free[p % 2] = ends
            yield

        def grow(hf, m, tP, tR, used):
            Pv = hf[:, :, :].rearrange("p a (b c m) -> p (a b) c m", c=2, m=m)
            Rv = hR[:, :, :].rearrange("p a (b c m) -> p (a b) c m", c=2, m=m)
            nb = 2 * SEQ // (2 * m)
            r = dve.do(lambda e: e.tensor_tensor(Rv[:, :, 0, :], Rv[:, :, 0, :], Pv[:, :, 1, m - 1:m].to_broadcast([P, nb, m]), ALU.mult), tP, tR, used)
            q = dve.do(lambda e: e.tensor_tensor(Pv[:, :, 1, :], Pv[:, :, 1, :], Pv[:, :, 0, m - 1:m].to_broadcast([P, nb, m]), ALU.mult), r, tP, used)
            return q, r

        gen = None
        if ada in lanes:
            lanes.remove(ada)
        for p in range(4):
            toks = {}
            for n in "qfig":
                b = two()
                t = gemm((n, p), X, 16, T, PAIR, b)
                o = []
                for j in range(2):
                    src, dst = ps[b[j]][:, 0:SEQ], hsets[p % 2][n][:, j, :]
                    c = 2 * p + j
                    if n == "i":
                        e1 = act.do(lambda e, d=dst, s=src: e.activation(d, s, ACT.Copy), t, hset_free[p % 2])
                    else:
                        e1 = act.do(lambda e, d=dst, s=src: e.activation(d, s, ACT.Sigmoid), t, hset_free[p % 2])
                        if n == "f":
                            e2 = dve.do(lambda e, d=dst, c=c: e.tensor_scalar(d, d, oml[:, c:c + 1], lb[:, c:c + 1], ALU.mult, ALU.add), e1, lb_tok)
                        else:
                            e2 = dve.do(lambda e, d=dst, s=src: e.tensor_tensor(d, s, d, ALU.mult), e1)
                            e1 = e2
                        o.append(e2)
                    main_free[b[j]] = [e1]
                    if n == "i":
                        o.append(e1)
                toks[n] = o
            if gen is not None:
                drain(gen)
            gen = hgrn_lane(p, toks["q"], toks["f"], toks["i"], toks["g"])
            lanes.append(gen)
        cfree = [down_done, hset_free[0]]
        for p in range(4):
            b = two()
            t = gemm(("ac", p), X, 16, T, PAIR, b)
            ta = []
            for j in range(2):
                e1 = act.do(lambda e, j=j, s=b[j]: e.activation(cu[:, j, :], ps[s][:, 0:SEQ], ACT.Copy), t, cfree)
                main_free[b[j]] = [e1]
                ta.append(e1)
            b = two()
            t = gemm(("ax", p), X, 16, T, PAIR, b)
            ty = []
            for j in range(2):
                c = 2 * p + j
                u, y = cu[:, j, :], cy[:, j, :]
                d = dve.do(lambda e, u=u, s=b[j]: e.tensor_tensor(u, ps[s][:, 0:SEQ], u, ALU.mult), t, ta[j])
                main_free[b[j]] = [d]
                a = act.do(lambda e, u=u, y=y, c=c: e.activation(y, u, ACT.Copy, scale=V("vw2", c)), d, cfree)
                d = dve.do(lambda e, u=u, y=y, c=c: e.scalar_tensor_tensor(
                    out=y[:, 1:SEQ], in0=u[:, 0:SEQ - 1], scalar=V("vw1", c), in1=y[:, 1:SEQ], op0=ALU.mult, op1=ALU.add), a, d)
                d = dve.do(lambda e, u=u, y=y, c=c: e.scalar_tensor_tensor(
                    out=y[:, 2:SEQ], in0=u[:, 0:SEQ - 2], scalar=V("vw0", c), in1=y[:, 2:SEQ], op0=ALU.mult, op1=ALU.add), d)
                ty.append(d)
            b = two()
            t = gemm(("ab", p), X, 16, T, PAIR, b)
            cf = []
            for j in range(2):
                y = cy[:, j, :]
                d = dve.do(lambda e, y=y, s=b[j]: e.tensor_tensor(y, ps[s][:, 0:SEQ], y, ALU.mult), t, ty[j])
                main_free[b[j]] = [d]
                cf += split_to(y, d, OC, 2 * p + j, 0, SEQ, [down_done, hset_free[0]])
            cfree = cf
        drain(gen)
        lanes.append(ada)
        mtok = [None] * KD
        sig = [None] * 8
        sgbuf = [(cu, cy), (cu2, cy2)]
        sgfree = [cfree, h_free]

        def gates(g):
            sig[g] = []
            for n, buf in zip(("ga", "gb"), sgbuf[g % 2]):
                b = two()
                t = gemm((n, g), X, 16, T, PAIR, b)
                o = []
                for j in range(2):
                    e1 = act.do(lambda e, j=j, s=b[j], buf=buf: e.activation(buf[:, j, :], ps[s][:, 0:SEQ], ACT.Sigmoid), t, sgfree[g % 2])
                    main_free[b[j]] = [e1]
                    o.append(e1)
                sig[g].append(o)

        def gated(g):
            ga, gb = sgbuf[g % 2]
            b = two()
            t = gemm(("ya", g), OC, 0, SEQ, PAIR, b)
            for j in range(2):
                c = 2 * g + j
                d = dve.do(lambda e, j=j, c=c, s=b[j]: e.tensor_tensor(merged[:, c, :], ps[s][:, 0:SEQ], ga[:, j, :], ALU.mult), t, sig[g][0][j], h_free)
                main_free[b[j]] = [d]
                mtok[c] = d
            b = two()
            t = gemm(("yb", g), OH, 0, SEQ, PAIR, b)
            cf = []
            for j in range(2):
                c = 2 * g + j
                d = dve.do(lambda e, j=j, s=b[j]: e.tensor_tensor(gb[:, j, :], ps[s][:, 0:SEQ], gb[:, j, :], ALU.mult), t, sig[g][1][j])
                main_free[b[j]] = [d]
                d = dve.do(lambda e, j=j, c=c: e.tensor_tensor(merged[:, c, :], merged[:, c, :], gb[:, j, :], ALU.add), d, mtok[c])
                mtok[c] = d
                cf.append(d)
            sgfree[g % 2] = cf

        for g in range(6):
            gates(g)
            gated(g)
        gates(6)
        gates(7)
        x_done = peds[-1]

        def split_merged():
            for c in range(12):
                yield
                split_to(merged[:, c, :], mtok[c], X, c, 16, T, x_done)

        split_lane = split_merged()
        lanes.insert(0, split_lane)
        gated(6)
        gated(7)
        drain(split_lane)
        for c in range(12, KD):
            split_to(merged[:, c, :], mtok[c], X, c, 16, T, x_done)
        m_read = X.tok[KD - 1]
        sq = Squares("h", 16, T, KD)
        mod_gt = mod_until(12)
        for g in range(8):
            b = two()
            t = gemm(("wo", g), X, 16, T, PAIR, b, hold=(g == 7))
            for j in range(2):
                c = 2 * g + j
                residual(b[j], c, 16, T, t, mod[:, 32 + c:33 + c], mod_gt)
                sq.add(H[:, c, 16:T], htok[c])
            if g == 0:
                ready_sqrt()
            if g == 4:
                mod_ffn = mod_until(20)
                sc_ffn = gain_of(1, "ffn2_g", mod_ffn)
        norm_to([H[:, c, 16:T] for c in range(KD)], htok, D, 16, T, lambda i: one_sc[:, 16 + i:17 + i], X, 0, peds[-1],
                shift=lambda i: mod[:, 48 + i:49 + i], squares=sq, deps=[sc_ffn, mod_ffn])
        sq = Squares("h", 16, T, KD)
        mod_end = mod_until(24)
        ffn(2, False, [peds[-1], m_read], sq, scale=lambda c: (mod[:, 80 + c:81 + c], mod_end))

        r, tr = sq.rstd(D, False)
        s_out = sem("s_out")
        oT = out.rearrange("(c p) t -> p c t", p=P)
        tot = 0
        done = []
        for c in range(KD):
            x = H[:, c, 16:T]
            if c % 4 == 1:
                d = pool.do(lambda e: e.tensor_tensor(x, x, r, ALU.mult), tr, htok[c])
                d = act.do(lambda e: e.activation(x, x, ACT.Copy, scale=V("fin_g", c)), d)
            else:
                d = dve.do(lambda e: e.scalar_tensor_tensor(out=x, in0=x, scalar=V("fin_g", c), in1=r, op0=ALU.mult, op1=ALU.mult), tr, htok[c])
            done.append(d)
            if c % 4 == 3:
                tot += 16
                sp.dma(lambda e, c=c: e.dma_start(oT[:, c - 3:c + 1, :], H[:, c - 3:c + 1, 16:T]), s_out, tot, done[-4:])
        sp.need([(s_out, tot)])
        assert at_slab[0] == len(plan)


_WEIGHTS = ["w_in", "w_q_up", "w_kv_up", "w_out", "w_gate", "w_up", "w_down", "w_ada_2", "w_in_2", "w_conv_out_2",
            "w_hgrn_out_2", "w_o_2", "w_ffn_gate_2", "w_ffn_up_2", "w_ffn_down_2", "na_rpb", "na_meta_bias"]


def lay_out(inputs):
    a = {n: np.ascontiguousarray(inputs[n][0]) for n in _WEIGHTS}
    a["hT"] = np.ascontiguousarray(np.concatenate([inputs["meta_tokens"], inputs["x"][0]], 0).T)
    pad = np.zeros(64, np.float32)
    rows = {"mix_g": inputs["mix_norm_g"][0], "na_q_g": inputs["na_q_g"][0], "na_k_g": inputs["na_k_g"][0],
            "cq_g": inputs["mla_cq_g"][0], "ckv_g": inputs["mla_ckv_g"][0],
            "mq_g": np.concatenate([inputs["mla_q_g"][0], pad]), "mk_g": np.concatenate([inputs["mla_k_g"][0], pad]),
            "na_out_g": inputs["na_out_g"][0], "mla_out_g": inputs["mla_out_g"][0], "ffn_g": inputs["ffn_norm_g"][0],
            "cw0": inputs["conv_w"][0, 0], "cw1": inputs["conv_w"][0, 1], "cw2": inputs["conv_w"][0, 2],
            "cb": inputs["conv_b"][0], "b_ada": inputs["b_ada_2"][0], "mix2_g": inputs["norm_mix_g_2"][0],
            "vw0": inputs["conv_w_2"][0, 0], "vw1": inputs["conv_w_2"][0, 1], "vw2": inputs["conv_w_2"][0, 2],
            "lb0": inputs["lb_param_2"][0], "lb1": inputs["lb_param_2"][1], "gnorm_g": inputs["gnorm_g_2"][0],
            "ffn2_g": inputs["norm_ffn_g_2"][0], "fin_g": inputs["norm_final_g_2"], "c": inputs["c_2"][0]}
    flat = np.concatenate([np.asarray(rows[n]) for n, _ in VEC_ROWS])
    a["vecs"] = np.ascontiguousarray(flat.reshape(NVEC, P).T)
    a["consts"] = constants()
    a["masks"] = level_masks()
    return a


def program(nc, arrays):
    aps = {n: nc.dram_tensor(f"in_{n}", list(a.shape), mybir.dt.from_np(a.dtype), kind="ExternalInput").ap()
           for n, a in arrays.items()}
    out = nc.dram_tensor("out_0", [D, SEQ], F32, kind="ExternalOutput").ap()
    build(nc, aps, out)


def kernel(**inputs):
    import concourse.bacc as _bacc
    from concourse.bass_utils import run_bass_kernel_spmd as _run

    inputs = {k: np.asarray(v) for k, v in inputs.items()}
    arrays = lay_out(inputs)
    nc = _bacc.Bacc("TRN2", target_bir_lowering=False, num_devices=1)
    program(nc, arrays)
    r = _run(nc, [{f"in_{n}": a for n, a in arrays.items()}], core_ids=[0])
    got = r.results[0]["out_0"]
    return np.ascontiguousarray(got.T).reshape(1, SEQ, D)
```
